# Optimizing a Trainium2 kernel written in Bass

```python
import math
import jax, jax.numpy as jnp
from jax import lax
import numpy as np

D_MODEL = 1024
BATCH = 1
SEQ = 256
DEPTH = 2

MEM_LEN = 256
N_EVEN = (DEPTH + 1) // 2
N_ODD = DEPTH // 2
EPS = 1e-6
NEG_BIG = -1e30
TINY = 1e-30

HGRN_HEADS = 4
HGRN_DK = 128
HGRN_DV = 128
HGRN_WIDTH = HGRN_HEADS * HGRN_DK
HGRN_CHUNK = 64
CONV_CH = D_MODEL - HGRN_WIDTH
CONV_WIDTH = 31
EVEN_IN = 4 * HGRN_WIDTH + 2 * CONV_CH
DA_HEADS = 8
DA_HEAD_DIM = 64
DA_VDIM = 2 * DA_HEAD_DIM
ODD_IN = 3 * DA_HEADS * 2 * DA_HEAD_DIM
Q_BLOCK = 128
REL_BUCKETS = 32
REL_MAX_DIST = 128
XA_HEADS = 4
XA_HEAD_DIM = D_MODEL // XA_HEADS
N_GROUPS = 4
EXPERTS_PER_GROUP = 4
N_EXPERTS = N_GROUPS * EXPERTS_PER_GROUP
TOP_K = 2
EXPERT_FF = 512

kernel_name = "hybrid_hgrn2_conv_diffattn_hmoe"

def rms_norm(x, g):
    xf = x.astype(jnp.float32)
    y = xf * lax.rsqrt(jnp.mean(xf * xf, axis=-1, keepdims=True) + EPS)
    return (y * g.astype(jnp.float32)).astype(x.dtype)

def layer_norm(x, g, b):
    xf = x.astype(jnp.float32)
    mu = jnp.mean(xf, axis=-1, keepdims=True)
    var = jnp.mean(jnp.square(xf - mu), axis=-1, keepdims=True)
    y = (xf - mu) * lax.rsqrt(var + EPS)
    return (y * g.astype(jnp.float32) + b.astype(jnp.float32)).astype(x.dtype)

def hgrn2_chunk_scan(q, k, v, log_f):
    B, S, H, DK = q.shape
    DV = v.shape[-1]
    C = HGRN_CHUNK
    n = S // C

    def to_chunks(t):
        return t.astype(jnp.float32).reshape(B, n, C, H, t.shape[-1]).transpose(1, 0, 3, 2, 4)

    qc, kc, vc, gc = to_chunks(q), to_chunks(k), to_chunks(v), to_chunks(log_f)
    causal = jnp.tril(jnp.ones((C, C), dtype=bool))[:, :, None]

    def step(state, inp):
        qi, ki, vi, gi = inp
        b = jnp.cumsum(gi, axis=2)
        o_inter = jnp.einsum('bhtk,bhkv->bhtv', qi * jnp.exp(b), state)
        diff = b[:, :, :, None, :] - b[:, :, None, :, :]
        decay = jnp.where(causal, jnp.exp(jnp.where(causal, diff, 0.0)), 0.0)
        scores = jnp.einsum('bhtk,bhsk,bhtsk->bhts', qi, ki, decay)
        o_intra = jnp.einsum('bhts,bhsv->bhtv', scores, vi)
        b_last = b[:, :, -1:, :]
        new_state = (jnp.exp(b_last[:, :, 0, :])[..., None] * state
                     + jnp.einsum('bhsk,bhsv->bhkv', ki * jnp.exp(b_last - b), vi))
        return new_state, o_inter + o_intra

    state0 = jnp.zeros((B, H, DK, DV), jnp.float32)
    _, o = lax.scan(step, state0, (qc, kc, vc, gc))
    return o.transpose(1, 0, 3, 2, 4).reshape(B, S, H, DV)

def hgrn_conv_mixer(h, w_in, w_out, lb, hg_norm, dw, db, ln_g, ln_b):
    B, S, _ = h.shape
    proj = h @ w_in
    W = HGRN_WIDTH
    zq, zf, zi, zg, cu, cv = jnp.split(
        proj, [W, 2 * W, 3 * W, 4 * W, 4 * W + CONV_CH], axis=-1)
    f = lb + (1.0 - lb) * jax.nn.sigmoid(zf.astype(jnp.float32))
    log_f = jnp.log(jnp.maximum(f, TINY))
    k = 1.0 - f
    q = jax.nn.silu(zq.astype(jnp.float32))
    heads = lambda t: t.reshape(B, S, HGRN_HEADS, -1)
    o = hgrn2_chunk_scan(heads(q), heads(k), heads(zi), heads(log_f))
    o = rms_norm(o, hg_norm).reshape(B, S, HGRN_HEADS * HGRN_DV)
    o_hgrn = (o * jax.nn.sigmoid(zg.astype(jnp.float32))).astype(h.dtype)
    u = cu * jax.nn.sigmoid(cv)
    c = lax.conv_general_dilated(
        u, dw[:, None, :], window_strides=(1,), padding=[(CONV_WIDTH - 1, 0)],
        dimension_numbers=('NWC', 'WIO', 'NWC'), feature_group_count=CONV_CH) + db
    c = jax.nn.silu(layer_norm(c, ln_g, ln_b))
    return jnp.concatenate([o_hgrn, c.astype(h.dtype)], axis=-1) @ w_out

def t5_bucket(rel):
    n = jnp.maximum(rel, 0)
    max_exact = REL_BUCKETS // 2
    nf = jnp.maximum(n, 1).astype(jnp.float32)
    large = max_exact + (jnp.log(nf / max_exact) / math.log(REL_MAX_DIST / max_exact)
                         * (REL_BUCKETS - max_exact)).astype(jnp.int32)
    large = jnp.clip(large, 0, REL_BUCKETS - 1)
    return jnp.where(n < max_exact, n, large)

def diff_attention(h, w_qkv, w_out, lq1, lk1, lq2, lk2, subln_g, rel_bias, lam_init):
    B, S, _ = h.shape
    q, k, v = jnp.split(h @ w_qkv, 3, axis=-1)
    q = q.reshape(B, S, DA_HEADS, 2, DA_HEAD_DIM)
    k = k.reshape(B, S, DA_HEADS, 2, DA_HEAD_DIM)
    v = v.reshape(B, S, DA_HEADS, DA_VDIM)
    f32 = jnp.float32
    lam = (jnp.exp(jnp.sum(lq1.astype(f32) * lk1.astype(f32)))
           - jnp.exp(jnp.sum(lq2.astype(f32) * lk2.astype(f32))) + lam_init)
    nb = S // Q_BLOCK
    qb = q.reshape(B, nb, Q_BLOCK, DA_HEADS, 2, DA_HEAD_DIM).transpose(1, 0, 3, 4, 2, 5)
    kt = k.transpose(0, 2, 3, 1, 4)
    vt = v.transpose(0, 2, 1, 3)
    k_pos = jnp.arange(S)
    table = rel_bias.astype(f32)
    scale = DA_HEAD_DIM ** -0.5

    def block(args):
        qblk, start = args
        q_pos = start + jnp.arange(Q_BLOCK)
        rel = q_pos[:, None] - k_pos[None, :]
        bias = table[t5_bucket(rel)].transpose(2, 0, 1)
        s = jnp.einsum('bhmqd,bhmkd->bhmqk', qblk, kt).astype(f32) * scale + bias[None, :, None]
        s = jnp.where(rel >= 0, s, NEG_BIG)
        p = jax.nn.softmax(s, axis=-1)
        a = p[:, :, 0] - lam * p[:, :, 1]
        return jnp.einsum('bhqk,bhkv->bhqv', a.astype(vt.dtype), vt)

    o = lax.map(block, (qb, jnp.arange(nb) * Q_BLOCK))
    o = o.transpose(1, 0, 3, 2, 4).reshape(B, S, DA_HEADS, DA_VDIM)
    o = rms_norm(o, subln_g) * (1.0 - lam_init)
    return o.reshape(B, S, DA_HEADS * DA_VDIM) @ w_out

def memory_cross_attention(h, mem_n, wq, wkv, wo):
    B, S, _ = h.shape
    M = mem_n.shape[1]
    q = (h @ wq).reshape(B, S, XA_HEADS, XA_HEAD_DIM)
    k, v = jnp.split(mem_n @ wkv, 2, axis=-1)
    k = k.reshape(B, M, XA_HEADS, XA_HEAD_DIM)
    v = v.reshape(B, M, XA_HEADS, XA_HEAD_DIM)
    s = jnp.einsum('bshd,bmhd->bhsm', q, k).astype(jnp.float32) * (XA_HEAD_DIM ** -0.5)
    p = jax.nn.softmax(s, axis=-1)
    o = jnp.einsum('bhsm,bmhd->bshd', p.astype(v.dtype), v).reshape(B, S, D_MODEL)
    return o @ wo

def hierarchical_moe(h, w_grp, b_grp, w_exp, b_exp, w1, w3, w2):
    B, S, D = h.shape
    t = h.reshape(-1, D)
    f32 = jnp.float32
    grp_logits = (t @ w_grp).astype(f32) + b_grp.astype(f32)
    grp_prob = jax.nn.softmax(grp_logits, axis=-1)
    g_sel = jnp.argmax(grp_logits, axis=-1)
    g_w = jnp.take_along_axis(grp_prob, g_sel[:, None], axis=-1)
    exp_logits = ((t @ w_exp).astype(f32) + b_exp.astype(f32)).reshape(-1, N_GROUPS, EXPERTS_PER_GROUP)
    in_grp = jnp.take_along_axis(exp_logits, g_sel[:, None, None], axis=1)[:, 0]
    top_v, top_i = lax.top_k(in_grp, TOP_K)
    top_w = jax.nn.softmax(top_v, axis=-1) * g_w
    expert_id = g_sel[:, None] * EXPERTS_PER_GROUP + top_i
    gate = jnp.sum(jax.nn.one_hot(expert_id, N_EXPERTS, dtype=f32) * top_w[..., None], axis=1)
    gate = gate.astype(t.dtype)
    out = jnp.zeros_like(t)
    for e in range(N_EXPERTS):
        hid = jax.nn.silu(t @ w1[e]) * (t @ w3[e])
        out = out + gate[:, e:e + 1] * (hid @ w2[e])
    return out.reshape(B, S, D)

def setup_inputs(seed: int = 0) -> dict:
    key = jax.random.key(seed)
    ks = iter(jax.random.split(key, 40))
    nrm = lambda shape, scale: jax.random.normal(next(ks), shape, jnp.float32) * scale
    gain = lambda shape: 1.0 + nrm(shape, 0.05)
    D = D_MODEL
    return {
        "x": nrm((BATCH, SEQ, D), 1.0),
        "mem": nrm((BATCH, MEM_LEN, D), 1.0),
        "rel_bias": nrm((REL_BUCKETS, DA_HEADS), 0.5),
        "mem_norm_g": gain((D,)),
        "final_norm_g": gain((D,)),
        "hgrn_lb": nrm((N_EVEN, HGRN_WIDTH), 0.5),
        "norm_mix_g": gain((DEPTH, D)),
        "norm_xattn_g": gain((DEPTH, D)),
        "norm_ffn_g": gain((DEPTH, D)),
        "even_w_in": nrm((N_EVEN, D, EVEN_IN), D ** -0.5),
        "even_w_out": nrm((N_EVEN, HGRN_HEADS * HGRN_DV + CONV_CH, D), (HGRN_HEADS * HGRN_DV + CONV_CH) ** -0.5),
        "hgrn_norm_g": gain((N_EVEN, HGRN_DV)),
        "conv_dw": nrm((N_EVEN, CONV_WIDTH, CONV_CH), CONV_WIDTH ** -0.5),
        "conv_db": nrm((N_EVEN, CONV_CH), 0.02),
        "conv_ln_g": gain((N_EVEN, CONV_CH)),
        "conv_ln_b": nrm((N_EVEN, CONV_CH), 0.02),
        "odd_w_qkv": nrm((N_ODD, D, ODD_IN), D ** -0.5),
        "odd_w_out": nrm((N_ODD, DA_HEADS * DA_VDIM, D), (DA_HEADS * DA_VDIM) ** -0.5),
        "lam_q1": nrm((N_ODD, DA_HEAD_DIM), 0.1),
        "lam_k1": nrm((N_ODD, DA_HEAD_DIM), 0.1),
        "lam_q2": nrm((N_ODD, DA_HEAD_DIM), 0.1),
        "lam_k2": nrm((N_ODD, DA_HEAD_DIM), 0.1),
        "subln_g": gain((N_ODD, DA_VDIM)),
        "xa_wq": nrm((DEPTH, D, D), D ** -0.5),
        "xa_wkv": nrm((DEPTH, D, 2 * D), D ** -0.5),
        "xa_wo": nrm((DEPTH, D, D), D ** -0.5),
        "moe_w_grp": nrm((DEPTH, D, N_GROUPS), D ** -0.5),
        "moe_b_grp": nrm((DEPTH, N_GROUPS), 0.01),
        "moe_w_exp": nrm((DEPTH, D, N_EXPERTS), D ** -0.5),
        "moe_b_exp": nrm((DEPTH, N_EXPERTS), 0.01),
        "moe_w1": nrm((DEPTH, N_EXPERTS, D, EXPERT_FF), D ** -0.5),
        "moe_w3": nrm((DEPTH, N_EXPERTS, D, EXPERT_FF), D ** -0.5),
        "moe_w2": nrm((DEPTH, N_EXPERTS, EXPERT_FF, D), EXPERT_FF ** -0.5),
    }

def reference(x, mem, rel_bias, mem_norm_g, final_norm_g, hgrn_lb,
              norm_mix_g, norm_xattn_g, norm_ffn_g,
              even_w_in, even_w_out, hgrn_norm_g, conv_dw, conv_db, conv_ln_g, conv_ln_b,
              odd_w_qkv, odd_w_out, lam_q1, lam_k1, lam_q2, lam_k2, subln_g,
              xa_wq, xa_wkv, xa_wo,
              moe_w_grp, moe_b_grp, moe_w_exp, moe_b_exp, moe_w1, moe_w3, moe_w2):
    lb_p = jax.nn.softmax(hgrn_lb.astype(jnp.float32), axis=0)
    lower_bounds = jnp.cumsum(lb_p, axis=0) - lb_p[0]
    mem_n = rms_norm(mem, mem_norm_g)
    for i in range(DEPTH):
        h = rms_norm(x, norm_mix_g[i])
        if i % 2 == 0:
            j = i // 2
            y = hgrn_conv_mixer(h, even_w_in[j], even_w_out[j], lower_bounds[j], hgrn_norm_g[j],
                                conv_dw[j], conv_db[j], conv_ln_g[j], conv_ln_b[j])
        else:
            j = i // 2
            lam_init = 0.8 - 0.6 * math.exp(-0.3 * i)
            y = diff_attention(h, odd_w_qkv[j], odd_w_out[j], lam_q1[j], lam_k1[j], lam_q2[j],
                               lam_k2[j], subln_g[j], rel_bias, lam_init)
        x = x + y
        x = x + memory_cross_attention(rms_norm(x, norm_xattn_g[i]), mem_n, xa_wq[i], xa_wkv[i], xa_wo[i])
        x = x + hierarchical_moe(rms_norm(x, norm_ffn_g[i]), moe_w_grp[i], moe_b_grp[i], moe_w_exp[i],
                                 moe_b_exp[i], moe_w1[i], moe_w3[i], moe_w2[i])
    return rms_norm(x, final_norm_g)


_drawn_inputs = setup_inputs


def setup_inputs(seed=0):
    import zlib

    import numpy as np

    out = dict(_drawn_inputs(seed))
    spreads = {}
    factors = {'moe_b_grp': 3.312, 'moe_b_exp': 8.0}
    for name, (base, spread) in spreads.items():
        noise = np.random.default_rng([zlib.crc32(name.encode()), seed]).standard_normal(out[name].shape)
        drawn = base * np.exp(spread * noise) if base else spread * noise
        out[name] = __import__('jax').numpy.asarray(drawn.astype(out[name].dtype))
    for name, factor in factors.items():
        out[name] = (out[name] * factor).astype(out[name].dtype)
    return out
```

```python
import math
from contextlib import ExitStack

import numpy as np
import concourse.bass as bass
from concourse import mybir

F32 = mybir.dt.float32
I32 = mybir.dt.int32
ALU = mybir.AluOpType
ACT = mybir.ActivationFunctionType
AX = mybir.AxisListType

P = 128
D, S, M = 1024, 256, 256
KD = D // P
TB = S // P
DEPTH = 2
EPS = 1e-6
UNIT = 4096
SLOTS = 6
PROJ = 16
NE, NG, EPG = 16, 4, 4
EU = 3
CAP = 64
FF = 512
CONVW = 31
PAD = CONVW - 1
HH = 4
DH = 8
LAM_INIT = 0.8 - 0.6 * math.exp(-0.3)
BIG = 1e30
BW = 384
RELS = 32
LEVELS = 7
LN_SPLIT = 2.0 ** 60

N_MIX0, N_MEM, N_XA0, N_FFN0, N_MIX1, N_XA1, N_FFN1, N_FINAL = range(8)

DVE_UNITS = (10, 11, 14, 15)
R_DB, R_LNG, R_LNB, R_HG, R_SUB, R_LB = 0, 4, 8, 12, 13, 14
ROWS = 18


def t5_onehot():
    rel = 2 * P - 1 - np.arange(BW)
    n = np.maximum(rel, 0)
    half = RELS // 2
    nf = np.maximum(n, 1).astype(np.float32)
    large = half + (np.log(nf / half) / np.float32(math.log(128 / half)) * half).astype(np.int32)
    bucket = np.where(n < half, n, np.clip(large, 0, RELS - 1))
    out = np.zeros((RELS + 1, BW), np.float32)
    ok = rel >= 0
    out[bucket[ok], np.arange(BW)[ok]] = 1.0
    out[RELS, ~ok] = 1.0
    return out


def shape_constants():
    i = np.arange(P)
    ident = np.eye(P)
    upper = (i[:, None] < i[None, :]) * 1.0
    ones = np.ones((P, P))
    iota = np.tile(i % CAP, (P, 1))
    s, t = i[:, None], i[None, :]
    masks = [(s == t) * 1.0]
    for lev in range(1, LEVELS + 1):
        m = 2 ** (lev - 1)
        masks.append(((s // (2 * m) == t // (2 * m)) & (s % (2 * m) < m) & (t % (2 * m) >= m)) * 1.0)
    ties = np.tile(np.arange(NE, 0, -1), (P, 1))
    return np.concatenate([ident, upper, ones, iota, ties, *masks], 1).astype(np.float32)


class Own:

    def __init__(self, eng):
        self.eng, self.base, self.n, self.last = eng, {}, {}, None

    def value(self, sem):
        return self.base.get(sem.name, 0) + self.n.get(sem.name, 0)

    def inc(self, ins, sem):
        self.n[sem.name] = self.n.get(sem.name, 0) + 1
        ins.then_inc(sem, 1)
        self.last = (sem, self.value(sem))

    def wait(self, back=0):
        self.eng.wait_ge(self.last[0], self.last[1] - back)

    def enter(self, i, per):
        self.outer = {s.name: self.value(s) for s in per}
        for s, k in per.items():
            self.base[s.name], self.n[s.name] = i * k + self.outer[s.name], 0

    def leave(self, times, per):
        for s, k in per.items():
            assert self.n[s.name] == k, (s.name, self.n[s.name], k)
            self.base[s.name], self.n[s.name] = self.outer[s.name] + times * k, 0


def build(nc, a, out):
    ctx = ExitStack()
    with ctx:
        def sb(name, shape, dt=F32):
            return ctx.enter_context(nc.sbuf_tensor(name, shape, dt))

        def sem(name):
            return ctx.enter_context(nc.semaphore(name))

        ring = sb("ring", [P, SLOTS, UNIT])
        x = sb("x", [P, TB, D])
        xs = sb("xs", [P, TB, D])
        hT = sb("hT", [P, KD, S])
        memT = sb("memT", [P, KD, M])
        kmem = sb("kmem", [P, KD, M])
        vmem = sb("vmem", [P, TB, D])
        AR = 13432
        arena = sb("arena", [P, AR])
        masks = sb("masks", [P, LEVELS + 1, P])
        consts = sb("consts", [P, 4 * P + NE])
        gains = sb("gains", [P, 7, KD])
        vecs = sb("vecs", [P, 32])
        dwT = sb("dwT", [P, HH, CONVW])
        lamrow = sb("lamrow", [P, 4, 64])
        st = sb("st", [P, 160])
        xtab = sb("xtab", [P, NE + 1], I32)
        ps = ctx.enter_context(nc.psum_tensor("ps", [P, 8, 512], F32))
        bias_dram = nc.dram_tensor("bias_dram", [DH, P, BW], F32)

        ident, upper, ones = consts[:, 0:P], consts[:, P:2 * P], consts[:, 2 * P:3 * P]
        iota, ties = consts[:, 3 * P:4 * P], consts[:, 4 * P:4 * P + NE]

        ss, ms, rt, rs = st[:, 0:2], st[:, 2:4], st[:, 4:6], st[:, 6:8]
        lam2, lamexp, nlam, lamd = st[:, 8:10], st[:, 10:12], st[:, 12:13], st[:, 13:14]
        lbz, lbe, lbr, lbp, lb, oml = (st[:, 16 + 4 * i:20 + 4 * i] for i in range(6))
        oss, oms, ort, ors = (st[:, 40 + 16 * i:56 + 16 * i] for i in range(4))
        bn, mv, crt, crs = st[:, 104:116], st[:, 116:120], st[:, 120:122], st[:, 122:124]
        sub = st[:, 124:125]
        xmx, xsum, xrc = st[:, 126:134], st[:, 134:142], st[:, 142:150]
        xcarry = st[:, 158:159]
        dmx, dsum, drc = (st[:, 126 + 4 * i:130 + 4 * i] for i in range(3))
        cve = st[:, 138:140]

        def carve(at, shape):
            n = int(np.prod(shape))
            assert at + n <= AR, (at, n)
            v = arena[:, at:at + n]
            if len(shape) == 2:
                return v.rearrange("p (a b) -> p a b", b=shape[1])
            if len(shape) == 3:
                return v.rearrange("p (a b c) -> p a b c", b=shape[1], c=shape[2])
            return v

        fgate = carve(0, [1024])
        logf = carve(1024, [1024])
        bcum = carve(2048, [1024])
        qh = carve(3072, [1024])
        kh = carve(4096, [1024])
        vh = carve(5120, [TB, 512])
        gh = carve(6144, [TB, 512])
        upad = carve(7168, [HH, PAD + S])
        cacc = carve(8312, [HH, S])
        Ebuf = [carve(1024, [1024]), carve(0, [1024])]
        Qt = [carve(9336, [1024]), carve(10360, [1024])]
        Kt = [carve(11384, [1024]), carve(12408, [1024])]
        scanmask = xs[:, 0, :]
        lntmp = xs[:, 1, :]
        scoresT = xs[:, 0, :].rearrange("p (a b) -> p a b", b=P)
        crossT = carve(0, [HH, P])
        oh = carve(9336, [TB, 512])
        ohsq = carve(11384, [TB, 512])
        cnorm = carve(10360, [TB, 512])
        rows = carve(7168, [P])
        dwrows = carve(7296, [512])
        onehot = carve(7808, [BW])
        table = carve(8192, [DH])
        tablerep = carve(8200, [DH, P])
        bstage = carve(9336, [DH, BW])

        qd = carve(0, [DH, S])
        kd = carve(2048, [DH, S])
        vd = carve(4096, [TB, D])
        biasd = carve(6144, [DH, 2 * P])
        sD = [carve(8192, [2, S]), carve(8704, [2, S])]
        aD = [carve(9216, [S]), carve(9472, [S])]
        aTD = [carve(9728, [TB, P]), carve(9984, [TB, P])]
        odsq = carve(10240, [TB, D])
        od = xs

        qx = carve(0, [KD, S])
        px = carve(2048, [4, 2, M])
        pxT = carve(4096, [TB, 4, S])

        hsel = carve(0, [KD, P])
        psel = carve(1024, [TB, P])
        pgate = [carve(1280, [TB, P]), carve(1536, [TB, P])]
        tsb = [carve(1792, [512]), carve(2304, [512])]
        sil = carve(2816, [S])
        hid = carve(3072, [S])
        ysb = [carve(3328, [512]), carve(3840, [512])]
        hselx = carve(4352, [KD, CAP])
        pselx = carve(4864, [TB, CAP])
        pgatex = carve(4992, [TB, P])
        tsbx = carve(5248, [512])
        silx = carve(5760, [S])
        hidx = carve(6016, [S])
        ysbx = carve(6272, [512])
        wr = carve(6784, [KD, NG + NE])
        rbias = carve(6944, [NG + NE])
        lg = carve(6964, [TB, NG + NE])
        r4 = [carve(7004 + 8 * i, [TB, NG]) for i in range(4)]
        r16 = [carve(7036 + 32 * i, [TB, NE]) for i in range(8)]
        r1 = [carve(7292 + 2 * i, [TB, 1]) for i in range(10)]
        gate = carve(7312, [TB, NE])
        rank = carve(7344, [TB, NE + 2])
        nx = carve(7382, [NE])
        cumx = carve(7414, [NE + 1])
        zeros = carve(7432, [512])
        fgain = carve(8192, [D])

        def bank(b):
            return ps[:, b, :]

        def pair(pj):
            b = 2 * (pj % 2)
            return ps[:, b:b + 2, :]

        landed = [sem(f"landed{i}") for i in range(SLOTS)]
        names = """x_in mem_in small_in const_in tab_in gain_in mask_in lam_in t5_stored t5_in
            router_in fgain_in out_done proj_done proj_read_act proj_read_dve act_step dve_step upad_zero
            table_rep t5_rows t5_read vec_tr vec_read lb_zero lb_exp lam_dot lam_exp
            sq_act ms_ready rt_ready rs_ready xs_act xs_dve tr_done hT_act hT_dve x_new
            f_ready ln_ready k_ready u_ready conv_done arg_ready exp_ready lev_ready
            lev_done lev_read cross_done cross_read o_done o_read o_sq oms_ready ort_ready on_ready
            ot_done ot_read ct_done cv_ready cr_ready cn_ready cb_done cb_read
            xsc_done xmax_ready xexp_ready xp_ready xpt_done xpt_read xo_done xo_read
            dsc_done dsc_read dmax_ready dexp_ready da_ready dat_done dat_read do_done do_read
            rl_done rexp_in rexp_ready member_ready rank_done table_ready
            psel_ready g_done hsel_ready h_done sil_ready hid_ready t_done tsb_ready y_done ysb_ready
            expert_done acc_done y_out
            xp xg xh xH xsil xhid xT xt xY xy xdone xstep""".split()
        q = {n: sem(n) for n in names}
        (x_in, mem_in, small_in, const_in, tab_in, gain_in, mask_in, lam_in, t5_stored, t5_in,
         router_in, fgain_in, out_done, proj_done, proj_read_act, proj_read_dve, act_step, dve_step, upad_zero,
         table_rep, t5_rows, t5_read, vec_tr, vec_read, lb_zero, lb_exp, lam_dot, lam_exp,
         sq_act, ms_ready, rt_ready, rs_ready, xs_act, xs_dve, tr_done, hT_act, hT_dve, x_new,
         f_ready, ln_ready, k_ready, u_ready, conv_done, arg_ready, exp_ready, lev_ready,
         lev_done, lev_read, cross_done, cross_read, o_done, o_read, o_sq, oms_ready, ort_ready, on_ready,
         ot_done, ot_read, ct_done, cv_ready, cr_ready, cn_ready, cb_done, cb_read,
         xsc_done, xmax_ready, xexp_ready, xp_ready, xpt_done, xpt_read, xo_done, xo_read,
         dsc_done, dsc_read, dmax_ready, dexp_ready, da_ready, dat_done, dat_read, do_done, do_read,
         rl_done, rexp_in, rexp_ready, member_ready, rank_done, table_ready,
         psel_ready, g_done, hsel_ready, h_done, sil_ready, hid_ready, t_done, tsb_ready, y_done, ysb_ready,
         expert_done, acc_done, y_out,
         xp, xg, xh, xH, xsil, xhid, xT, xt, xY, xy, xdone, xstep) = (q[n] for n in names)
        XSTEPS = 4

        def col_unit(w, c, by_row):
            v = w.rearrange("(p k) n -> p k n", k=KD) if by_row else w.rearrange("(k p) n -> p k n", p=P)
            return v[:, :, c * 512:(c + 1) * 512]

        def proj_source(L, u):
            if u < 6:
                if L == 0:
                    return col_unit(a["even_w_in"][0], (1, 0, 4, 5, 2, 3)[u], True)
                return col_unit(a["odd_w_qkv"][0], u, True)
            if u < 10:
                return col_unit(a["xa_wkv"][L], u - 6, True)
            if u < 12:
                return col_unit((a["even_w_out"] if L == 0 else a["odd_w_out"])[0], u - 10, False)
            if u < 14:
                return col_unit(a["xa_wq"][L], u - 12, True)
            return col_unit(a["xa_wo"][L], u - 14, False)

        LAYER_UNITS = PROJ + EU * NE
        EX_DONE = NE + 1
        assert EU * 2 == SLOTS

        def slot(L, u):
            return (L * LAYER_UNITS + u) % SLOTS

        def arrival(L, u):
            return 16 * ((L * LAYER_UNITS + u) // SLOTS + 1)

        def read_count(L, u):
            mine = [v for v in range(u + 1) if (v in DVE_UNITS) == (u in DVE_UNITS)]
            per = len(DVE_UNITS) if u in DVE_UNITS else PROJ - len(DVE_UNITS)
            return (proj_read_dve if u in DVE_UNITS else proj_read_act), L * per + len(mine)

        def wait_read(eng, L, u):
            s_, v_ = read_count(L, u)
            eng.wait_ge(s_, v_)

        def wait_source(eng, n, blk):
            if n == N_MIX0:
                eng.wait_ge(x_in, 16)
            elif n == N_MEM:
                eng.wait_ge(mem_in, 16)
            elif n in (N_XA0, N_FFN0, N_XA1, N_FFN1):
                wait_read(eng, 0 if n in (N_XA0, N_FFN0) else 1, 11 if n in (N_XA0, N_XA1) else 15)
            else:
                eng.wait_ge(x_new, (2 if n == N_MIX1 else 4) - 1 + blk)

        def norm_buffers(n):
            if n == N_MEM:
                return kmem[:, :, :].rearrange("p a b -> p (a b)").rearrange("p (b d) -> p b d", b=TB), vmem, memT
            return x, xs, hT

        def rounds(e_, e):
            return (e_.value_load(xtab[0:1, bass.ds(e, 1)], min_val=0, max_val=64),
                    e_.value_load(xtab[0:1, bass.ds(e + 1, 1)], min_val=0, max_val=64))

        TAPS_PER_LEVEL = 3

        block = ctx.enter_context(nc.Block())

        @block.sync
        def _(sp):
            sp.dma_start(x[:, :, :], a["x"][0].rearrange("(b p) d -> p b d", p=P)).then_inc(x_in, 16)
            for L in range(DEPTH):
                for u in range(PROJ):
                    if u >= SLOTS:
                        sp.wait_ge(proj_done, L * PROJ + u - SLOTS + 1)
                    elif L > 0:
                        e = NE - 2 + u // EU
                        sp.wait_ge(expert_done, (L - 1) * EX_DONE + e + 2)
                    s_ = slot(L, u)
                    sp.dma_start(ring[:, s_, :].rearrange("p (k n) -> p k n", k=KD),
                                 proj_source(L, u)).then_inc(landed[s_], 16)

                def load_expert(e, j, r):
                    s_ = slot(L, PROJ + EU * j + r)
                    if r < 2:
                        w = a["moe_w1" if r == 0 else "moe_w3"][L]
                        sp.dma_start(ring[:, s_, :],
                                     w[bass.ds(e, 1), :, :].rearrange("e (p k) f -> p (e k f)", k=KD)
                                     ).then_inc(landed[s_], 16)
                    else:
                        w = a["moe_w2"][L]
                        sp.dma_start(ring[:, s_, :].rearrange("p (c n) -> p c n", c=2),
                                     w[bass.ds(e, 1), :, :].rearrange("e (c r m) d -> r (e c) (m d)", c=2, m=2)
                                     ).then_inc(landed[s_], 16)

                for j in range(2):
                    for r in range(EU):
                        sp.wait_ge(proj_done, L * PROJ + PROJ - SLOTS + EU * j + r + 1)
                        load_expert(j, j, r)
                with sp.Fori(1, NE // 2) as it:
                    for j in range(2):
                        sp.wait_ge(expert_done, it * 2 + (L * EX_DONE + j))
                        for r in range(EU):
                            load_expert(it * 2 + j, j, r)
            for b in range(TB):
                sp.wait_ge(y_out, b + 1)
                sp.dma_start(out[0].rearrange("(b p) d -> p b d", p=P)[:, b, :], xs[:, b, :]).then_inc(out_done, 16)
            sp.wait_ge(out_done, 32)

        @block.gpsimd
        def _(pool):
            for r, name in {R_DB: "conv_db", R_LNG: "conv_ln_g", R_LNB: "conv_ln_b", R_LB: "hgrn_lb"}.items():
                pool.dma_start(rows[r:r + 4, :], a[name][0].rearrange("(c p) -> c p", p=P)).then_inc(small_in, 16)
            pool.dma_start(rows[R_HG:R_HG + 1, :], a["hgrn_norm_g"]).then_inc(small_in, 16)
            pool.dma_start(rows[R_SUB:R_SUB + 1, :], a["subln_g"]).then_inc(small_in, 16)
            pool.dma_start(dwrows[0:CONVW, :], a["conv_dw"][0]).then_inc(small_in, 16)
            for i, name in enumerate(("lam_q1", "lam_k1", "lam_q2", "lam_k2")):
                pool.dma_start(lamrow[:, i, :], a[name].broadcast_to([P, 64])).then_inc(lam_in, 16)
            pool.wait_ge(vec_read, 2)
            pool.wait_ge(t5_read, DH)
            nc.gpsimd.memset(upad[:, :, 0:PAD], 0.0).then_inc(upad_zero, 1)

        @block.scalar
        def _(act):
            s = nc.scalar
            own = Own(act)
            act.dma_start(consts[:, :], a["consts"][:, 0:4 * P + NE]).then_inc(const_in, 16)
            act.dma_start(table[0:RELS, :], a["rel_bias"]).then_inc(tab_in, 16)
            act.dma_start(onehot[0:RELS + 1, :], a["onehot"]).then_inc(tab_in, 16)
            for n, (name, i) in enumerate([("norm_mix_g", 0), ("mem_norm_g", None), ("norm_xattn_g", 0),
                                           ("norm_ffn_g", 0), ("norm_mix_g", 1), ("norm_xattn_g", 1),
                                           ("norm_ffn_g", 1)]):
                v = a[name] if i is None else a[name][i]
                act.dma_start(gains[:, n, :], v.rearrange("(p k) -> p k", k=KD)).then_inc(gain_in, 16)
            act.dma_start(norm_buffers(N_MEM)[0], a["mem"][0].rearrange("(b p) d -> p b d", p=P)).then_inc(mem_in, 16)
            act.dma_start(masks[:, :, :], a["consts"][:, 4 * P + NE:].rearrange("p (l t) -> p l t", t=P)
                          ).then_inc(mask_in, 16)

            for h in range(DH):
                act.wait_ge(t5_rows, h + 1)
                own.inc(s.activation(bstage[:, h, :], ps[:, h, 0:BW], ACT.Copy), t5_read)
            own.wait()
            act.dma_start(bias_dram.ap().rearrange("h p j -> p h j"), bstage[:, :, :]).then_inc(t5_stored, 16)
            act.wait_ge(lb_zero, 1)
            own.inc(s.activation(lbe, lbz, ACT.Exp), lb_exp)
            act.wait_ge(lam_dot, 2)
            own.inc(s.activation(lamexp, lam2, ACT.Exp), lam_exp)

            def norm(n):
                src, dst, _ = norm_buffers(n)
                wait_source(act, n, 0)
                own.inc(s.activation(dst[:, 0, :], src[:, 0, :], ACT.Square, accum_out=ss[:, 0:1]), sq_act)
                act.wait_ge(ms_ready, n + 1)
                own.inc(s.activation(rt, ms, ACT.Sqrt), rt_ready)
                act.wait_ge(rs_ready, n + 1)
                ins = s.activation(dst[:, 0, :], src[:, 0, :], ACT.Copy, scale=rs[:, 0:1])
                own.inc(ins, xs_act)

            def norm_T(n):
                if n == N_MIX0:
                    act.wait_ge(gain_in, 16 * 7)
                for k in range(4):
                    if k % 2 == 0:
                        act.wait_ge(tr_done, 4 * n + k // 2 + 1)
                    own.inc(s.activation(norm_buffers(n)[2][:, k, :], bank(4 + k // 2)[:, (k % 2) * S:(k % 2 + 1) * S],
                                         ACT.Copy, scale=gains[:, n, k:k + 1]), hT_act)

            def read_unit(L, u, dst, func=ACT.Copy):
                act.wait_ge(proj_done, L * PROJ + u + 1)
                own.inc(s.activation(dst, pair(L * PROJ + u), func), proj_read_act)

            def read_unit_T(L, u, dst, func=ACT.Copy):
                act.wait_ge(proj_done, L * PROJ + u + 1)
                own.inc(s.activation(dst, pair(L * PROJ + u).rearrange("p a (f t) -> p (a f) t", f=2), func),
                        proj_read_act)

            def flat(v):
                return v.rearrange("p (a b) -> p a b", a=2)

            def mixer0():
                def level_exp(lev):
                    act.wait_ge(arg_ready, lev)
                    own.inc(s.activation(Ebuf[lev % 2], Ebuf[lev % 2], ACT.Exp), exp_ready)

                read_unit(0, 0, flat(fgate), ACT.Sigmoid)
                act.wait_ge(f_ready, 1)
                own.inc(s.activation(lntmp, lntmp, ACT.Ln), act_step)
                own.inc(s.activation(logf, logf, ACT.Ln), ln_ready)
                read_unit(0, 1, flat(qh), ACT.Silu)
                read_unit_T(0, 2, upad[:, :, PAD:])
                level_exp(1)
                read_unit(0, 3, flat(cacc[:, :, :].rearrange("p a b -> p (a b)")), ACT.Sigmoid)
                level_exp(2)
                read_unit(0, 4, vh[:, :, :])
                level_exp(3)
                read_unit(0, 5, gh[:, :, :], ACT.Sigmoid)
                level_exp(4)
                read_unit_T(0, 6, kmem[:, 0:4, :])
                level_exp(5)
                read_unit_T(0, 7, kmem[:, 4:8, :])
                level_exp(6)
                read_unit(0, 8, vmem[:, :, 0:512])
                level_exp(7)
                read_unit(0, 9, vmem[:, :, 512:1024])
                level_exp(8)
                act.wait_ge(o_done, 1)
                own.inc(s.activation(oh[:, :, :], ps[:, 4:6, :], ACT.Copy), o_read)
                own.wait()
                own.inc(s.activation(ohsq[:, :, :], oh[:, :, :], ACT.Square), o_sq)
                act.wait_ge(oms_ready, 1)
                own.inc(s.activation(ort[:, 0:8], oms[:, 0:8], ACT.Sqrt), ort_ready)
                act.wait_ge(ot_done, 1)
                own.inc(s.activation(hT[:, 0:4, :], ps[:, 6:8, :].rearrange("p a (f t) -> p (a f) t", f=2),
                                     ACT.Copy, scale=vecs[:, R_HG:R_HG + 1]), ot_read)
                act.wait_ge(cv_ready, 1)
                own.inc(s.activation(crt, cve, ACT.Sqrt), cr_ready)
                for c in range(HH):
                    if c % 2 == 0:
                        act.wait_ge(cb_done, c // 2 + 1)
                    own.inc(s.activation(hT[:, 4 + c, :], bank(4 + c // 2)[:, (c % 2) * S:(c % 2 + 1) * S], ACT.Silu,
                                         bias=vecs[:, R_LNB + c:R_LNB + c + 1],
                                         scale=vecs[:, R_LNG + c:R_LNG + c + 1]), cb_read)

            def mixer1():
                act.wait_ge(hT_act, 4 * (N_MIX1 + 1))
                act.dma_start(biasd[:, :, :], bass.AP(bias_dram, P - 1, [[BW - 1, P], [P * BW, DH], [1, 2 * P]])
                              ).then_inc(t5_in, 16)
                read_unit_T(1, 0, qd[:, 0:4, :])
                read_unit_T(1, 1, qd[:, 4:8, :])
                read_unit_T(1, 2, kd[:, 0:4, :])
                read_unit_T(1, 3, kd[:, 4:8, :])
                read_unit(1, 4, vd[:, :, 0:512])
                read_unit(1, 5, vd[:, :, 512:1024])

                def back(j):
                    h, i = j // 2, j % 2
                    act.wait_ge(dat_done, j + 1)
                    own.inc(s.activation(aTD[j % 2][:, 0:i + 1, :], bank(6)[:, 0:P * (i + 1)].rearrange(
                        "p (a b) -> p a b", b=P), ACT.Copy), dat_read)
                    act.wait_ge(do_done, j + 1)
                    own.inc(s.activation(od[:, i, h * P:(h + 1) * P], bank(7)[:, 0:P], ACT.Copy), do_read)

                for j in range(2 * DH):
                    nk = P * (j % 2 + 1)
                    act.wait_ge(dmax_ready, j + 1)
                    for m in range(2):
                        c = 2 * (j % 2) + m
                        own.inc(s.activation(sD[j % 2][:, m, 0:nk], sD[j % 2][:, m, 0:nk], ACT.Exp,
                                             bias=dmx[:, c:c + 1], accum_out=dsum[:, c:c + 1]), dexp_ready)
                    if j >= 1:
                        back(j - 1)
                    if j in (3, 6, 9, 12):
                        u = 6 + (j - 3) // 3
                        if u < 8:
                            read_unit_T(1, u, kmem[:, 4 * (u - 6):4 * (u - 5), :])
                        else:
                            read_unit(1, u, vmem[:, :, 512 * (u - 8):512 * (u - 7)])
                back(2 * DH - 1)
                own.wait()
                own.inc(s.activation(odsq[:, :, :], od[:, :, :], ACT.Square), o_sq)
                act.wait_ge(oms_ready, 2)
                own.inc(s.activation(ort, oms, ACT.Sqrt), ort_ready)
                for b in range(4):
                    act.wait_ge(ot_done, 2 + b)
                    own.inc(s.activation(hT[:, 2 * b:2 * b + 2, :], bank(4 + b).rearrange("p (f t) -> p f t", f=2),
                                         ACT.Copy, scale=sub), ot_read)

            def cross_attention(L):
                read_unit_T(L, 12, qx[:, 0:4, :])
                read_unit_T(L, 13, qx[:, 4:8, :])
                for c in range(4):
                    act.wait_ge(xmax_ready, 4 * L + c + 1)
                    for j in range(2):
                        own.inc(s.activation(px[:, c, j, :], bank(4 + c)[:, j * M:(j + 1) * M], ACT.Exp,
                                             bias=xmx[:, 2 * c + j:2 * c + j + 1], scale=1.0 / 16,
                                             accum_out=xsum[:, 2 * c + j:2 * c + j + 1]), xexp_ready)
                for c in range(4):
                    i, hp = c // 2, c % 2
                    act.wait_ge(xpt_done, 4 * L + c + 1)
                    own.inc(s.activation(pxT[:, :, 2 * hp:2 * hp + 2, i * P:(i + 1) * P],
                                         bank(4 + c).rearrange("p (m h t) -> p m h t", m=2, h=2), ACT.Copy), xpt_read)
                for b in range(4):
                    act.wait_ge(xo_done, 4 * L + b + 1)
                    own.inc(s.activation(hT[:, 2 * b:2 * b + 2, :], bank(4 + b).rearrange("p (f t) -> p f t", f=2),
                                         ACT.Copy), xo_read)

            def moe(L):
                act.dma_start(wr[:, :, 0:NG], a["moe_w_grp"][L].rearrange("(p k) n -> p k n", k=KD)).then_inc(router_in, 16)
                act.dma_start(wr[:, :, NG:], a["moe_w_exp"][L].rearrange("(p k) n -> p k n", k=KD)).then_inc(router_in, 16)
                act.dma_start(rbias[:, 0:NG], a["moe_b_grp"][L:L + 1, :].broadcast_to([P, NG])).then_inc(router_in, 16)
                act.dma_start(rbias[:, NG:], a["moe_b_exp"][L:L + 1, :].broadcast_to([P, NE])).then_inc(router_in, 16)
                if L == DEPTH - 1:
                    act.dma_start(fgain, a["final_norm_g"].unsqueeze(0).broadcast_to([P, D])).then_inc(fgain_in, 16)
                norm_T(N_FFN0 if L == 0 else N_FFN1)
                act.wait_ge(rexp_in, 2 * L + 1)
                own.inc(s.activation(r4[1], r4[0], ACT.Exp), rexp_ready)
                act.wait_ge(rexp_in, 2 * L + 2)
                own.inc(s.activation(r1[8], r1[7], ACT.Exp), rexp_ready)
                act.wait_ge(table_ready, L + 1)
                per = {sil_ready: 2, ysb_ready: 2}
                with act.Fori(0, NE // 2) as it:
                    own.enter(it, per)
                    for j in range(2):
                        act.wait_ge(h_done, it * 2 + (L * NE + j + 1))
                        own.inc(s.activation(sil, bank(4)[:, 0:S], ACT.Silu), sil_ready)
                        act.wait_ge(y_done, it * 2 + (L * NE + j + 1))
                        own.inc(s.activation(ysb[j], bank(5), ACT.Copy), ysb_ready)
                        x0, x1 = rounds(s, it * 2 + j)
                        with act.If(x1 > x0):
                            with act.Fori(x0, x1) as X:
                                act.wait_ge(xH, X + 1)
                                s.activation(silx, bank(4)[:, 0:S], ACT.Silu).then_inc(xsil, 1)
                                act.wait_ge(xY, X + 1)
                                s.activation(ysbx, bank(4), ACT.Copy).then_inc(xy, 1)
                    own.leave(NE // 2, per)

            norm(N_MIX0)
            norm_T(N_MIX0)
            norm(N_MEM)
            norm_T(N_MEM)
            mixer0()
            norm(N_XA0)
            norm_T(N_XA0)
            cross_attention(0)
            norm(N_FFN0)
            moe(0)
            norm(N_MIX1)
            norm_T(N_MIX1)
            mixer1()
            norm(N_XA1)
            norm_T(N_XA1)
            cross_attention(1)
            norm(N_FFN1)
            moe(1)
            norm(N_FINAL)

        @block.vector
        def _(dve):
            v = nc.vector
            own = Own(dve)

            def step(ins, sem_=None):
                own.inc(ins, dve_step if sem_ is None else sem_)
                own.wait()

            step(v.memset(table[RELS:RELS + 1, :], -BIG))
            dve.wait_ge(tab_in, 32)
            step(v.tensor_copy(tablerep[0:RELS + 1, :, :],
                               table[0:RELS + 1, :].unsqueeze(2).to_broadcast([RELS + 1, DH, P])), table_rep)
            dve.wait_ge(vec_tr, 1)
            own.inc(v.tensor_copy(vecs[:, 0:ROWS], bank(0)[:, 0:ROWS]), vec_read)
            step(v.tensor_copy(dwT[:, :, :], bank(0)[:, 32:32 + HH * 32].rearrange("p (c j) -> p c j", c=HH)[:, :, 0:CONVW]),
                 vec_read)
            lbv = vecs[:, R_LB:R_LB + 4]
            step(v.tensor_tensor(lbz, lbv, lbv, ALU.subtract), lb_zero)
            dve.wait_ge(lb_exp, 1)
            step(v.reciprocal(lbr, lbe))
            step(v.tensor_tensor(lbp, lbe, lbr, ALU.mult))
            step(v.tensor_tensor(lb, lbp, lbp, ALU.subtract))
            step(v.tensor_scalar(oml, lb, -1.0, 1.0, ALU.mult, ALU.add))
            step(v.tensor_scalar(sub, vecs[:, R_SUB:R_SUB + 1], 1.0 - LAM_INIT, None, ALU.mult))
            dve.wait_ge(lam_in, 16 * 4)
            for i in range(2):
                own.inc(v.tensor_tensor_reduce(lamrow[:, 2 * i, :], lamrow[:, 2 * i, :], lamrow[:, 2 * i + 1, :], 1.0, 0.0,
                                               ALU.mult, ALU.add, lam2[:, i:i + 1]), lam_dot)
            dve.wait_ge(lam_exp, 1)
            step(v.tensor_tensor(lamd, lamexp[:, 1:2], lamexp[:, 0:1], ALU.subtract))
            step(v.tensor_scalar(nlam, lamd, LAM_INIT, None, ALU.subtract))

            def norm(n):
                src, dst, _ = norm_buffers(n)
                wait_source(dve, n, 1)
                step(v.tensor_tensor_reduce(dst[:, 1, :], src[:, 1, :], src[:, 1, :], 1.0, 0.0, ALU.mult, ALU.add,
                                            ss[:, 1:2]))
                dve.wait_ge(sq_act, n + 1)
                own.inc(v.tensor_scalar(ms, ss, 1.0 / D, EPS, ALU.mult, ALU.add), ms_ready)
                dve.wait_ge(rt_ready, n + 1)
                step(v.reciprocal(rs, rt), rs_ready)
                step(v.tensor_scalar(dst[:, 1, :], src[:, 1, :], rs[:, 1:2], None, ALU.mult), xs_dve)

            def norm_T(n):
                if n == N_MIX0:
                    dve.wait_ge(gain_in, 16 * 7)
                for k in range(4, 8):
                    if k % 2 == 0:
                        dve.wait_ge(tr_done, 4 * n + k // 2 + 1)
                    own.inc(v.tensor_scalar(norm_buffers(n)[2][:, k, :], bank(4 + k // 2)[:, (k % 2) * S:(k % 2 + 1) * S],
                                            gains[:, n, k:k + 1], None, ALU.mult), hT_dve)
                own.wait()

            def add_unit(L, u):
                h = (u % 2) * 512
                dve.wait_ge(proj_done, L * PROJ + u + 1)
                step(v.tensor_tensor(x[:, :, h:h + 512], x[:, :, h:h + 512], pair(L * PROJ + u), ALU.add), proj_read_dve)

            def head_norm(o, osq, nh, blocks):
                n = nh * TB
                dve.wait_ge(o_sq, blocks)
                step(v.tensor_reduce(oss[:, 0:n], osq.rearrange("p b (h c) -> p (b h) c", c=P), AX.X, ALU.add))
                own.inc(v.tensor_scalar(oms[:, 0:n], oss[:, 0:n], 1.0 / P, EPS, ALU.mult, ALU.add), oms_ready)
                dve.wait_ge(ort_ready, blocks)
                step(v.reciprocal(ors[:, 0:n], ort[:, 0:n]))

            def mixer0():
                wait_read(dve, 0, 0)
                for h in range(HH):
                    own.inc(v.tensor_scalar(fgate[:, h * S:(h + 1) * S], fgate[:, h * S:(h + 1) * S],
                                            oml[:, h:h + 1], lb[:, h:h + 1], ALU.mult, ALU.add), dve_step)
                own.wait()
                step(v.tensor_scalar(lntmp, fgate, 1e-30, LN_SPLIT, ALU.max, ALU.mult))
                own.inc(v.tensor_scalar(logf, fgate, 1.0 / LN_SPLIT, None, ALU.max), dve_step)
                step(v.tensor_scalar(lntmp, lntmp, 1.0, None, ALU.min), f_ready)
                own.inc(v.tensor_scalar(kh, fgate, -1.0, 1.0, ALU.mult, ALU.add), k_ready)
                step(v.memset(scanmask, 1.0))
                step(v.memset(scanmask.rearrange("p (a b) -> p a b", b=P)[:, :, 0:1], 0.0))
                dve.wait_ge(ln_ready, 1)
                step(v.tensor_tensor(logf, logf, lntmp, ALU.add))
                step(v.tensor_tensor_scan(bcum, scanmask, logf, 0.0, ALU.mult, ALU.add))
                dve.wait_ge(t5_stored, 16)
                for b_ in (*Qt, *Kt):
                    own.inc(v.memset(b_, 0.0), dve_step)
                own.wait()
                dve.wait_ge(mask_in, 16)

                def halves(b_, lev):
                    m = 2 ** (lev - 1)
                    w = b_.rearrange("p (n s m) -> p n s m", s=2, m=m)
                    return w[:, :, 0, :], w[:, :, 1, :], m

                def args(lev):
                    b0, b1, m = halves(bcum, lev)
                    e0, e1, _ = halves(Ebuf[lev % 2], lev)
                    ref = b0[:, :, m - 1:m].to_broadcast([P, 512 // m, m])
                    own.inc(v.tensor_tensor(e0, ref, b0, ALU.subtract), dve_step)
                    if m < P:
                        ins = v.tensor_tensor(e1, b1, ref, ALU.subtract)
                    else:
                        ins = v.tensor_copy(e1, b1)
                    step(ins, arg_ready)

                def mul(lev):
                    q0_, q1_, _ = halves(Qt[lev % 2], lev)
                    k0_, k1_, _ = halves(Kt[lev % 2], lev)
                    e0, e1, _ = halves(Ebuf[lev % 2], lev)
                    dve.wait_ge(exp_ready, lev)
                    if lev == 1:
                        wait_read(dve, 0, 1)
                    own.inc(v.tensor_tensor(q1_, halves(qh, lev)[1], e1, ALU.mult), dve_step)
                    step(v.tensor_tensor(k0_, halves(kh, lev)[0], e0, ALU.mult), lev_ready)

                def take(lev):
                    b_ = 4 + 2 * (lev % 2)
                    src = ps[:, b_:b_ + 2, :].rearrange("p a (n t) -> p (a n) t", t=P)
                    mk = masks[:, lev:lev + 1, :].to_broadcast([P, 8, P])
                    dve.wait_ge(lev_done, lev + 1)
                    if lev == 0:
                        step(v.tensor_tensor(scoresT, src, mk, ALU.mult), lev_read)
                    else:
                        t_ = lntmp.rearrange("p (n t) -> p n t", t=P)
                        step(v.tensor_tensor(t_, src, mk, ALU.mult), lev_read)
                        step(v.tensor_tensor(scoresT, scoresT, t_, ALU.add))

                taps = iter(range(CONVW))

                def tap():
                    j = next(taps, None)
                    if j is None:
                        return
                    for c in range(HH):
                        w = dwT[:, c, j:j + 1]
                        if j == 0:
                            ins = v.tensor_scalar(cacc[:, c, :], upad[:, c, 0:S], w, vecs[:, R_DB + c:R_DB + c + 1],
                                                  ALU.mult, ALU.add)
                        else:
                            ins = v.scalar_tensor_tensor(out=cacc[:, c, :], in0=upad[:, c, j:j + S], scalar=w,
                                                         in1=cacc[:, c, :], op0=ALU.mult, op1=ALU.add)
                        own.inc(ins, conv_done if j == CONVW - 1 else dve_step)
                    own.wait()

                args(1)
                args(2)
                mul(1)
                wait_read(dve, 0, 3)
                step(v.tensor_tensor(upad[:, :, PAD:], upad[:, :, PAD:], cacc[:, :, :], ALU.mult), u_ready)
                dve.wait_ge(upad_zero, 1)
                for lev in range(3, LEVELS + 2):
                    args(lev)
                    take(lev - 3)
                    mul(lev - 1)
                    for _ in range(TAPS_PER_LEVEL):
                        tap()
                take(LEVELS - 1)
                mul(LEVELS + 1)
                take(LEVELS)
                dve.wait_ge(cross_done, 1)
                step(v.tensor_copy(crossT[:, :, :], bank(4).rearrange("p (n t) -> p n t", t=P)), cross_read)
                for _ in range(CONVW):
                    tap()
                head_norm(ohsq, ohsq, HH, 1)
                o_ = oh[:, :, :].rearrange("p b (h c) -> p (b h) c", c=P)
                step(v.tensor_tensor(o_, o_, ors[:, 0:8].unsqueeze(2).to_broadcast([P, 8, P]), ALU.mult))
                step(v.tensor_tensor(oh[:, :, :], oh[:, :, :], gh[:, :, :], ALU.mult), on_ready)
                dve.wait_ge(ct_done, 1)
                for b_ in range(TB):
                    own.inc(v.bn_stats(bn[:, 6 * b_:6 * b_ + 6], bank(4 + b_)), dve_step)
                own.wait()
                for b_ in range(TB):
                    own.inc(v.bn_aggr(mv[:, 2 * b_:2 * b_ + 2], bn[:, 6 * b_:6 * b_ + 6]), dve_step)
                own.wait()
                own.inc(v.tensor_scalar(cve, mv.rearrange("p (b t) -> p b t", t=2)[:, :, 1], EPS, None, ALU.add), cv_ready)
                dve.wait_ge(cr_ready, 1)
                step(v.reciprocal(crs, crt))
                for b_ in range(TB):
                    own.inc(v.tensor_scalar(cnorm[:, b_, :], bank(4 + b_), mv[:, 2 * b_:2 * b_ + 1], crs[:, b_:b_ + 1],
                                            ALU.subtract, ALU.mult), cn_ready)
                add_unit(0, 10)
                add_unit(0, 11)

            def mixer1():
                dve.wait_ge(t5_in, 16)
                def front(j):
                    h, i = j // 2, j % 2
                    nk = P * (i + 1)
                    dve.wait_ge(dsc_done, j + 1)
                    step(v.scalar_tensor_tensor(out=sD[j % 2][:, :, 0:nk], in0=ps[:, 4:6, 0:nk], scalar=0.125,
                                                in1=biasd[:, h:h + 1, 2 * P - nk:2 * P].to_broadcast([P, 2, nk]),
                                                op0=ALU.mult, op1=ALU.add), dsc_read)
                    own.inc(v.tensor_reduce(dmx[:, 2 * i:2 * i + 2], sD[j % 2][:, :, 0:nk], AX.X, ALU.max, negate=True),
                            dmax_ready)

                def back(j):
                    i = j % 2
                    nk = P * (i + 1)
                    dve.wait_ge(dexp_ready, 2 * j + 2)
                    step(v.reciprocal(drc[:, 2 * i:2 * i + 2], dsum[:, 2 * i:2 * i + 2]))
                    step(v.tensor_scalar(drc[:, 2 * i + 1:2 * i + 2], drc[:, 2 * i + 1:2 * i + 2], nlam, None, ALU.mult))
                    step(v.tensor_scalar(sD[i][:, 1, 0:nk], sD[i][:, 1, 0:nk], drc[:, 2 * i + 1:2 * i + 2], None, ALU.mult))
                    own.inc(v.scalar_tensor_tensor(out=aD[i][:, 0:nk], in0=sD[i][:, 0, 0:nk], scalar=drc[:, 2 * i:2 * i + 1],
                                                   in1=sD[i][:, 1, 0:nk], op0=ALU.mult, op1=ALU.add), da_ready)

                front(0)
                for j in range(2 * DH):
                    if j + 1 < 2 * DH:
                        if j >= 1:
                            own.wait()
                        front(j + 1)
                    back(j)
                own.wait()
                head_norm(od, odsq, DH, 2)
                for b_ in range(TB):
                    o_ = od[:, b_, :].rearrange("p (h c) -> p h c", c=P)
                    own.inc(v.tensor_tensor(o_, o_, ors[:, 8 * b_:8 * b_ + 8].unsqueeze(2).to_broadcast([P, 8, P]),
                                            ALU.mult), on_ready)
                add_unit(1, 10)
                add_unit(1, 11)

            def cross_attention(L):
                for c in range(4):
                    dve.wait_ge(xsc_done, 4 * L + c + 1)
                    step(v.tensor_reduce(xmx[:, 2 * c:2 * c + 2], bank(4 + c).rearrange("p (h m) -> p h m", h=2),
                                         AX.X, ALU.max, negate=True))
                    own.inc(v.tensor_scalar(xmx[:, 2 * c:2 * c + 2], xmx[:, 2 * c:2 * c + 2], 1.0 / 16, None, ALU.mult),
                            xmax_ready)
                for c in range(4):
                    dve.wait_ge(xexp_ready, 8 * L + 2 * c + 2)
                    step(v.reciprocal(xrc[:, 2 * c:2 * c + 2], xsum[:, 2 * c:2 * c + 2]))
                    own.inc(v.tensor_tensor(px[:, c, :, :], px[:, c, :, :],
                                            xrc[:, 2 * c:2 * c + 2].unsqueeze(2).to_broadcast([P, 2, M]), ALU.mult), xp_ready)
                add_unit(L, 14)
                add_unit(L, 15)

            def moe(L):
                n = N_FFN0 if L == 0 else N_FFN1
                norm_T(n)
                own.inc(v.memset(zeros, 0.0), dve_step)
                own.inc(v.memset(tsb[1], 0.0), dve_step)
                own.inc(v.memset(ysb[1], 0.0), ysb_ready)
                own.inc(v.memset(rank[:, :, NE:], -1.0), dve_step)
                if L == 0:
                    own.inc(v.memset(xcarry, 0.0), xstep)
                tie2 = ties.unsqueeze(1).to_broadcast([P, TB, NE])
                tie4 = ties[:, NE - NG:].unsqueeze(1).to_broadcast([P, TB, NG])
                g4, e16 = lg[:, :, 0:NG], lg[:, :, NG:]
                wide4 = lambda c: c.to_broadcast([P, TB, NG])
                wide = lambda c: c.to_broadcast([P, TB, NE])
                dve.wait_ge(router_in, 64 * (L + 1))
                dve.wait_ge(rl_done, L + 1)
                step(v.tensor_tensor(lg, bank(4)[:, 0:TB * (NG + NE)].rearrange("p (b n) -> p b n", b=TB),
                                     rbias.unsqueeze(1).to_broadcast([P, TB, NG + NE]), ALU.add))
                step(v.tensor_reduce(r1[0], g4, AX.X, ALU.max))
                step(v.tensor_tensor(r4[0], g4, wide4(r1[0]), ALU.subtract), rexp_in)
                step(v.tensor_scalar(r4[2], r4[0], 0.0, None, ALU.is_equal))
                step(v.tensor_tensor(r4[2], r4[2], tie4, ALU.mult))
                step(v.tensor_reduce(r1[1], r4[2], AX.X, ALU.max))
                step(v.tensor_tensor(r4[3], r4[2], wide4(r1[1]), ALU.is_equal))
                step(v.tensor_scalar(r4[2], r4[3], BIG, BIG, ALU.mult, ALU.subtract))
                step(v.tensor_tensor(r16[0].rearrange("p b (g e) -> p b g e", g=NG), e16.rearrange("p b (g e) -> p b g e", g=NG),
                                     r4[2].unsqueeze(3).to_broadcast([P, TB, NG, EPG]), ALU.add))
                step(v.tensor_reduce(r1[4], r16[0], AX.X, ALU.max))
                step(v.tensor_tensor(r16[1], r16[0], wide(r1[4]), ALU.is_equal))
                step(v.tensor_tensor(r16[2], r16[1], tie2, ALU.mult))
                step(v.tensor_reduce(r1[5], r16[2], AX.X, ALU.max))
                step(v.tensor_tensor(r16[3], r16[2], wide(r1[5]), ALU.is_equal))
                step(v.tensor_scalar(r16[4], r16[3], -2 * BIG, None, ALU.mult))
                step(v.tensor_tensor(r16[4], r16[4], r16[0], ALU.add))
                step(v.tensor_reduce(r1[6], r16[4], AX.X, ALU.max))
                step(v.tensor_tensor(r1[7], r1[6], r1[4], ALU.subtract), rexp_in)
                step(v.tensor_tensor(r16[1], r16[4], wide(r1[6]), ALU.is_equal))
                step(v.tensor_tensor(r16[2], r16[1], tie2, ALU.mult))
                step(v.tensor_reduce(r1[5], r16[2], AX.X, ALU.max))
                step(v.tensor_tensor(r16[5], r16[2], wide(r1[5]), ALU.is_equal))
                step(v.tensor_tensor(r16[1], r16[3], r16[5], ALU.add), member_ready)
                dve.wait_ge(rexp_ready, 2 * L + 2)
                step(v.tensor_reduce(r1[2], r4[1], AX.X, ALU.add))
                step(v.reciprocal(r1[3], r1[2]))
                step(v.tensor_scalar(r1[9], r1[8], 1.0, None, ALU.add))
                step(v.reciprocal(r1[5], r1[9]))
                step(v.tensor_tensor(r1[0], r1[3], r1[5], ALU.mult))
                step(v.tensor_tensor(r1[1], r1[0], r1[8], ALU.mult))
                step(v.tensor_tensor(r16[6], r16[3], wide(r1[0]), ALU.mult))
                step(v.tensor_tensor(r16[7], r16[5], wide(r1[1]), ALU.mult))
                step(v.tensor_tensor(gate, r16[6], r16[7], ALU.add))
                dve.wait_ge(rank_done, L + 1)
                rk = rank[:, :, 0:NE]
                step(v.tensor_scalar(rk, bank(5)[:, 0:TB * NE].rearrange("p (b e) -> p b e", b=TB), 1.0, None, ALU.add))
                step(v.tensor_tensor(rk, rk, r16[1], ALU.mult))
                step(v.tensor_scalar(rk, rk, 1.0, None, ALU.subtract))
                cnt = bank(5)[:, TB * NE:(TB + 1) * NE]
                step(v.tensor_scalar(nx, cnt, float(CAP), None, ALU.is_gt))
                for i in range(2, S // CAP):
                    step(v.tensor_scalar(cumx[:, 0:NE], cnt, float(CAP * i), None, ALU.is_gt))
                    step(v.tensor_tensor(nx, nx, cumx[:, 0:NE], ALU.add))
                step(v.tensor_copy(cumx[:, 0:1], xcarry))
                step(v.tensor_tensor_scan(cumx[:, 1:NE + 1], ones[:, 0:NE], nx, xcarry, ALU.mult, ALU.add))
                step(v.tensor_copy(xcarry, cumx[:, NE:NE + 1]))
                step(v.tensor_copy(xtab[:, :], cumx), table_ready)

                def at(t, b_, e):
                    return t[:, b_, bass.ds(e, 1)]

                def build_psel(e):
                    for b_ in range(TB):
                        for j in range(2):
                            last = b_ == TB - 1 and j == 1
                            own.inc(v.tensor_scalar(psel[:, b_, j * CAP:(j + 1) * CAP], iota[:, 0:CAP],
                                                    at(rank, b_, e + j), None, ALU.is_equal),
                                    psel_ready if last else dve_step)

                def build_pgate(e, j):
                    for b_ in range(TB):
                        own.inc(v.tensor_scalar(pgate[j][:, b_, :], iota, at(rank, b_, e), at(gate, b_, e),
                                                ALU.is_equal, ALU.mult), dve_step)

                def take_gather(half, g):
                    dve.wait_ge(g_done, g)
                    own.inc(v.tensor_tensor(hsel[:, 4 * half:4 * half + 4, :], bank(6).rearrange("p (k t) -> p k t", t=P),
                                            gains[:, n, 4 * half:4 * half + 4].unsqueeze(2).to_broadcast([P, 4, P]),
                                            ALU.mult), hsel_ready)

                GB = (NE + 2) * L
                build_psel(0)
                take_gather(0, GB + 1)
                take_gather(1, GB + 2)
                own.wait()
                per = {dve_step: 3 + 4, psel_ready: 1, hid_ready: 2, tsb_ready: 2, hsel_ready: 2}
                with dve.Fori(0, NE // 2) as it:
                    own.enter(it, per)
                    for j in range(2):
                        e = it * 2 + j
                        build_pgate(e, j)
                        if j == 0:
                            build_psel(e + 2)
                        else:
                            dve.wait_ge(h_done, it * 2 + (L * NE + 2))
                            take_gather(0, it * 2 + (GB + 3))
                        dve.wait_ge(sil_ready, it * 2 + (L * NE + j + 1))
                        own.inc(v.tensor_tensor(hid, sil, bank(4)[:, S:2 * S], ALU.mult), hid_ready)
                        if j == 1:
                            take_gather(1, it * 2 + (GB + 4))
                        dve.wait_ge(t_done, it * 2 + (L * NE + j + 1))
                        own.inc(v.tensor_copy(tsb[j], bank(7)), tsb_ready)
                        further(e, n)
                    own.leave(NE // 2, per)
                dve.wait_ge(acc_done, L + 1)
                for b_ in range(TB):
                    own.inc(v.tensor_tensor(x[:, b_, :].rearrange("p (c n) -> p c n", c=2),
                                            x[:, b_, :].rearrange("p (c n) -> p c n", c=2),
                                            ps[:, 2 * b_:2 * b_ + 2, :], ALU.add), x_new)
                own.wait()

            def further(e, n):
                x0, x1 = rounds(v, e)
                with dve.If(x1 > x0):
                    with dve.Fori(x0, x1) as X:
                        own.wait()
                        dve.wait_ge(xdone, X + 1)
                        dve.wait_ge(xstep, X * XSTEPS + 1)
                        r_ = rank[:, :, bass.ds(e, 1)]
                        v.tensor_scalar(r_, r_, float(CAP), None, ALU.subtract).then_inc(xstep, 1)
                        dve.wait_ge(xstep, X * XSTEPS + 2)
                        for b_ in range(TB):
                            v.tensor_scalar(pselx[:, b_, :], iota[:, 0:CAP], rank[:, b_, bass.ds(e, 1)], None,
                                            ALU.is_equal).then_inc(xstep, 1)
                        for b_ in range(TB):
                            v.tensor_scalar(pgatex[:, b_, :], iota, rank[:, b_, bass.ds(e, 1)],
                                            gate[:, b_, bass.ds(e, 1)], ALU.is_equal, ALU.mult
                                            ).then_inc(xstep if b_ == 0 else xp, 1)
                        dve.wait_ge(xg, X + 1)
                        v.tensor_tensor(hselx, bank(4).rearrange("p (k t) -> p k t", k=KD),
                                        gains[:, n, :].unsqueeze(2).to_broadcast([P, KD, CAP]), ALU.mult).then_inc(xh, 1)
                        dve.wait_ge(xsil, X + 1)
                        v.tensor_tensor(hidx, silx, bank(4)[:, S:2 * S], ALU.mult).then_inc(xhid, 1)
                        dve.wait_ge(xT, X + 1)
                        v.tensor_copy(tsbx, bank(7)).then_inc(xt, 1)

            norm(N_MIX0)
            norm_T(N_MIX0)
            norm(N_MEM)
            norm_T(N_MEM)
            mixer0()
            norm(N_XA0)
            norm_T(N_XA0)
            cross_attention(0)
            norm(N_FFN0)
            moe(0)
            norm(N_MIX1)
            norm_T(N_MIX1)
            mixer1()
            norm(N_XA1)
            norm_T(N_XA1)
            cross_attention(1)
            norm(N_FFN1)
            moe(1)
            norm(N_FINAL)
            dve.wait_ge(fgain_in, 16)
            dve.wait_ge(xs_act, N_FINAL + 1)
            for b_ in range(TB):
                own.inc(v.tensor_tensor(xs[:, b_, :], xs[:, b_, :], fgain, ALU.mult), y_out)

        @block.tensor
        def _(pe):
            t = nc.tensor

            pe.wait_ge(const_in, 16)
            pe.wait_ge(tab_in, 32)
            pe.wait_ge(table_rep, 1)
            for h in range(DH):
                t.matmul(ps[:, h, 0:BW], tablerep[0:RELS + 1, h, :], onehot[0:RELS + 1, :], start=True, stop=True
                         ).then_inc(t5_rows, 1)
            pe.wait_ge(small_in, 16 * 7)
            pe.wait_ge(t5_read, 1)
            t.transpose(bank(0)[:, 0:ROWS], rows[0:ROWS, :], ident[0:ROWS, 0:ROWS])
            for c in range(HH):
                ins = t.transpose(bank(0)[:, 32 + 32 * c:32 + 32 * c + CONVW], dwrows[0:CONVW, c * P:(c + 1) * P],
                                  ident[0:CONVW, 0:CONVW])
            ins.then_inc(vec_tr, 1)
            pe.wait_ge(t5_read, DH)

            def norm_T(n):
                dst = norm_buffers(n)[1]
                if n == N_MEM:
                    pe.wait_ge(hT_act, 4 * n)
                    pe.wait_ge(hT_dve, 4 * n)
                pe.wait_ge(xs_act, n + 1)
                pe.wait_ge(xs_dve, n + 1)
                for k in range(KD):
                    for b in range(TB):
                        at = (k % 2) * S + b * P
                        ins = t.transpose(bank(4 + k // 2)[:, at:at + P],
                                          dst[:, b, :].rearrange("p (r k) -> p k r", k=KD)[:, k, :], ident)
                    if k % 2 == 1:
                        ins.then_inc(tr_done, 1)

            def wait_hT(n):
                pe.wait_ge(hT_act, 4 * (n + 1))
                pe.wait_ge(hT_dve, 4 * (n + 1))

            def unit(L, u, src, transposed):
                pj = L * PROJ + u
                if pj >= 2:
                    wait_read(pe, *divmod(pj - 2, PROJ))
                pe.wait_ge(landed[slot(L, u)], arrival(L, u))
                w = ring[:, slot(L, u), :].rearrange("p (k n) -> p k n", k=KD)
                dst = pair(pj)
                if transposed:
                    for f in range(4):
                        for k in range(KD):
                            ins = t.matmul(dst[:, f // 2, (f % 2) * S:(f % 2 + 1) * S], w[:, k, f * P:(f + 1) * P],
                                           src[:, k, :], start=(k == 0), stop=(k == KD - 1))
                else:
                    for b in range(TB):
                        for k in range(KD):
                            ins = t.matmul(dst[:, b, :], src[:, k, b * P:(b + 1) * P], w[:, k, :],
                                           start=(k == 0), stop=(k == KD - 1))
                ins.then_inc(proj_done, 1)

            def mixer0():
                def level(lev):
                    if lev == 0:
                        kk, qq = kh, qh
                        pe.wait_ge(k_ready, 1)
                        wait_read(pe, 0, 1)
                    else:
                        kk, qq = Kt[lev % 2], Qt[lev % 2]
                        pe.wait_ge(lev_ready, lev)
                    if lev == LEVELS + 1:
                        pe.wait_ge(lev_read, LEVELS)
                        for h in range(HH):
                            ins = t.matmul(bank(4)[:, h * P:(h + 1) * P], kk[:, h * S:h * S + P],
                                           qq[:, h * S + P:(h + 1) * S], start=True, stop=True)
                        ins.then_inc(cross_done, 1)
                        return
                    if lev >= 2:
                        pe.wait_ge(lev_read, lev - 1)
                    for i in range(8):
                        at = i * P
                        ins = t.matmul(bank(4 + 2 * (lev % 2) + i // 4)[:, (i % 4) * P:(i % 4 + 1) * P],
                                       kk[:, at:at + P], qq[:, at:at + P], start=True, stop=True)
                    ins.then_inc(lev_done, 1)

                wait_hT(N_MIX0)
                for u in range(4):
                    unit(0, u, hT, True)
                wait_hT(N_MEM)
                level(0)
                unit(0, 4, hT, False)
                level(1)
                unit(0, 5, hT, False)
                level(2)
                unit(0, 6, memT, True)
                level(3)
                unit(0, 7, memT, True)
                level(4)
                unit(0, 8, memT, False)
                level(5)
                unit(0, 9, memT, False)
                level(6)
                level(7)
                level(8)
                wait_read(pe, 0, 4)
                pe.wait_ge(lev_read, LEVELS + 1)
                pe.wait_ge(cross_read, 1)
                for h in range(HH):
                    hv = slice(h * P, (h + 1) * P)
                    t.matmul(bank(4)[:, hv], scoresT[:, 2 * h, :], vh[:, 0, hv], start=True, stop=True)
                for h in range(HH):
                    hv = slice(h * P, (h + 1) * P)
                    t.matmul(bank(5)[:, hv], scoresT[:, 2 * h + 1, :], vh[:, 1, hv], start=True, stop=False)
                    ins = t.matmul(bank(5)[:, hv], crossT[:, h, :], vh[:, 0, hv], start=False, stop=True)
                ins.then_inc(o_done, 1)
                pe.wait_ge(conv_done, HH)
                pe.wait_ge(o_read, 1)
                for b in range(TB):
                    for c in range(HH):
                        ins = t.transpose(bank(4 + b)[:, c * P:(c + 1) * P], cacc[:, c, b * P:(b + 1) * P], ident)
                ins.then_inc(ct_done, 1)
                pe.wait_ge(on_ready, 1)
                for h in range(HH):
                    for b in range(TB):
                        at = (h % 2) * S + b * P
                        ins = t.transpose(bank(6 + h // 2)[:, at:at + P], oh[:, b, h * P:(h + 1) * P], ident)
                ins.then_inc(ot_done, 1)
                pe.wait_ge(cn_ready, TB)
                for c in range(HH):
                    for b in range(TB):
                        at = (c % 2) * S + b * P
                        ins = t.transpose(bank(4 + c // 2)[:, at:at + P], cnorm[:, b, c * P:(c + 1) * P], ident)
                    if c % 2 == 1:
                        ins.then_inc(cb_done, 1)
                pe.wait_ge(ot_read, 1)
                pe.wait_ge(cb_read, HH)
                unit(0, 10, hT, False)
                unit(0, 11, hT, False)

            def mixer1():
                wait_hT(N_MIX1)
                for u in range(4):
                    unit(1, u, hT, True)
                unit(1, 4, hT, False)
                unit(1, 5, hT, False)

                def scores(j):
                    h, i = j // 2, j % 2
                    if j >= 1:
                        pe.wait_ge(dsc_read, j)
                    for m in range(2):
                        mp = slice(64 * m, 64 * m + 64)
                        ins = t.matmul(bank(4 + m)[:, 0:P * (i + 1)], qd[mp, h, i * P:(i + 1) * P],
                                       kd[mp, h, 0:P * (i + 1)], start=True, stop=True)
                    ins.then_inc(dsc_done, 1)

                wait_read(pe, 1, 3)
                scores(0)
                for j in range(2 * DH):
                    h, i = j // 2, j % 2
                    if j + 1 < 2 * DH:
                        scores(j + 1)
                    if j in (1, 4, 7, 10):
                        u = 6 + (j - 1) // 3
                        unit(1, u, memT, u < 8)
                    pe.wait_ge(da_ready, j + 1)
                    if j >= 1:
                        pe.wait_ge(dat_read, j)
                    for c in range(i + 1):
                        ins = t.transpose(bank(6)[:, c * P:(c + 1) * P], aD[j % 2][:, c * P:(c + 1) * P], ident)
                    ins.then_inc(dat_done, 1)
                    pe.wait_ge(dat_read, j + 1)
                    wait_read(pe, 1, 5)
                    if j >= 1:
                        pe.wait_ge(do_read, j)
                    for c in range(i + 1):
                        ins = t.matmul(bank(7)[:, 0:P], aTD[j % 2][:, c, :], vd[:, c, h * P:(h + 1) * P],
                                       start=(c == 0), stop=(c == i))
                    ins.then_inc(do_done, 1)
                pe.wait_ge(do_read, 2 * DH)
                pe.wait_ge(on_ready, 1 + TB)
                for h in range(DH):
                    for b in range(TB):
                        at = (h % 2) * S + b * P
                        ins = t.transpose(bank(4 + h // 2)[:, at:at + P], od[:, b, h * P:(h + 1) * P], ident)
                    if h % 2 == 1:
                        ins.then_inc(ot_done, 1)
                pe.wait_ge(ot_read, 5)
                unit(1, 10, hT, False)
                unit(1, 11, hT, False)

            def cross_attention(L):
                n = N_XA0 if L == 0 else N_XA1
                norm_T(n)
                wait_hT(n)
                unit(L, 12, hT, True)
                unit(L, 13, hT, True)
                wait_read(pe, L, 9)
                wait_read(pe, L, 13)
                for c in range(4):
                    i, hp = c // 2, c % 2
                    for j in range(2):
                        for k in range(2):
                            f = 2 * (2 * hp + j) + k
                            ins = t.matmul(bank(4 + c)[:, j * M:(j + 1) * M], qx[:, f, i * P:(i + 1) * P],
                                           kmem[:, f, :], start=(k == 0), stop=(k == 1))
                    ins.then_inc(xsc_done, 1)
                for c in range(4):
                    pe.wait_ge(xp_ready, 4 * L + c + 1)
                    for m in range(2):
                        for j in range(2):
                            at = (2 * m + j) * P
                            ins = t.transpose(bank(4 + c)[:, at:at + P], px[:, c, j, m * P:(m + 1) * P], ident)
                    ins.then_inc(xpt_done, 1)
                pe.wait_ge(xpt_read, 4 * (L + 1))
                for f in range(KD):
                    for m in range(2):
                        ins = t.matmul(bank(4 + f // 2)[:, (f % 2) * S:(f % 2 + 1) * S], vmem[:, m, f * P:(f + 1) * P],
                                       pxT[:, m, f // 2, :], start=(m == 0), stop=(m == 1))
                    if f % 2 == 1:
                        ins.then_inc(xo_done, 1)
                pe.wait_ge(xo_read, 4 * (L + 1))
                unit(L, 14, hT, False)
                unit(L, 15, hT, False)

            def moe(L):
                n = N_FFN0 if L == 0 else N_FFN1
                norm_T(n)
                wait_hT(n)
                pe.wait_ge(router_in, 64 * (L + 1))
                for b in range(TB):
                    for k in range(KD):
                        ins = t.matmul(bank(4)[:, b * (NG + NE):(b + 1) * (NG + NE)], hT[:, k, b * P:(b + 1) * P],
                                       wr[:, k, :], start=(k == 0), stop=(k == KD - 1))
                ins.then_inc(rl_done, 1)
                pe.wait_ge(member_ready, L + 1)
                mem_ = r16[1]
                t.matmul(bank(5)[:, 0:NE], upper, mem_[:, 0, :], start=True, stop=True)
                t.matmul(bank(5)[:, NE:2 * NE], upper, mem_[:, 1, :], start=True, stop=False)
                t.matmul(bank(5)[:, NE:2 * NE], ones, mem_[:, 0, :], start=False, stop=True)
                t.matmul(bank(5)[:, 2 * NE:3 * NE], ones, mem_[:, 0, :], start=True, stop=False)
                t.matmul(bank(5)[:, 2 * NE:3 * NE], ones, mem_[:, 1, :], start=False, stop=True).then_inc(rank_done, 1)

                def gather(half):
                    for k in range(4 * half, 4 * half + 4):
                        for b in range(TB):
                            ins = t.matmul(bank(6)[:, (k % 4) * P:(k % 4 + 1) * P],
                                           xs[:, b, :].rearrange("p (r k) -> p k r", k=KD)[:, k, :], psel[:, b, :],
                                           start=(b == 0), stop=(b == TB - 1))
                    ins.then_inc(g_done, 1)

                def first(j, tokens, done, start_sem=None):
                    for r in range(2):
                        pe.wait_ge(landed[slot(L, PROJ + EU * j + r)], where(j, r))
                        w = ring[:, slot(L, PROJ + EU * j + r), :].rearrange("p (k c n) -> p k c n", k=KD, c=2)
                        for k in range(KD):
                            for c in range(2):
                                ins = t.matmul(bank(4)[64 * c:64 * c + 64, r * S:(r + 1) * S], tokens[:, k, :],
                                               w[:, k, c, :], start=(k == 0), stop=(k == KD - 1))
                                if start_sem is not None:
                                    ins.then_inc(start_sem, 1)
                                    start_sem = None
                    ins.then_inc(done, 1)

                def turn(sel, hidden, done):
                    for b in range(TB):
                        t.transpose(bank(7)[:, b * P:(b + 1) * P], sel[:, b, :], ident)
                    for m in range(2):
                        ins = t.transpose(bank(7)[:, S + m * P:S + (m + 1) * P],
                                          hidden.rearrange("p (r m) -> p m r", m=2)[:, m, :], ident)
                    ins.then_inc(done, 1)

                def second(j, turned, dst, done):
                    pe.wait_ge(landed[slot(L, PROJ + EU * j + 2)], where(j, 2))
                    w = ring[:, slot(L, PROJ + EU * j + 2), :].rearrange("p (c m n) -> p c m n", c=2, m=2)
                    for c in range(2):
                        for m in range(2):
                            at = S + m * P + c * CAP
                            for o in range(2):
                                ins = t.matmul(dst[64 * o:64 * o + 64, :], turned[:, at:at + CAP],
                                               w[:, c, m, o * 512:(o + 1) * 512], start=(c + m == 0), stop=(c + m == 2))
                    ins.then_inc(done, 1)

                def scatter(turned, y):
                    for b in range(TB):
                        for o in range(2):
                            half = slice(64 * o, 64 * o + 64)
                            ins = t.matmul(bank(2 * b + o), turned[half, b * P:(b + 1) * P], y[half, :],
                                           start=False, stop=False, skip_group_check=True)
                    return ins

                def where(j, r):
                    return it * 16 + arrival(L, PROJ + EU * j + r)

                wait_read(pe, L, 15)
                pe.wait_ge(table_ready, L + 1)
                pe.wait_ge(psel_ready, (NE // 2 + 1) * L + 1)
                zb = zeros.bitcast(mybir.dt.bfloat16)
                for b in range(4):
                    ins = t.matmul(bank(b), zb[:, 0:P], zb[:, 0:512], start=True, stop=False, skip_group_check=True)
                if L == 0:
                    ins.then_inc(xdone, 1)
                gather(0)
                pe.wait_ge(hsel_ready, (NE + 2) * L + 1)
                gather(1)
                with pe.Fori(0, NE // 2) as it:
                    for j in range(2):
                        pe.wait_ge(hsel_ready, it * 2 + ((NE + 2) * L + 2))
                        first(j, hsel[:, :, j * CAP:(j + 1) * CAP], h_done, expert_done)
                        pe.wait_ge(ysb_ready, it * 2 + (L * (NE + 1) + j + 1))
                        scatter(tsb[1 - j], ysb[1 - j])
                        if j == 0:
                            pe.wait_ge(psel_ready, it + ((NE // 2 + 1) * L + 2))
                            gather(0)
                        else:
                            pe.wait_ge(hsel_ready, it * 2 + ((NE + 2) * L + 3))
                            gather(1)
                        pe.wait_ge(hid_ready, it * 2 + (L * NE + j + 1))
                        turn(pgate[j], hid, t_done)
                        pe.wait_ge(tsb_ready, it * 2 + (L * NE + j + 1))
                        second(j, tsb[j], bank(5), y_done)
                        x0, x1 = rounds(t, it * 2 + j)
                        with pe.If(x1 > x0):
                            with pe.Fori(x0, x1) as X:
                                pe.wait_ge(xp, X + 1)
                                for k in range(KD):
                                    for b in range(TB):
                                        ins = t.matmul(bank(4)[:, k * CAP:(k + 1) * CAP],
                                                       xs[:, b, :].rearrange("p (r k) -> p k r", k=KD)[:, k, :],
                                                       pselx[:, b, :], start=(b == 0), stop=(b == TB - 1))
                                ins.then_inc(xg, 1)
                                pe.wait_ge(xh, X + 1)
                                first(j, hselx, xH)
                                pe.wait_ge(xhid, X + 1)
                                turn(pgatex, hidx, xT)
                                pe.wait_ge(xt, X + 1)
                                second(j, tsbx, bank(4), xY)
                                pe.wait_ge(xy, X + 1)
                                scatter(tsbx, ysbx).then_inc(xdone, 1)
                pe.wait_ge(ysb_ready, (NE + 1) * (L + 1))
                scatter(tsb[1], ysb[1]).then_inc(acc_done, 1)
                pe.wait_ge(hsel_ready, (NE + 2) * (L + 1))
                t.matmul(bank(6)[:, 0:2], zb[:, 0:P], zb[:, 0:2], start=True, stop=True).then_inc(expert_done, 1)

            norm_T(N_MIX0)
            norm_T(N_MEM)
            mixer0()
            cross_attention(0)
            moe(0)
            norm_T(N_MIX1)
            mixer1()
            cross_attention(1)
            moe(1)


INPUTS = ["x", "mem", "rel_bias", "mem_norm_g", "final_norm_g", "hgrn_lb", "norm_mix_g", "norm_xattn_g",
          "norm_ffn_g", "even_w_in", "even_w_out", "hgrn_norm_g", "conv_dw", "conv_db", "conv_ln_g", "conv_ln_b",
          "odd_w_qkv", "odd_w_out", "lam_q1", "lam_k1", "lam_q2", "lam_k2", "subln_g", "xa_wq", "xa_wkv", "xa_wo",
          "moe_w_grp", "moe_b_grp", "moe_w_exp", "moe_b_exp", "moe_w1", "moe_w3", "moe_w2"]


def kernel(**inputs):
    import concourse.bacc as bacc
    from concourse.bass_utils import run_bass_kernel_spmd

    arrays = {f"in_{n}": np.ascontiguousarray(inputs[n]) for n in INPUTS}
    arrays["in_consts"] = shape_constants()
    arrays["in_onehot"] = t5_onehot()
    nc = bacc.Bacc("TRN2", target_bir_lowering=False, num_devices=1)
    aps = {n[3:]: nc.dram_tensor(n, v.shape, mybir.dt.from_np(v.dtype), kind="ExternalInput").ap()
           for n, v in arrays.items()}
    y = nc.dram_tensor("out", (1, S, D), F32, kind="ExternalOutput").ap()
    build(nc, aps, y)
    r = run_bass_kernel_spmd(nc, [arrays], core_ids=[0])
    return r.results[0]["out"]
```

```python
import math
from contextlib import ExitStack

import numpy as np
import concourse.bass as bass
from concourse import mybir

F32 = mybir.dt.float32
I32 = mybir.dt.int32
R32 = mybir.dt.float32r
ALU = mybir.AluOpType
ACT = mybir.ActivationFunctionType
AX = mybir.AxisListType

P = 128
D, S, M = 1024, 256, 256
KD = D // P
TB = S // P
DEPTH = 2
EPS = 1e-6
UNIT = 4096
SLOTS = 6
PROJ = 16
PIECES = 4
NE, NG, EPG = 16, 4, 4
EU = 3
CAP = 64
FF = 512
CONVW = 31
PAD = CONVW - 1
HH = 4
DH = 8
LAM_INIT = 0.8 - 0.6 * math.exp(-0.3)
BIG = 1e30
BW = 384
RELS = 32
LEVELS = 7
LN_SPLIT = 2.0 ** 60

N_MIX0, N_MEM, N_XA0, N_FFN0, N_MIX1, N_XA1, N_FFN1, N_FINAL = range(8)

DVE_UNITS = (10, 11, 14, 15)
R_DB, R_LNG, R_LNB, R_HG, R_SUB, R_LB = 0, 4, 8, 12, 13, 14
ROWS = 18


NR = NG + NE
O_GAINS = 5 * P + NE
O_VECS = O_GAINS + 7 * KD
O_RBIAS = O_VECS + ROWS
O_WR = O_RBIAS + DEPTH * NR
SMALL = O_WR + DEPTH * KD * NR
MIXC = (LEVELS + 1) * P + HH * CONVW
EARLY = 256 + DH + BW


def t5_onehot():
    rel = 2 * P - 1 - np.arange(BW)
    n = np.maximum(rel, 0)
    half = RELS // 2
    nf = np.maximum(n, 1).astype(np.float32)
    large = half + (np.log(nf / half) / np.float32(math.log(128 / half)) * half).astype(np.int32)
    bucket = np.where(n < half, n, np.clip(large, 0, RELS - 1))
    out = np.zeros((RELS + 1, BW), np.float32)
    ok = rel >= 0
    out[bucket[ok], np.arange(BW)[ok]] = 1.0
    out[RELS, ~ok] = 1.0
    return out


def shape_constants():
    i = np.arange(P)
    ident = np.eye(P)
    upper = (i[:, None] < i[None, :]) * 1.0
    ones = np.ones((P, P))
    iota = np.tile(i % CAP, (P, 1))
    s, t = i[:, None], i[None, :]
    masks = [(s == t) * 1.0]
    for lev in range(1, LEVELS + 1):
        m = 2 ** (lev - 1)
        masks.append(((s // (2 * m) == t // (2 * m)) & (s % (2 * m) < m) & (t % (2 * m) >= m)) * 1.0)
    ties = np.tile(np.arange(NE, 0, -1), (P, 1))
    return (np.concatenate([ident, upper, ones, iota, ident[::-1], ties], 1).astype(np.float32),
            np.concatenate(masks, 1).astype(np.float32))


class Own:

    def __init__(self, eng):
        self.eng, self.base, self.n, self.last = eng, {}, {}, None

    def value(self, sem):
        return self.base.get(sem.name, 0) + self.n.get(sem.name, 0)

    def inc(self, ins, sem):
        self.n[sem.name] = self.n.get(sem.name, 0) + 1
        ins.then_inc(sem, 1)
        self.last = (sem, self.value(sem))

    def wait(self, back=0):
        self.eng.wait_ge(self.last[0], self.last[1] - back)

    def enter(self, i, per):
        self.outer = {s.name: self.value(s) for s in per}
        for s, k in per.items():
            self.base[s.name], self.n[s.name] = i * k + self.outer[s.name], 0

    def leave(self, times, per):
        for s, k in per.items():
            assert self.n[s.name] == k, (s.name, self.n[s.name], k)
            self.base[s.name], self.n[s.name] = self.outer[s.name] + times * k, 0


def build(nc, a, out):
    ctx = ExitStack()
    with ctx:
        offsets = {}

        def sb(name, shape, dt=F32):
            offsets[name] = (nc.sbuf_base + 31) // 32 * 32
            return ctx.enter_context(nc.sbuf_tensor(name, shape, dt))

        def in_place_of(name, at, shape):
            return nc.alloc_sbuf_tensor_at(f"{name}_{at}_r", [P, *shape], R32, offset=offsets[name] + 4 * at)

        def sem(name):
            return ctx.enter_context(nc.semaphore(name))

        ring = sb("ring", [P, SLOTS, UNIT])
        x = sb("x", [P, TB, D])
        xs = sb("xs", [P, TB, D])
        hT = sb("hT", [P, KD, S])
        memT = sb("memT", [P, KD, M])
        kmem = sb("kmem", [P, KD, M])
        vmem = sb("vmem", [P, TB, D])
        AR = 13432
        arena = sb("arena", [P, AR])
        small = sb("small", [P, SMALL])
        mixc = sb("mixc", [P, MIXC])
        st = sb("st", [P, 160])
        xtab = sb("xtab", [P, NE + 1], I32)
        ps = ctx.enter_context(nc.psum_tensor("ps", [P, 8, 512], F32))
        bias_dram = nc.dram_tensor("bias_dram", [DH, BW], F32)

        ident, upper, ones, iota, anti = (small[:, i * P:(i + 1) * P] for i in range(5))
        ties = small[:, 5 * P:5 * P + NE]
        gains = small[:, O_GAINS:O_VECS].rearrange("p (n k) -> p n k", k=KD)
        vecs = small[:, O_VECS:O_RBIAS]
        rbias = [small[:, O_RBIAS + i * NR:O_RBIAS + (i + 1) * NR] for i in range(DEPTH)]
        wr = [small[:, O_WR + i * KD * NR:O_WR + (i + 1) * KD * NR].rearrange("p (k n) -> p k n", k=KD)
              for i in range(DEPTH)]
        masks = mixc[:, 0:(LEVELS + 1) * P].rearrange("p (l t) -> p l t", t=P)
        dwT = mixc[:, (LEVELS + 1) * P:].rearrange("p (c j) -> p c j", j=CONVW)

        ss, ms, rt, rs = st[:, 0:2], st[:, 2:4], st[:, 4:6], st[:, 6:8]
        lam2, lamexp, lamd, lamv = st[:, 8:10], st[:, 10:12], st[:, 12:13], st[:, 150:154]
        lbz, lbe, lbr, lbp, lb, oml = (st[:, 16 + 4 * i:20 + 4 * i] for i in range(6))
        oss, oms, ort, ors = (st[:, 40 + 16 * i:56 + 16 * i] for i in range(4))
        bn, mv, crt, crs = st[:, 104:116], st[:, 116:120], st[:, 120:122], st[:, 122:124]
        sub = st[:, 124:125]
        xmx, xsum, xrc = st[:, 126:134], st[:, 134:142], st[:, 142:150]
        xcarry = st[:, 158:159]
        dmx, dsum, drc = (st[:, 126 + 8 * i:134 + 8 * i] for i in range(3))
        cve = st[:, 138:140]

        def carve(at, shape):
            n = int(np.prod(shape))
            assert at + n <= AR, (at, n)
            v = arena[:, at:at + n]
            if len(shape) == 2:
                return v.rearrange("p (a b) -> p a b", b=shape[1])
            if len(shape) == 3:
                return v.rearrange("p (a b c) -> p a b c", b=shape[1], c=shape[2])
            return v

        hThi = in_place_of("hT", 0, [KD, S])
        hTlo = {True: in_place_of("arena", 9336, [KD, S]), False: in_place_of("xs", 0, [KD, S])}
        pieces = {True: (in_place_of("kmem", 0, [PIECES, 512]), in_place_of("vmem", 0, [PIECES, 512])),
                  False: (in_place_of("arena", 1024, [PIECES, 512]), in_place_of("arena", 3072, [PIECES, 512]))}

        fgate = carve(0, [1024])
        logf = carve(1024, [1024])
        bcum = carve(2048, [1024])
        qh = carve(3072, [1024])
        kh = carve(4096, [1024])
        vh = carve(5120, [TB, 512])
        gh = carve(6144, [TB, 512])
        upad = carve(7168, [HH, PAD + S])
        cacc = carve(8312, [HH, S])
        Ebuf = [carve(1024, [1024]), carve(0, [1024])]
        Qt = [carve(9336, [1024]), carve(10360, [1024])]
        Kt = [carve(11384, [1024]), carve(12408, [1024])]
        scanmask = xs[:, 0, :]
        lntmp = xs[:, 1, :]
        scoresT = xs[:, 0, :].rearrange("p (a b) -> p a b", b=P)
        crossT = carve(0, [HH, P])
        oh = carve(9336, [TB, 512])
        ohsq = carve(11384, [TB, 512])
        cnorm = carve(10360, [TB, 512])
        csilu = carve(11384, [HH, S])
        early = carve(12408, [EARLY])
        lamrow = early[:, 0:256].rearrange("p (i n) -> p i n", i=4)
        table = early[0:RELS + 1, 256:256 + DH]
        onehot = early[0:RELS + 1, 256 + DH:]
        t5stage = carve(11384, [BW])[0:DH, :]

        qd = carve(0, [DH, S])
        kd = carve(2048, [DH, S])
        vd = carve(4096, [TB, D])
        biasd = carve(6144, [DH, 2 * P])
        biasrev = carve(4096, [DH, 2 * P])
        sD = [carve(8192, [2, 2, S]), carve(9216, [2, 2, S])]
        aTD = carve(10240, [2, TB, P])
        odsq = carve(10752, [TB, D])
        od = xs

        qx = carve(5120, [KD, S])
        px = carve(7168, [4, 2, M])
        pxT = carve(9216, [TB, 4, S])

        hsel = carve(0, [KD, P])
        psel = carve(1024, [TB, P])
        pgate = [carve(1280, [TB, P]), carve(1536, [TB, P])]
        pturn = [carve(1792, [S]), carve(2048, [S])]
        hturn = carve(2304, [S])
        sil = carve(2816, [S])
        hid = carve(3072, [S])
        ysb = [carve(3328, [512]), carve(3840, [512])]
        hselx = carve(4352, [KD, CAP])
        pselx = carve(4864, [TB, CAP])
        pgatex = carve(4992, [TB, P])
        tsbx = carve(5248, [512])
        silx = carve(5760, [S])
        hidx = carve(6016, [S])
        ysbx = carve(6272, [512])
        lg = carve(6964, [TB, NG + NE])
        r4 = [carve(7004 + 8 * i, [TB, NG]) for i in range(4)]
        r16 = [carve(7036 + 32 * i, [TB, NE]) for i in range(8)]
        r1 = [carve(7292 + 2 * i, [TB, 1]) for i in range(10)]
        gate = carve(7312, [TB, NE])
        rank = carve(7344, [TB, NE + 2])
        nx = carve(7382, [NE])
        cumx = carve(7414, [NE + 1])
        zeros = carve(7432, [512])
        fgain = carve(8192, [D])

        def bank(b):
            return ps[:, b, :]

        def pair(pj):
            b = 2 * (pj % 2)
            return ps[:, b:b + 2, :]

        landed = [sem(f"landed{i}") for i in range(SLOTS)]
        names = """x_in mem_in small_in mixc_in early_in t5_stored t5_in
            fgain_in out_done piece_hi piece_lo piece_used hi_ready lo_ready qk_zero proj_done proj_read_act proj_read_dve act_step dve_step upad_zero
            t5_row t5_read t5_turned t5_ready lb_zero lb_exp lam_dot lam_exp
            sq_act ms_ready rt_ready rs_ready xs_act xs_dve tr_done cs_ready hT_act hT_dve x_new
            f_ready ln_ready k_ready conv_done arg_ready exp_ready lev_ready
            lev_done lev_read cross_done cross_read o_done o_read o_sq oms_ready ort_ready on_ready
            ot_done ct_done cv_ready cr_ready cn_ready cb_done
            xsc_done xmax_ready xexp_ready xp_ready xpt_done xpt_read xo_done
            dsc_done dsc_read dmax_ready dexp_ready da_ready dat_done dat_read do_done do_read
            rl_done rexp_in rexp_ready member_ready rank_done table_ready
            psel_ready g_done hsel_ready h_done sil_ready hid_ready t_done hturn_ready pturn_ready scatter_done y_done ysb_ready
            expert_done y_out
            xp xg xh xH xsil xhid xT xt xY xy xdone xstep""".split()
        q = {n: sem(n) for n in names}
        (x_in, mem_in, small_in, mixc_in, early_in, t5_stored, t5_in,
         fgain_in, out_done, piece_hi, piece_lo, piece_used, hi_ready, lo_ready, qk_zero, proj_done, proj_read_act, proj_read_dve, act_step, dve_step, upad_zero,
         t5_row, t5_read, t5_turned, t5_ready, lb_zero, lb_exp, lam_dot, lam_exp,
         sq_act, ms_ready, rt_ready, rs_ready, xs_act, xs_dve, tr_done, cs_ready, hT_act, hT_dve, x_new,
         f_ready, ln_ready, k_ready, conv_done, arg_ready, exp_ready, lev_ready,
         lev_done, lev_read, cross_done, cross_read, o_done, o_read, o_sq, oms_ready, ort_ready, on_ready,
         ot_done, ct_done, cv_ready, cr_ready, cn_ready, cb_done,
         xsc_done, xmax_ready, xexp_ready, xp_ready, xpt_done, xpt_read, xo_done,
         dsc_done, dsc_read, dmax_ready, dexp_ready, da_ready, dat_done, dat_read, do_done, do_read,
         rl_done, rexp_in, rexp_ready, member_ready, rank_done, table_ready,
         psel_ready, g_done, hsel_ready, h_done, sil_ready, hid_ready, t_done, hturn_ready, pturn_ready, scatter_done, y_done, ysb_ready,
         expert_done, y_out,
         xp, xg, xh, xH, xsil, xhid, xT, xt, xY, xy, xdone, xstep) = (q[n] for n in names)
        XSTEPS = 4

        def col_unit(w, c, by_row):
            v = w.rearrange("(p k) n -> p k n", k=KD) if by_row else w.rearrange("(k p) n -> p k n", p=P)
            return v[:, :, c * 512:(c + 1) * 512]

        def proj_source(L, u):
            if u < 6:
                if L == 0:
                    return col_unit(a["even_w_in"][0], (5, 4, 1, 0, 2, 3)[u], True)
                return col_unit(a["odd_w_qkv"][0], u, True)
            if u < 10:
                return col_unit(a["xa_wkv"][L], u - 6, True)
            if u < 12:
                return col_unit((a["even_w_out"] if L == 0 else a["odd_w_out"])[0], u - 10, False)
            if u < 14:
                return col_unit(a["xa_wq"][L], u - 12, True)
            return col_unit(a["xa_wo"][L], u - 14, False)

        LAYER_UNITS = PROJ + EU * NE
        EX_DONE = NE + 1
        assert EU * 2 == SLOTS

        def slot(L, u):
            return (L * LAYER_UNITS + u) % SLOTS

        def arrival(L, u):
            return 16 * ((L * LAYER_UNITS + u) // SLOTS + 1)

        def read_count(L, u):
            mine = [v for v in range(u + 1) if (v in DVE_UNITS) == (u in DVE_UNITS)]
            per = len(DVE_UNITS) if u in DVE_UNITS else PROJ - len(DVE_UNITS)
            return (proj_read_dve if u in DVE_UNITS else proj_read_act), L * per + len(mine)

        def wait_read(eng, L, u):
            s_, v_ = read_count(L, u)
            eng.wait_ge(s_, v_)

        def wait_source(eng, n, blk):
            if n == N_MIX0:
                eng.wait_ge(x_in, 16)
            elif n == N_MEM:
                eng.wait_ge(mem_in, 16)
            elif n in (N_XA0, N_FFN0, N_XA1, N_FFN1):
                wait_read(eng, 0 if n in (N_XA0, N_FFN0) else 1, 11 if n in (N_XA0, N_XA1) else 15)
            else:
                eng.wait_ge(x_new, (2 if n == N_MIX1 else 4) - 1 + blk)

        def norm_buffers(n):
            if n == N_MEM:
                return kmem[:, :, :].rearrange("p a b -> p (a b)").rearrange("p (b d) -> p b d", b=TB), vmem, memT
            return x, xs, hT

        def rounds(e_, e):
            return (e_.value_load(xtab[0:1, bass.ds(e, 1)], min_val=0, max_val=64),
                    e_.value_load(xtab[0:1, bass.ds(e + 1, 1)], min_val=0, max_val=64))

        SPLIT = [u for u in range(PROJ) if not 6 <= u < 10]
        T_MIX, T_OUT, T_XA, T_XO = range(4)

        def split_at(L, u):
            return L * len(SPLIT) + SPLIT.index(u)

        def piece(L, u, k):
            hi, lo = pieces[u < 6]
            return split_at(L, u) * KD + k, hi[:, k % PIECES, :], lo[:, k % PIECES, :]

        def wait_piece_used(eng, L, u, k):
            n, k = split_at(L, u), k - PIECES
            if k < 0:
                n, k = n - 1, k + KD
            if n < 0:
                return
            if k == KD - 1:
                L_, i_ = divmod(n, len(SPLIT))
                eng.wait_ge(proj_done, L_ * PROJ + SPLIT[i_] + 1)
            else:
                eng.wait_ge(piece_used, n * (KD - 1) + k + 1)

        def turn_lo(L, t_):
            return hTlo[L == 0 and t_ == T_MIX]

        def norm_turn(n):
            return {N_MIX0: (0, T_MIX), N_XA0: (0, T_XA), N_MIX1: (1, T_MIX), N_XA1: (1, T_XA)}.get(n)

        def plain_turns(n):
            return sum(norm_turn(m) is None for m in range(n + 1))

        TAPS_BEFORE, TAPS_PER_LEVEL = 8, 3

        block = ctx.enter_context(nc.Block())

        @block.sync
        def _(sp):
            sp.dma_start(x[:, :, :], a["x"][0].rearrange("(b p) d -> p b d", p=P)).then_inc(x_in, 16)
            sp.wait_ge(small_in, 16)
            for L in range(DEPTH):
                for u in range(PROJ):
                    if u >= SLOTS:
                        sp.wait_ge(proj_done, L * PROJ + u - SLOTS + 1)
                    elif L > 0:
                        e = NE - 2 + u // EU
                        sp.wait_ge(expert_done, (L - 1) * EX_DONE + e + 2)
                    s_ = slot(L, u)
                    sp.dma_start(ring[:, s_, :].rearrange("p (k n) -> p k n", k=KD),
                                 proj_source(L, u)).then_inc(landed[s_], 16)

                def load_expert(e, j, r):
                    s_ = slot(L, PROJ + EU * j + r)
                    if r < 2:
                        w = a["moe_w1" if r == 0 else "moe_w3"][L]
                        sp.dma_start(ring[:, s_, :],
                                     w[bass.ds(e, 1), :, :].rearrange("e (p k) f -> p (e k f)", k=KD)
                                     ).then_inc(landed[s_], 16)
                    else:
                        w = a["moe_w2"][L]
                        sp.dma_start(ring[:, s_, :].rearrange("p (c n) -> p c n", c=2),
                                     w[bass.ds(e, 1), :, :].rearrange("e (c r m) d -> r (e c) (m d)", c=2, m=2)
                                     ).then_inc(landed[s_], 16)

                for j in range(2):
                    for r in range(EU):
                        sp.wait_ge(proj_done, L * PROJ + PROJ - SLOTS + EU * j + r + 1)
                        load_expert(j, j, r)
                with sp.Fori(1, NE // 2) as it:
                    for j in range(2):
                        sp.wait_ge(expert_done, it * 2 + (L * EX_DONE + j))
                        for r in range(EU):
                            load_expert(it * 2 + j, j, r)
            for b in range(TB):
                sp.wait_ge(y_out, b + 1)
                sp.dma_start(out[0].rearrange("(b p) d -> p b d", p=P)[:, b, :], xs[:, b, :]).then_inc(out_done, 16)
            sp.wait_ge(out_done, 32)

        @block.gpsimd
        def _(pool):
            g_ = nc.gpsimd
            g_.memset(upad[:, :, 0:PAD], 0.0).then_inc(upad_zero, 1)
            for L in range(DEPTH):
                for u in SPLIT:
                    for k in range(KD):
                        n, hi, lo = piece(L, u, k)
                        pool.wait_ge(piece_hi, n + 1)
                        g_.tensor_tensor(lo, ring[:, slot(L, u), k * 512:(k + 1) * 512], hi.bitcast(F32),
                                         ALU.subtract).then_inc(piece_lo, 1)
                    if (L, u) == (0, 5):
                        pool.wait_ge(t5_stored, 16)
                        pool.wait_ge(proj_done, 6)
                        for b_ in (*Qt, *Kt):
                            g_.memset(b_, 0.0).then_inc(qk_zero, 1)

        @block.scalar
        def _(act):
            s = nc.scalar
            own = Own(act)
            act.dma_start(small[:, :], a["small"]).then_inc(small_in, 16)
            act.dma_start(early, a["early"]).then_inc(early_in, 16)
            act.wait_ge(small_in, 16)
            act.dma_start(norm_buffers(N_MEM)[0], a["mem"][0].rearrange("(b p) d -> p b d", p=P)).then_inc(mem_in, 16)
            act.dma_start(mixc[:, :], a["mixc"]).then_inc(mixc_in, 16)

            act.wait_ge(t5_row, 1)
            own.inc(s.activation(t5stage, bank(4)[0:DH, 0:BW], ACT.Copy), t5_read)
            own.wait()
            act.dma_start(bias_dram.ap(), t5stage).then_inc(t5_stored, 16)

            def constants():
                act.wait_ge(lb_zero, 1)
                own.inc(s.activation(lbe, lbz, ACT.Exp), lb_exp)
                act.wait_ge(lam_dot, 2)
                own.inc(s.activation(lamexp, lam2, ACT.Exp), lam_exp)

            def norm(n):
                src, dst, _ = norm_buffers(n)
                wait_source(act, n, 0)
                own.inc(s.activation(dst[:, 0, :], src[:, 0, :], ACT.Square, accum_out=ss[:, 0:1]), sq_act)
                act.wait_ge(ms_ready, n + 1)
                own.inc(s.activation(rt, ms, ACT.Sqrt), rt_ready)
                act.wait_ge(rs_ready, n + 1)
                ins = s.activation(dst[:, 0, :], src[:, 0, :], ACT.Copy, scale=rs[:, 0:1])
                own.inc(ins, xs_act)

            def split(L, u, half):
                for k in range(4 * half, 4 * half + 4):
                    n, hi, _ = piece(L, u, k)
                    if k == 0:
                        act.wait_ge(landed[slot(L, u)], arrival(L, u))
                    wait_piece_used(act, L, u, k)
                    own.inc(s.activation(hi, ring[:, slot(L, u), k * 512:(k + 1) * 512], ACT.Copy), piece_hi)

            def turn_hi(src, b, scale=1.0):
                own.inc(s.activation(hThi[:, 2 * b:2 * b + 2, :], src, ACT.Copy, scale=scale), hi_ready)

            def norm_T(n):
                if norm_turn(n) is not None:
                    for k in range(KD):
                        if k % 2 == 0:
                            act.wait_ge(tr_done, 4 * n + k // 2 + 1)
                        own.inc(s.activation(hThi[:, k, :], bank(4 + k // 2)[:, (k % 2) * S:(k % 2 + 1) * S],
                                             ACT.Copy, scale=gains[:, n, k:k + 1]), hi_ready if k % 2 else act_step)
                    return
                for k in range(4):
                    if k % 2 == 0:
                        act.wait_ge(tr_done, 4 * n + k // 2 + 1)
                    own.inc(s.activation(norm_buffers(n)[2][:, k, :], bank(4 + k // 2)[:, (k % 2) * S:(k % 2 + 1) * S],
                                         ACT.Copy, scale=gains[:, n, k:k + 1]), hT_act)

            def read_unit(L, u, dst, func=ACT.Copy):
                act.wait_ge(proj_done, L * PROJ + u + 1)
                own.inc(s.activation(dst, pair(L * PROJ + u), func), proj_read_act)

            def read_unit_T(L, u, dst, func=ACT.Copy):
                act.wait_ge(proj_done, L * PROJ + u + 1)
                own.inc(s.activation(dst, pair(L * PROJ + u).rearrange("p a (f t) -> p (a f) t", f=2), func),
                        proj_read_act)

            def flat(v):
                return v.rearrange("p (a b) -> p a b", a=2)

            def mixer0():
                def level_exp(lev):
                    act.wait_ge(arg_ready, lev)
                    own.inc(s.activation(Ebuf[lev % 2], Ebuf[lev % 2], ACT.Exp), exp_ready)

                act.wait_ge(tr_done, 4 * (N_MEM + 1))
                split(0, 0, 0)
                split(0, 0, 1)
                split(0, 1, 0)
                read_unit(0, 0, flat(cacc[:, :, :].rearrange("p a b -> p (a b)")), ACT.Sigmoid)
                split(0, 1, 1)
                split(0, 2, 0)
                read_unit_T(0, 1, upad[:, :, PAD:])
                constants()
                split(0, 2, 1)
                split(0, 3, 0)
                read_unit(0, 2, flat(fgate), ACT.Sigmoid)
                split(0, 3, 1)
                split(0, 4, 0)
                read_unit(0, 3, flat(qh), ACT.Silu)
                act.wait_ge(f_ready, 1)
                own.inc(s.activation(lntmp, lntmp, ACT.Ln), act_step)
                own.inc(s.activation(logf, logf, ACT.Ln), ln_ready)
                split(0, 4, 1)
                split(0, 5, 0)
                read_unit(0, 4, vh[:, :, :])
                split(0, 5, 1)
                level_exp(1)
                level_exp(2)
                read_unit(0, 5, gh[:, :, :], ACT.Sigmoid)
                level_exp(3)
                level_exp(4)
                read_unit_T(0, 6, kmem[:, 0:4, :])
                level_exp(5)
                read_unit_T(0, 7, kmem[:, 4:8, :])
                level_exp(6)
                read_unit(0, 8, vmem[:, :, 0:512])
                level_exp(7)
                read_unit(0, 9, vmem[:, :, 512:1024])
                level_exp(8)
                act.wait_ge(o_done, 1)
                own.inc(s.activation(oh[:, :, :], ps[:, 4:6, :], ACT.Copy), o_read)
                own.wait()
                own.inc(s.activation(ohsq[:, :, :], oh[:, :, :], ACT.Square), o_sq)
                split(0, 10, 0)
                act.wait_ge(oms_ready, 1)
                own.inc(s.activation(ort[:, 0:8], oms[:, 0:8], ACT.Sqrt), ort_ready)
                act.wait_ge(ot_done, 1)
                for b in range(2):
                    turn_hi(bank(6 + b).rearrange("p (f t) -> p f t", f=2), b, vecs[:, R_HG:R_HG + 1])
                act.wait_ge(cv_ready, 1)
                own.inc(s.activation(crt, cve, ACT.Sqrt), cr_ready)
                for c in range(HH):
                    if c % 2 == 0:
                        act.wait_ge(cb_done, c // 2 + 1)
                    own.inc(s.activation(csilu[:, c, :], bank(4 + c // 2)[:, (c % 2) * S:(c % 2 + 1) * S], ACT.Silu,
                                         bias=vecs[:, R_LNB + c:R_LNB + c + 1],
                                         scale=vecs[:, R_LNG + c:R_LNG + c + 1]), cs_ready)
                for b in range(2):
                    act.wait_ge(cs_ready, 2 * b + 2)
                    turn_hi(csilu[:, 2 * b:2 * b + 2, :], 2 + b)
                out_units(0)

            def out_units(L):
                split(L, 10, 1)
                split(L, 11, 0)
                split(L, 11, 1)
                split(L, 12, 0)

            def read_memory(u):
                if u < 8:
                    read_unit_T(1, u, kmem[:, 4 * (u - 6):4 * (u - 5), :])
                else:
                    read_unit(1, u, vmem[:, :, 512 * (u - 8):512 * (u - 7)])

            def mixer1():
                act.wait_ge(t5_stored, 16)
                act.dma_start(biasrev, bass.AP(bias_dram, 0, [[1, P], [BW, DH], [1, 2 * P]])).then_inc(t5_in, 16)
                for u in range(4):
                    split(1, u, 1)
                    split(1, u + 1, 0)
                    act.wait_ge(proj_done, PROJ + u + 1)
                    dst = (qd if u < 2 else kd)[:, 4 * (u % 2):4 * (u % 2) + 4, :]
                    own.inc(s.activation(dst, pair(PROJ + u).rearrange("p a (f t) -> p (a f) t", f=2), ACT.Copy,
                                         scale=0.125 if u < 2 else 1.0), proj_read_act)
                act.wait_ge(t5_turned, 1)
                own.inc(s.activation(biasd, ps[:, 4:8, :].rearrange("p a (h k) -> p (a h) k", h=2), ACT.Copy), t5_ready)
                split(1, 4, 1)
                split(1, 5, 0)
                read_unit(1, 4, vd[:, :, 0:512])
                split(1, 5, 1)
                read_unit(1, 5, vd[:, :, 512:1024])

                def back(j):
                    hp, i = j // 2, j % 2
                    act.wait_ge(dat_done, j + 1)
                    own.inc(s.activation(aTD[:, :, 0:i + 1, :], bank(6)[:, 0:2 * P * (i + 1)].rearrange(
                        "p (h a b) -> p h a b", h=2, b=P), ACT.Copy), dat_read)
                    act.wait_ge(do_done, j + 1)
                    own.inc(s.activation(od[:, i, 2 * hp * P:2 * (hp + 1) * P], bank(7)[:, 0:2 * P], ACT.Copy), do_read)

                for j in range(DH):
                    i = j % 2
                    nk = P * (i + 1)
                    act.wait_ge(dmax_ready, j + 1)
                    for m in range(2):
                        for h in range(2):
                            c = 4 * i + 2 * m + h
                            own.inc(s.activation(sD[i][:, m, h, 0:nk], sD[i][:, m, h, 0:nk], ACT.Exp,
                                                 bias=dmx[:, c:c + 1], accum_out=dsum[:, c:c + 1]), dexp_ready)
                    if j % 2 == 0 and j >= 2:
                        read_memory(6 + j // 2 - 1)
                    if j >= 1:
                        back(j - 1)
                read_memory(9)
                back(DH - 1)
                split(1, 10, 0)
                act.wait_ge(do_read, DH)
                own.inc(s.activation(odsq, od[:, :, :], ACT.Square), o_sq)
                act.wait_ge(oms_ready, 2)
                own.inc(s.activation(ort, oms, ACT.Sqrt), ort_ready)
                for b in range(4):
                    act.wait_ge(ot_done, 2 + b)
                    turn_hi(bank(4 + b).rearrange("p (f t) -> p f t", f=2), b, sub)
                out_units(1)

            def cross_attention(L):
                split(L, 12, 1)
                split(L, 13, 0)
                read_unit_T(L, 12, qx[:, 0:4, :])
                split(L, 13, 1)
                read_unit_T(L, 13, qx[:, 4:8, :])
                for c in range(4):
                    act.wait_ge(xmax_ready, 4 * L + c + 1)
                    for j in range(2):
                        own.inc(s.activation(px[:, c, j, :], bank(4 + c)[:, j * M:(j + 1) * M], ACT.Exp,
                                             bias=xmx[:, 2 * c + j:2 * c + j + 1], scale=1.0 / 16,
                                             accum_out=xsum[:, 2 * c + j:2 * c + j + 1]), xexp_ready)
                for c in range(4):
                    i, hp = c // 2, c % 2
                    act.wait_ge(xpt_done, 4 * L + c + 1)
                    own.inc(s.activation(pxT[:, :, 2 * hp:2 * hp + 2, i * P:(i + 1) * P],
                                         bank(4 + c).rearrange("p (m h t) -> p m h t", m=2, h=2), ACT.Copy), xpt_read)
                split(L, 14, 0)
                for b in range(4):
                    act.wait_ge(xo_done, 4 * L + b + 1)
                    turn_hi(bank(4 + b).rearrange("p (f t) -> p f t", f=2), b)
                split(L, 14, 1)
                split(L, 15, 0)
                split(L, 15, 1)

            def moe(L):
                if L == DEPTH - 1:
                    act.dma_start(fgain, a["final_norm_g"].unsqueeze(0).broadcast_to([P, D])).then_inc(fgain_in, 16)
                norm_T(N_FFN0 if L == 0 else N_FFN1)
                act.wait_ge(rexp_in, 2 * L + 1)
                own.inc(s.activation(r4[1], r4[0], ACT.Exp), rexp_ready)
                act.wait_ge(rexp_in, 2 * L + 2)
                own.inc(s.activation(r1[8], r1[7], ACT.Exp), rexp_ready)
                act.wait_ge(table_ready, L + 1)
                per = {sil_ready: 2, act_step: 2, ysb_ready: 2}
                with act.Fori(0, NE // 2) as it:
                    own.enter(it, per)
                    for j in range(2):
                        act.wait_ge(h_done, it * 2 + (L * NE + j + 1))
                        own.inc(s.activation(sil, bank(4)[:, 0:S], ACT.Silu), sil_ready)
                        act.wait_ge(y_done, it * 2 + (L * NE + j + 1))
                        own.inc(s.activation(ysb[j][0:64, :], bank(5)[0:64, :], ACT.Copy), act_step)
                        own.inc(s.activation(ysb[1 - j][64:P, :], bank(5)[64:P, :], ACT.Copy), ysb_ready)
                        x0, x1 = rounds(s, it * 2 + j)
                        with act.If(x1 > x0):
                            with act.Fori(x0, x1) as X:
                                act.wait_ge(xH, X + 1)
                                s.activation(silx, bank(4)[:, 0:S], ACT.Silu).then_inc(xsil, 1)
                                act.wait_ge(xY, X + 1)
                                s.activation(ysbx, bank(4), ACT.Copy).then_inc(xy, 1)
                    own.leave(NE // 2, per)
                if L + 1 < DEPTH:
                    split(L + 1, 0, 0)

            norm(N_MIX0)
            norm_T(N_MIX0)
            norm(N_MEM)
            norm_T(N_MEM)
            mixer0()
            norm(N_XA0)
            norm_T(N_XA0)
            cross_attention(0)
            norm(N_FFN0)
            moe(0)
            norm(N_MIX1)
            norm_T(N_MIX1)
            mixer1()
            norm(N_XA1)
            norm_T(N_XA1)
            cross_attention(1)
            norm(N_FFN1)
            moe(1)
            norm(N_FINAL)

        @block.vector
        def _(dve):
            v = nc.vector
            own = Own(dve)

            def step(ins, sem_=None):
                own.inc(ins, dve_step if sem_ is None else sem_)
                own.wait()

            def constants():
                lbv = vecs[:, R_LB:R_LB + 4]
                dve.wait_ge(small_in, 16)
                step(v.tensor_tensor(lbz, lbv, lbv, ALU.subtract), lb_zero)
                dve.wait_ge(early_in, 16)
                for i in range(2):
                    own.inc(v.tensor_tensor_reduce(lamrow[:, 2 * i, :], lamrow[:, 2 * i, :], lamrow[:, 2 * i + 1, :],
                                                   1.0, 0.0, ALU.mult, ALU.add, lam2[:, i:i + 1]), lam_dot)
                dve.wait_ge(lb_exp, 1)
                step(v.reciprocal(lbr, lbe))
                step(v.tensor_tensor(lbp, lbe, lbr, ALU.mult))
                step(v.tensor_tensor(lb, lbp, lbp, ALU.subtract))
                step(v.tensor_scalar(oml, lb, -1.0, 1.0, ALU.mult, ALU.add))
                step(v.tensor_scalar(sub, vecs[:, R_SUB:R_SUB + 1], 1.0 - LAM_INIT, None, ALU.mult))
                dve.wait_ge(lam_exp, 1)
                step(v.tensor_tensor(lamd, lamexp[:, 1:2], lamexp[:, 0:1], ALU.subtract))
                step(v.memset(lamv[:, 0:2], 1.0))
                for i in range(2):
                    step(v.tensor_scalar(lamv[:, 2 + i:3 + i], lamd, LAM_INIT, None, ALU.subtract))

            def norm(n):
                src, dst, _ = norm_buffers(n)
                wait_source(dve, n, 1)
                step(v.tensor_tensor_reduce(dst[:, 1, :], src[:, 1, :], src[:, 1, :], 1.0, 0.0, ALU.mult, ALU.add,
                                            ss[:, 1:2]))
                dve.wait_ge(sq_act, n + 1)
                own.inc(v.tensor_scalar(ms, ss, 1.0 / D, EPS, ALU.mult, ALU.add), ms_ready)
                dve.wait_ge(rt_ready, n + 1)
                step(v.reciprocal(rs, rt), rs_ready)
                step(v.tensor_scalar(dst[:, 1, :], src[:, 1, :], rs[:, 1:2], None, ALU.mult), xs_dve)

            def turn_lo_part(L, t_, b, src, gain=None, waits=True):
                if waits:
                    dve.wait_ge(hi_ready, 4 * (4 * L + t_) + b + 1)
                for k in range(2):
                    lo, hi = turn_lo(L, t_)[:, 2 * b + k, :], hThi[:, 2 * b + k, :].bitcast(F32)
                    done = lo_ready if k else dve_step
                    if gain is None:
                        own.inc(v.tensor_tensor(lo, src[:, k * S:(k + 1) * S], hi, ALU.subtract), done)
                    else:
                        own.inc(v.scalar_tensor_tensor(out=lo, in0=src[:, k * S:(k + 1) * S], scalar=gain(k), in1=hi,
                                                       op0=ALU.mult, op1=ALU.subtract), done)

            def norm_T(n):
                if norm_turn(n) is not None:
                    dve.wait_ge(tr_done, 4 * n + 4)
                    for b in range(4):
                        turn_lo_part(*norm_turn(n), b, bank(4 + b), lambda k: gains[:, n, 2 * b + k:2 * b + k + 1])
                    return
                for k in range(4, 8):
                    if k % 2 == 0:
                        dve.wait_ge(tr_done, 4 * n + k // 2 + 1)
                    own.inc(v.tensor_scalar(norm_buffers(n)[2][:, k, :], bank(4 + k // 2)[:, (k % 2) * S:(k % 2 + 1) * S],
                                            gains[:, n, k:k + 1], None, ALU.mult), hT_dve)
                own.wait()

            def add_unit(L, u):
                h = (u % 2) * 512
                dve.wait_ge(proj_done, L * PROJ + u + 1)
                step(v.tensor_tensor(x[:, :, h:h + 512], x[:, :, h:h + 512], pair(L * PROJ + u), ALU.add), proj_read_dve)

            def head_norm(o, osq, nh, blocks):
                n = nh * TB
                dve.wait_ge(o_sq, blocks)
                step(v.tensor_reduce(oss[:, 0:n], osq.rearrange("p b (h c) -> p (b h) c", c=P), AX.X, ALU.add))
                own.inc(v.tensor_scalar(oms[:, 0:n], oss[:, 0:n], 1.0 / P, EPS, ALU.mult, ALU.add), oms_ready)
                dve.wait_ge(ort_ready, blocks)
                step(v.reciprocal(ors[:, 0:n], ort[:, 0:n]))

            def forget():
                wait_read(dve, 0, 2)
                for h in range(HH):
                    own.inc(v.tensor_scalar(fgate[:, h * S:(h + 1) * S], fgate[:, h * S:(h + 1) * S],
                                            oml[:, h:h + 1], lb[:, h:h + 1], ALU.mult, ALU.add), dve_step)
                own.wait()
                step(v.tensor_scalar(lntmp, fgate, 1e-30, LN_SPLIT, ALU.max, ALU.mult))
                own.inc(v.tensor_scalar(logf, fgate, 1.0 / LN_SPLIT, None, ALU.max), dve_step)
                step(v.tensor_scalar(lntmp, lntmp, 1.0, None, ALU.min), f_ready)
                own.inc(v.tensor_scalar(kh, fgate, -1.0, 1.0, ALU.mult, ALU.add), k_ready)
                step(v.memset(scanmask, 1.0))
                step(v.memset(scanmask.rearrange("p (a b) -> p a b", b=P)[:, :, 0:1], 0.0))
                dve.wait_ge(ln_ready, 1)
                step(v.tensor_tensor(logf, logf, lntmp, ALU.add))
                step(v.tensor_tensor_scan(bcum, scanmask, logf, 0.0, ALU.mult, ALU.add))

            def mixer0():

                def halves(b_, lev):
                    m = 2 ** (lev - 1)
                    w = b_.rearrange("p (n s m) -> p n s m", s=2, m=m)
                    return w[:, :, 0, :], w[:, :, 1, :], m

                def args(lev):
                    b0, b1, m = halves(bcum, lev)
                    e0, e1, _ = halves(Ebuf[lev % 2], lev)
                    ref = b0[:, :, m - 1:m].to_broadcast([P, 512 // m, m])
                    own.inc(v.tensor_tensor(e0, ref, b0, ALU.subtract), dve_step)
                    if m < P:
                        ins = v.tensor_tensor(e1, b1, ref, ALU.subtract)
                    else:
                        ins = v.tensor_copy(e1, b1)
                    step(ins, arg_ready)

                def mul(lev):
                    q0_, q1_, _ = halves(Qt[lev % 2], lev)
                    k0_, k1_, _ = halves(Kt[lev % 2], lev)
                    e0, e1, _ = halves(Ebuf[lev % 2], lev)
                    dve.wait_ge(exp_ready, lev)
                    if lev == 1:
                        wait_read(dve, 0, 3)
                        dve.wait_ge(qk_zero, 4)
                    own.inc(v.tensor_tensor(q1_, halves(qh, lev)[1], e1, ALU.mult), dve_step)
                    step(v.tensor_tensor(k0_, halves(kh, lev)[0], e0, ALU.mult), lev_ready)

                def take(lev):
                    b_ = 4 + 2 * (lev % 2)
                    src = ps[:, b_:b_ + 2, :].rearrange("p a (n t) -> p (a n) t", t=P)
                    mk = masks[:, lev:lev + 1, :].to_broadcast([P, 8, P])
                    dve.wait_ge(lev_done, lev + 1)
                    if lev == 0:
                        step(v.tensor_tensor(scoresT, src, mk, ALU.mult), lev_read)
                    else:
                        t_ = lntmp.rearrange("p (n t) -> p n t", t=P)
                        step(v.tensor_tensor(t_, src, mk, ALU.mult), lev_read)
                        step(v.tensor_tensor(scoresT, scoresT, t_, ALU.add))

                taps = iter(range(CONVW))

                def tap():
                    j = next(taps, None)
                    if j is None:
                        return
                    for c in range(HH):
                        w = dwT[:, c, j:j + 1]
                        if j == 0:
                            ins = v.tensor_scalar(cacc[:, c, :], upad[:, c, 0:S], w, vecs[:, R_DB + c:R_DB + c + 1],
                                                  ALU.mult, ALU.add)
                        else:
                            ins = v.scalar_tensor_tensor(out=cacc[:, c, :], in0=upad[:, c, j:j + S], scalar=w,
                                                         in1=cacc[:, c, :], op0=ALU.mult, op1=ALU.add)
                        own.inc(ins, conv_done if j == CONVW - 1 else dve_step)
                    own.wait()

                constants()
                wait_read(dve, 0, 1)
                step(v.tensor_tensor(upad[:, :, PAD:], upad[:, :, PAD:], cacc[:, :, :], ALU.mult))
                dve.wait_ge(upad_zero, 1)
                dve.wait_ge(mixc_in, 16)
                for _ in range(TAPS_BEFORE):
                    tap()
                forget()
                args(1)
                args(2)
                for _ in range(TAPS_BEFORE):
                    tap()
                mul(1)
                for lev in range(3, LEVELS + 2):
                    args(lev)
                    take(lev - 3)
                    mul(lev - 1)
                    for _ in range(TAPS_PER_LEVEL):
                        tap()
                take(LEVELS - 1)
                mul(LEVELS + 1)
                take(LEVELS)
                dve.wait_ge(cross_done, 1)
                step(v.tensor_copy(crossT[:, :, :], bank(4).rearrange("p (n t) -> p n t", t=P)), cross_read)
                for _ in range(CONVW):
                    tap()
                head_norm(ohsq, ohsq, HH, 1)
                o_ = oh[:, :, :].rearrange("p b (h c) -> p (b h) c", c=P)
                step(v.tensor_tensor(o_, o_, ors[:, 0:8].unsqueeze(2).to_broadcast([P, 8, P]), ALU.mult))
                step(v.tensor_tensor(oh[:, :, :], oh[:, :, :], gh[:, :, :], ALU.mult), on_ready)
                dve.wait_ge(ct_done, 1)
                for b_ in range(TB):
                    own.inc(v.bn_stats(bn[:, 6 * b_:6 * b_ + 6], bank(4 + b_)), dve_step)
                own.wait()
                for b_ in range(TB):
                    own.inc(v.bn_aggr(mv[:, 2 * b_:2 * b_ + 2], bn[:, 6 * b_:6 * b_ + 6]), dve_step)
                own.wait()
                own.inc(v.tensor_scalar(cve, mv.rearrange("p (b t) -> p b t", t=2)[:, :, 1], EPS, None, ALU.add), cv_ready)
                dve.wait_ge(cr_ready, 1)
                step(v.reciprocal(crs, crt))
                for b_ in range(TB):
                    own.inc(v.tensor_scalar(cnorm[:, b_, :], bank(4 + b_), mv[:, 2 * b_:2 * b_ + 1], crs[:, b_:b_ + 1],
                                            ALU.subtract, ALU.mult), cn_ready)
                for b_ in range(2):
                    turn_lo_part(0, T_OUT, b_, bank(6 + b_), lambda k: vecs[:, R_HG:R_HG + 1])
                for b_ in range(2):
                    turn_lo_part(0, T_OUT, 2 + b_, csilu[:, 2 * b_:2 * b_ + 2, :].rearrange("p a b -> p (a b)"))
                add_unit(0, 10)
                add_unit(0, 11)

            def mixer1():
                def front(j):
                    hp, i = j // 2, j % 2
                    nk = P * (i + 1)
                    dve.wait_ge(dsc_done, j + 1)
                    sc = ps[:, 4:6, :].rearrange("p m (h k) -> p m h k", h=2)
                    for m in range(2):
                        step(v.tensor_tensor(sD[i][:, m, :, 0:nk], sc[:, m, :, 0:nk],
                                             biasd[:, 2 * hp:2 * hp + 2, 2 * P - nk:2 * P], ALU.add), dsc_read)
                    own.inc(v.tensor_reduce(dmx[:, 4 * i:4 * i + 4].rearrange("p (m h) -> p m h", m=2),
                                            sD[i][:, :, :, 0:nk], AX.X, ALU.max, negate=True), dmax_ready)

                def back(j):
                    i = j % 2
                    nk = P * (i + 1)
                    dve.wait_ge(dexp_ready, 4 * j + 4)
                    rc = drc[:, 4 * i:4 * i + 4]
                    step(v.reciprocal(rc, dsum[:, 4 * i:4 * i + 4]))
                    step(v.tensor_tensor(rc, rc, lamv, ALU.mult))
                    own.inc(v.tensor_tensor(sD[i][:, 1, :, 0:nk], sD[i][:, 1, :, 0:nk],
                                            rc[:, 2:4].unsqueeze(2).to_broadcast([P, 2, nk]), ALU.mult), dve_step)
                    own.wait()
                    for h in range(2):
                        own.inc(v.scalar_tensor_tensor(out=sD[i][:, 0, h, 0:nk], in0=sD[i][:, 0, h, 0:nk],
                                                       scalar=rc[:, h:h + 1], in1=sD[i][:, 1, h, 0:nk],
                                                       op0=ALU.mult, op1=ALU.add), da_ready)

                dve.wait_ge(t5_ready, 1)
                front(0)
                for j in range(DH):
                    if j + 1 < DH:
                        if j >= 1:
                            dve.wait_ge(dat_done, j)
                        front(j + 1)
                    back(j)
                own.wait()
                head_norm(od, odsq, DH, 2)
                for b_ in range(TB):
                    o_ = od[:, b_, :].rearrange("p (h c) -> p h c", c=P)
                    own.inc(v.tensor_tensor(o_, o_, ors[:, 8 * b_:8 * b_ + 8].unsqueeze(2).to_broadcast([P, 8, P]),
                                            ALU.mult), on_ready)
                dve.wait_ge(ot_done, 5)
                for b_ in range(4):
                    turn_lo_part(1, T_OUT, b_, bank(4 + b_), lambda k: sub)
                add_unit(1, 10)
                add_unit(1, 11)

            def cross_attention(L):
                for c in range(4):
                    dve.wait_ge(xsc_done, 4 * L + c + 1)
                    step(v.tensor_reduce(xmx[:, 2 * c:2 * c + 2], bank(4 + c).rearrange("p (h m) -> p h m", h=2),
                                         AX.X, ALU.max, negate=True))
                    own.inc(v.tensor_scalar(xmx[:, 2 * c:2 * c + 2], xmx[:, 2 * c:2 * c + 2], 1.0 / 16, None, ALU.mult),
                            xmax_ready)
                for c in range(4):
                    dve.wait_ge(xexp_ready, 8 * L + 2 * c + 2)
                    step(v.reciprocal(xrc[:, 2 * c:2 * c + 2], xsum[:, 2 * c:2 * c + 2]))
                    own.inc(v.tensor_tensor(px[:, c, :, :], px[:, c, :, :],
                                            xrc[:, 2 * c:2 * c + 2].unsqueeze(2).to_broadcast([P, 2, M]), ALU.mult), xp_ready)
                for b_ in range(4):
                    turn_lo_part(L, T_XO, b_, bank(4 + b_))
                add_unit(L, 14)
                add_unit(L, 15)

            def moe(L):
                n = N_FFN0 if L == 0 else N_FFN1
                norm_T(n)
                own.inc(v.memset(zeros, 0.0), dve_step)
                for b_ in (*pturn, ysb[0]):
                    own.inc(v.memset(b_, 0.0), dve_step)
                own.inc(v.memset(ysb[1], 0.0), ysb_ready)
                own.inc(v.memset(rank[:, :, NE:], -1.0), dve_step)
                if L == 0:
                    own.inc(v.memset(xcarry, 0.0), xstep)
                tie2 = ties.unsqueeze(1).to_broadcast([P, TB, NE])
                tie4 = ties[:, NE - NG:].unsqueeze(1).to_broadcast([P, TB, NG])
                g4, e16 = lg[:, :, 0:NG], lg[:, :, NG:]
                wide4 = lambda c: c.to_broadcast([P, TB, NG])
                wide = lambda c: c.to_broadcast([P, TB, NE])
                dve.wait_ge(rl_done, L + 1)
                step(v.tensor_tensor(lg, bank(4)[:, 0:TB * (NG + NE)].rearrange("p (b n) -> p b n", b=TB),
                                     rbias[L].unsqueeze(1).to_broadcast([P, TB, NG + NE]), ALU.add))
                step(v.tensor_reduce(r1[0], g4, AX.X, ALU.max))
                step(v.tensor_tensor(r4[0], g4, wide4(r1[0]), ALU.subtract), rexp_in)
                step(v.tensor_scalar(r4[2], r4[0], 0.0, None, ALU.is_equal))
                step(v.tensor_tensor(r4[2], r4[2], tie4, ALU.mult))
                step(v.tensor_reduce(r1[1], r4[2], AX.X, ALU.max))
                step(v.tensor_tensor(r4[3], r4[2], wide4(r1[1]), ALU.is_equal))
                step(v.tensor_scalar(r4[2], r4[3], BIG, BIG, ALU.mult, ALU.subtract))
                step(v.tensor_tensor(r16[0].rearrange("p b (g e) -> p b g e", g=NG), e16.rearrange("p b (g e) -> p b g e", g=NG),
                                     r4[2].unsqueeze(3).to_broadcast([P, TB, NG, EPG]), ALU.add))
                step(v.tensor_reduce(r1[4], r16[0], AX.X, ALU.max))
                step(v.tensor_tensor(r16[1], r16[0], wide(r1[4]), ALU.is_equal))
                step(v.tensor_tensor(r16[2], r16[1], tie2, ALU.mult))
                step(v.tensor_reduce(r1[5], r16[2], AX.X, ALU.max))
                step(v.tensor_tensor(r16[3], r16[2], wide(r1[5]), ALU.is_equal))
                step(v.tensor_scalar(r16[4], r16[3], -2 * BIG, None, ALU.mult))
                step(v.tensor_tensor(r16[4], r16[4], r16[0], ALU.add))
                step(v.tensor_reduce(r1[6], r16[4], AX.X, ALU.max))
                step(v.tensor_tensor(r1[7], r1[6], r1[4], ALU.subtract), rexp_in)
                step(v.tensor_tensor(r16[1], r16[4], wide(r1[6]), ALU.is_equal))
                step(v.tensor_tensor(r16[2], r16[1], tie2, ALU.mult))
                step(v.tensor_reduce(r1[5], r16[2], AX.X, ALU.max))
                step(v.tensor_tensor(r16[5], r16[2], wide(r1[5]), ALU.is_equal))
                step(v.tensor_tensor(r16[1], r16[3], r16[5], ALU.add), member_ready)
                dve.wait_ge(rexp_ready, 2 * L + 2)
                step(v.tensor_reduce(r1[2], r4[1], AX.X, ALU.add))
                step(v.reciprocal(r1[3], r1[2]))
                step(v.tensor_scalar(r1[9], r1[8], 1.0, None, ALU.add))
                step(v.reciprocal(r1[5], r1[9]))
                step(v.tensor_tensor(r1[0], r1[3], r1[5], ALU.mult))
                step(v.tensor_tensor(r1[1], r1[0], r1[8], ALU.mult))
                step(v.tensor_tensor(r16[6], r16[3], wide(r1[0]), ALU.mult))
                step(v.tensor_tensor(r16[7], r16[5], wide(r1[1]), ALU.mult))
                step(v.tensor_tensor(gate, r16[6], r16[7], ALU.add))
                dve.wait_ge(rank_done, L + 1)
                rk = rank[:, :, 0:NE]
                step(v.tensor_scalar(rk, bank(5)[:, 0:TB * NE].rearrange("p (b e) -> p b e", b=TB), 1.0, None, ALU.add))
                step(v.tensor_tensor(rk, rk, r16[1], ALU.mult))
                step(v.tensor_scalar(rk, rk, 1.0, None, ALU.subtract))
                cnt = bank(5)[:, TB * NE:(TB + 1) * NE]
                step(v.tensor_scalar(nx, cnt, float(CAP), None, ALU.is_gt))
                for i in range(2, S // CAP):
                    step(v.tensor_scalar(cumx[:, 0:NE], cnt, float(CAP * i), None, ALU.is_gt))
                    step(v.tensor_tensor(nx, nx, cumx[:, 0:NE], ALU.add))
                step(v.tensor_copy(cumx[:, 0:1], xcarry))
                step(v.tensor_tensor_scan(cumx[:, 1:NE + 1], ones[:, 0:NE], nx, xcarry, ALU.mult, ALU.add))
                step(v.tensor_copy(xcarry, cumx[:, NE:NE + 1]))
                step(v.tensor_copy(xtab[:, :], cumx), table_ready)

                def at(t, b_, e):
                    return t[:, b_, bass.ds(e, 1)]

                def build_psel(e):
                    for b_ in range(TB):
                        for j in range(2):
                            last = b_ == TB - 1 and j == 1
                            own.inc(v.tensor_scalar(psel[:, b_, j * CAP:(j + 1) * CAP], iota[:, 0:CAP],
                                                    at(rank, b_, e + j), None, ALU.is_equal),
                                    psel_ready if last else dve_step)

                def build_pgate(e, o):
                    for b_ in range(TB):
                        for j in range(2):
                            at_ = (j ^ o) * CAP
                            own.inc(v.tensor_scalar(pgate[o][:, b_, at_:at_ + CAP], iota[:, 0:CAP], at(rank, b_, e + j),
                                                    at(gate, b_, e + j), ALU.is_equal, ALU.mult), dve_step)

                def take_gather(half, g):
                    dve.wait_ge(g_done, g)
                    own.inc(v.tensor_tensor(hsel[:, 4 * half:4 * half + 4, :], bank(6).rearrange("p (k t) -> p k t", t=P),
                                            gains[:, n, 4 * half:4 * half + 4].unsqueeze(2).to_broadcast([P, 4, P]),
                                            ALU.mult), hsel_ready)

                GB = (NE + 2) * L
                build_psel(0)
                take_gather(0, GB + 1)
                take_gather(1, GB + 2)
                own.wait()
                per = {dve_step: 3 + 8, psel_ready: 1, hid_ready: 2, hturn_ready: 2, pturn_ready: 2, hsel_ready: 2}
                with dve.Fori(0, NE // 2) as it:
                    own.enter(it, per)
                    for j in range(2):
                        e = it * 2
                        o = 1 - j
                        if j == 0:
                            build_pgate(e, 1)
                            build_pgate(e, 0)
                            build_psel(e + 2)
                        else:
                            dve.wait_ge(h_done, it * 2 + (L * NE + 2))
                            take_gather(0, it * 2 + (GB + 3))
                        dve.wait_ge(sil_ready, it * 2 + (L * NE + j + 1))
                        own.inc(v.tensor_tensor(hid, sil, bank(4)[:, S:2 * S], ALU.mult), hid_ready)
                        if j == 1:
                            take_gather(1, it * 2 + (GB + 4))
                        dve.wait_ge(t_done, it * 2 + (L * NE + j + 1))
                        own.inc(v.tensor_copy(hturn, bank(7)[:, S:2 * S]), hturn_ready)
                        if j == 0:
                            dve.wait_ge(scatter_done, it + ((NE // 2 + 1) * L + 1))
                        own.inc(v.tensor_copy(pturn[o], bank(7)[:, 0:S]), pturn_ready)
                        further(e + j, n)
                    own.leave(NE // 2, per)
                dve.wait_ge(scatter_done, (NE // 2 + 1) * (L + 1))
                for b_ in range(TB):
                    own.inc(v.tensor_tensor(x[:, b_, :].rearrange("p (c n) -> p c n", c=2),
                                            x[:, b_, :].rearrange("p (c n) -> p c n", c=2),
                                            ps[:, 2 * b_:2 * b_ + 2, :], ALU.add), x_new)
                own.wait()

            def further(e, n):
                x0, x1 = rounds(v, e)
                with dve.If(x1 > x0):
                    with dve.Fori(x0, x1) as X:
                        own.wait()
                        dve.wait_ge(xdone, X + 1)
                        dve.wait_ge(xstep, X * XSTEPS + 1)
                        r_ = rank[:, :, bass.ds(e, 1)]
                        v.tensor_scalar(r_, r_, float(CAP), None, ALU.subtract).then_inc(xstep, 1)
                        dve.wait_ge(xstep, X * XSTEPS + 2)
                        for b_ in range(TB):
                            v.tensor_scalar(pselx[:, b_, :], iota[:, 0:CAP], rank[:, b_, bass.ds(e, 1)], None,
                                            ALU.is_equal).then_inc(xstep, 1)
                        for b_ in range(TB):
                            v.tensor_scalar(pgatex[:, b_, :], iota, rank[:, b_, bass.ds(e, 1)],
                                            gate[:, b_, bass.ds(e, 1)], ALU.is_equal, ALU.mult
                                            ).then_inc(xstep if b_ == 0 else xp, 1)
                        dve.wait_ge(xg, X + 1)
                        v.tensor_tensor(hselx, bank(4).rearrange("p (k t) -> p k t", k=KD),
                                        gains[:, n, :].unsqueeze(2).to_broadcast([P, KD, CAP]), ALU.mult).then_inc(xh, 1)
                        dve.wait_ge(xsil, X + 1)
                        v.tensor_tensor(hidx, silx, bank(4)[:, S:2 * S], ALU.mult).then_inc(xhid, 1)
                        dve.wait_ge(xT, X + 1)
                        v.tensor_copy(tsbx, bank(7)).then_inc(xt, 1)

            norm(N_MIX0)
            norm_T(N_MIX0)
            norm(N_MEM)
            norm_T(N_MEM)
            mixer0()
            norm(N_XA0)
            norm_T(N_XA0)
            cross_attention(0)
            norm(N_FFN0)
            moe(0)
            norm(N_MIX1)
            norm_T(N_MIX1)
            mixer1()
            norm(N_XA1)
            norm_T(N_XA1)
            cross_attention(1)
            norm(N_FFN1)
            moe(1)
            norm(N_FINAL)
            dve.wait_ge(fgain_in, 16)
            dve.wait_ge(xs_act, N_FINAL + 1)
            for b_ in range(TB):
                own.inc(v.tensor_tensor(xs[:, b_, :], xs[:, b_, :], fgain, ALU.mult), y_out)

        @block.tensor
        def _(pe):
            t = nc.tensor

            pe.wait_ge(small_in, 16)
            pe.wait_ge(early_in, 16)
            t.matmul(bank(4)[0:DH, 0:BW], table, onehot, start=True, stop=True).then_inc(t5_row, 1)

            def norm_T(n):
                dst = norm_buffers(n)[1]
                if n == N_MIX0:
                    pe.wait_ge(t5_read, 1)
                if n == N_MEM:
                    pe.wait_ge(lo_ready, 4)
                pe.wait_ge(xs_act, n + 1)
                pe.wait_ge(xs_dve, n + 1)
                for k in range(KD):
                    for b in range(TB):
                        at = (k % 2) * S + b * P
                        ins = t.transpose(bank(4 + k // 2)[:, at:at + P],
                                          dst[:, b, :].rearrange("p (r k) -> p k r", k=KD)[:, k, :], ident)
                    if k % 2 == 1:
                        ins.then_inc(tr_done, 1)

            def wait_hT(n):
                pe.wait_ge(hT_act, 4 * plain_turns(n))
                pe.wait_ge(hT_dve, 4 * plain_turns(n))

            def split_unit(L, u, t_, transposed, first=False):
                pj = L * PROJ + u
                if pj >= 2:
                    wait_read(pe, *divmod(pj - 2, PROJ))
                dst = pair(pj)
                h_lo = turn_lo(L, t_)
                for k in range(KD):
                    n, w_hi, w_lo = piece(L, u, k)
                    if first and k % 2 == 0:
                        pe.wait_ge(lo_ready, 4 * (4 * L + t_) + k // 2 + 1)
                    pe.wait_ge(piece_lo, n + 1)
                    for i, (w, h) in enumerate(((w_hi, hThi), (w_hi, h_lo), (w_lo, hThi))):
                        for f in range(4 if transposed else 2):
                            if transposed:
                                o_, l_, r_ = dst[:, f // 2, (f % 2) * S:(f % 2 + 1) * S], w[:, f * P:(f + 1) * P], h[:, k, :]
                            else:
                                o_, l_, r_ = dst[:, f, :], h[:, k, f * P:(f + 1) * P], w
                            ins = t.matmul(o_, l_, r_, start=(k == 0 and i == 0 and not (transposed and f % 2)),
                                           stop=(k == KD - 1 and i == 2), skip_group_check=True)
                    ins.then_inc(piece_used if k < KD - 1 else proj_done, 1)

            def unit(L, u, src, transposed, part=None):
                pj = L * PROJ + u
                if pj >= 2:
                    wait_read(pe, *divmod(pj - 2, PROJ))
                pe.wait_ge(landed[slot(L, u)], arrival(L, u))
                w = ring[:, slot(L, u), :].rearrange("p (k n) -> p k n", k=KD)
                dst = pair(pj)
                if transposed:
                    for f in range(4) if part is None else (2 * part, 2 * part + 1):
                        for k in range(KD):
                            ins = t.matmul(dst[:, f // 2, (f % 2) * S:(f % 2 + 1) * S], w[:, k, f * P:(f + 1) * P],
                                           src[:, k, :], start=(k == 0), stop=(k == KD - 1))
                else:
                    for b in range(TB) if part is None else (part,):
                        for k in range(KD):
                            ins = t.matmul(dst[:, b, :], src[:, k, b * P:(b + 1) * P], w[:, k, :],
                                           start=(k == 0), stop=(k == KD - 1))
                if part != 0:
                    ins.then_inc(proj_done, 1)

            def mixer0():
                def level(lev):
                    if lev == 0:
                        kk, qq = kh, qh
                        pe.wait_ge(k_ready, 1)
                        wait_read(pe, 0, 3)
                    else:
                        kk, qq = Kt[lev % 2], Qt[lev % 2]
                        pe.wait_ge(lev_ready, lev)
                    if lev == LEVELS + 1:
                        pe.wait_ge(lev_read, LEVELS)
                        for h in range(HH):
                            ins = t.matmul(bank(4)[:, h * P:(h + 1) * P], kk[:, h * S:h * S + P],
                                           qq[:, h * S + P:(h + 1) * S], start=True, stop=True)
                        ins.then_inc(cross_done, 1)
                        return
                    if lev >= 2:
                        pe.wait_ge(lev_read, lev - 1)
                    for i in range(8):
                        at = i * P
                        ins = t.matmul(bank(4 + 2 * (lev % 2) + i // 4)[:, (i % 4) * P:(i % 4 + 1) * P],
                                       kk[:, at:at + P], qq[:, at:at + P], start=True, stop=True)
                    ins.then_inc(lev_done, 1)

                for u in range(4):
                    split_unit(0, u, T_MIX, True, u == 0)
                wait_hT(N_MEM)
                split_unit(0, 4, T_MIX, False)
                level(0)
                split_unit(0, 5, T_MIX, False)
                level(1)
                level(2)
                unit(0, 6, memT, True)
                level(3)
                unit(0, 7, memT, True)
                level(4)
                unit(0, 8, memT, False)
                level(5)
                unit(0, 9, memT, False)
                level(6)
                level(7)
                level(8)
                wait_read(pe, 0, 4)
                pe.wait_ge(lev_read, LEVELS + 1)
                pe.wait_ge(cross_read, 1)
                for h in range(HH):
                    hv = slice(h * P, (h + 1) * P)
                    t.matmul(bank(4)[:, hv], scoresT[:, 2 * h, :], vh[:, 0, hv], start=True, stop=True)
                for h in range(HH):
                    hv = slice(h * P, (h + 1) * P)
                    t.matmul(bank(5)[:, hv], scoresT[:, 2 * h + 1, :], vh[:, 1, hv], start=True, stop=False)
                    ins = t.matmul(bank(5)[:, hv], crossT[:, h, :], vh[:, 0, hv], start=False, stop=True)
                ins.then_inc(o_done, 1)
                pe.wait_ge(conv_done, HH)
                pe.wait_ge(o_read, 1)
                for b in range(TB):
                    for c in range(HH):
                        ins = t.transpose(bank(4 + b)[:, c * P:(c + 1) * P], cacc[:, c, b * P:(b + 1) * P], ident)
                ins.then_inc(ct_done, 1)
                pe.wait_ge(on_ready, 1)
                for h in range(HH):
                    for b in range(TB):
                        at = (h % 2) * S + b * P
                        ins = t.transpose(bank(6 + h // 2)[:, at:at + P], oh[:, b, h * P:(h + 1) * P], ident)
                ins.then_inc(ot_done, 1)
                pe.wait_ge(cn_ready, TB)
                for c in range(HH):
                    for b in range(TB):
                        at = (c % 2) * S + b * P
                        ins = t.transpose(bank(4 + c // 2)[:, at:at + P], cnorm[:, b, c * P:(c + 1) * P], ident)
                    if c % 2 == 1:
                        ins.then_inc(cb_done, 1)
                split_unit(0, 10, T_OUT, False, True)
                split_unit(0, 11, T_OUT, False)

            def mixer1():
                for u in range(4):
                    split_unit(1, u, T_MIX, True, u == 0)
                pe.wait_ge(t5_in, 16)
                for h in range(DH):
                    ins = t.matmul(bank(4 + h // 2)[:, (h % 2) * S:(h % 2 + 1) * S], anti, biasrev[:, h, :],
                                   start=True, stop=True)
                ins.then_inc(t5_turned, 1)
                split_unit(1, 4, T_MIX, False)
                split_unit(1, 5, T_MIX, False)

                def scores(j):
                    hp, i = j // 2, j % 2
                    if j >= 1:
                        pe.wait_ge(dsc_read, 2 * j)
                    for h in range(2):
                        for m in range(2):
                            mp = slice(64 * m, 64 * m + 64)
                            ins = t.matmul(bank(4 + m)[:, h * S:h * S + P * (i + 1)],
                                           qd[mp, 2 * hp + h, i * P:(i + 1) * P],
                                           kd[mp, 2 * hp + h, 0:P * (i + 1)], start=True, stop=True)
                    ins.then_inc(dsc_done, 1)

                wait_read(pe, 1, 3)
                pe.wait_ge(t5_ready, 1)
                scores(0)
                for j in range(DH):
                    hp, i = j // 2, j % 2
                    unit(1, 6 + j // 2, memT, j < 4, part=i)
                    if j + 1 < DH:
                        scores(j + 1)
                    pe.wait_ge(da_ready, 2 * j + 2)
                    if j >= 1:
                        pe.wait_ge(dat_read, j)
                    for h in range(2):
                        for c in range(i + 1):
                            at = (h * (i + 1) + c) * P
                            ins = t.transpose(bank(6)[:, at:at + P], sD[i][:, 0, h, c * P:(c + 1) * P], ident)
                    ins.then_inc(dat_done, 1)
                    pe.wait_ge(dat_read, j + 1)
                    wait_read(pe, 1, 5)
                    if j >= 1:
                        pe.wait_ge(do_read, j)
                    for h in range(2):
                        for c in range(i + 1):
                            ins = t.matmul(bank(7)[:, h * P:(h + 1) * P], aTD[:, h, c, :],
                                           vd[:, c, (2 * hp + h) * P:(2 * hp + h + 1) * P],
                                           start=(c == 0), stop=(c == i))
                    ins.then_inc(do_done, 1)
                pe.wait_ge(do_read, DH)
                pe.wait_ge(on_ready, 1 + TB)
                for h in range(DH):
                    for b in range(TB):
                        at = (h % 2) * S + b * P
                        ins = t.transpose(bank(4 + h // 2)[:, at:at + P], od[:, b, h * P:(h + 1) * P], ident)
                    if h % 2 == 1:
                        ins.then_inc(ot_done, 1)
                split_unit(1, 10, T_OUT, False, True)
                split_unit(1, 11, T_OUT, False)

            def cross_attention(L):
                n = N_XA0 if L == 0 else N_XA1
                norm_T(n)
                split_unit(L, 12, T_XA, True, True)
                split_unit(L, 13, T_XA, True)
                wait_read(pe, L, 9)
                wait_read(pe, L, 13)
                for c in range(4):
                    i, hp = c // 2, c % 2
                    for j in range(2):
                        for k in range(2):
                            f = 2 * (2 * hp + j) + k
                            ins = t.matmul(bank(4 + c)[:, j * M:(j + 1) * M], qx[:, f, i * P:(i + 1) * P],
                                           kmem[:, f, :], start=(k == 0), stop=(k == 1))
                    ins.then_inc(xsc_done, 1)
                for c in range(4):
                    pe.wait_ge(xp_ready, 4 * L + c + 1)
                    for m in range(2):
                        for j in range(2):
                            at = (2 * m + j) * P
                            ins = t.transpose(bank(4 + c)[:, at:at + P], px[:, c, j, m * P:(m + 1) * P], ident)
                    ins.then_inc(xpt_done, 1)
                pe.wait_ge(xpt_read, 4 * (L + 1))
                for f in range(KD):
                    for m in range(2):
                        ins = t.matmul(bank(4 + f // 2)[:, (f % 2) * S:(f % 2 + 1) * S], vmem[:, m, f * P:(f + 1) * P],
                                       pxT[:, m, f // 2, :], start=(m == 0), stop=(m == 1))
                    if f % 2 == 1:
                        ins.then_inc(xo_done, 1)
                split_unit(L, 14, T_XO, False, True)
                split_unit(L, 15, T_XO, False)

            def moe(L):
                n = N_FFN0 if L == 0 else N_FFN1
                norm_T(n)
                wait_hT(n)
                for b in range(TB):
                    for k in range(KD):
                        ins = t.matmul(bank(4)[:, b * (NG + NE):(b + 1) * (NG + NE)], hT[:, k, b * P:(b + 1) * P],
                                       wr[L][:, k, :], start=(k == 0), stop=(k == KD - 1))
                ins.then_inc(rl_done, 1)
                pe.wait_ge(member_ready, L + 1)
                mem_ = r16[1]
                t.matmul(bank(5)[:, 0:NE], upper, mem_[:, 0, :], start=True, stop=True)
                t.matmul(bank(5)[:, NE:2 * NE], upper, mem_[:, 1, :], start=True, stop=False)
                t.matmul(bank(5)[:, NE:2 * NE], ones, mem_[:, 0, :], start=False, stop=True)
                t.matmul(bank(5)[:, 2 * NE:3 * NE], ones, mem_[:, 0, :], start=True, stop=False)
                t.matmul(bank(5)[:, 2 * NE:3 * NE], ones, mem_[:, 1, :], start=False, stop=True).then_inc(rank_done, 1)

                def gather(half):
                    for k in range(4 * half, 4 * half + 4):
                        for b in range(TB):
                            ins = t.matmul(bank(6)[:, (k % 4) * P:(k % 4 + 1) * P],
                                           xs[:, b, :].rearrange("p (r k) -> p k r", k=KD)[:, k, :], psel[:, b, :],
                                           start=(b == 0), stop=(b == TB - 1))
                    ins.then_inc(g_done, 1)

                def first(j, tokens, done, start_sem=None):
                    for r in range(2):
                        pe.wait_ge(landed[slot(L, PROJ + EU * j + r)], where(j, r))
                        w = ring[:, slot(L, PROJ + EU * j + r), :].rearrange("p (k c n) -> p k c n", k=KD, c=2)
                        for k in range(KD):
                            for c in range(2):
                                ins = t.matmul(bank(4)[64 * c:64 * c + 64, r * S:(r + 1) * S], tokens[:, k, :],
                                               w[:, k, c, :], start=(k == 0), stop=(k == KD - 1))
                                if start_sem is not None:
                                    ins.then_inc(start_sem, 1)
                                    start_sem = None
                    ins.then_inc(done, 1)

                def turn(sel, hidden, done):
                    for b in range(TB):
                        t.transpose(bank(7)[:, b * P:(b + 1) * P], sel[:, b, :], ident)
                    for m in range(2):
                        ins = t.transpose(bank(7)[:, S + m * P:S + (m + 1) * P],
                                          hidden.rearrange("p (r m) -> p m r", m=2)[:, m, :], ident)
                    ins.then_inc(done, 1)

                def second(j, hidden, dst, swap, done):
                    pe.wait_ge(landed[slot(L, PROJ + EU * j + 2)], where(j, 2))
                    w = ring[:, slot(L, PROJ + EU * j + 2), :].rearrange("p (c m n) -> p c m n", c=2, m=2)
                    for c in range(2):
                        for m in range(2):
                            at = m * P + c * CAP
                            for o in range(2):
                                half = slice(64 * (o ^ swap), 64 * (o ^ swap) + 64)
                                ins = t.matmul(dst[half, :], hidden[:, at:at + CAP],
                                               w[:, c, m, o * 512:(o + 1) * 512], start=(c + m == 0), stop=(c + m == 2))
                    ins.then_inc(done, 1)

                def scatter():
                    for b in range(TB):
                        for o in range(2):
                            ins = t.matmul(bank(2 * b + o), pturn[o][:, b * P:(b + 1) * P], ysb[o],
                                           start=False, stop=False, skip_group_check=True)
                    ins.then_inc(scatter_done, 1)

                def where(j, r):
                    return it * 16 + arrival(L, PROJ + EU * j + r)

                wait_read(pe, L, 15)
                pe.wait_ge(table_ready, L + 1)
                pe.wait_ge(psel_ready, (NE // 2 + 1) * L + 1)
                zb = zeros.bitcast(mybir.dt.bfloat16)
                for b in range(4):
                    ins = t.matmul(bank(b), zb[:, 0:P], zb[:, 0:512], start=True, stop=False, skip_group_check=True)
                if L == 0:
                    ins.then_inc(xdone, 1)
                gather(0)
                pe.wait_ge(hsel_ready, (NE + 2) * L + 1)
                gather(1)
                with pe.Fori(0, NE // 2) as it:
                    for j in range(2):
                        pe.wait_ge(hsel_ready, it * 2 + ((NE + 2) * L + 2))
                        first(j, hsel[:, :, j * CAP:(j + 1) * CAP], h_done, expert_done)
                        if j == 0:
                            pe.wait_ge(psel_ready, it + ((NE // 2 + 1) * L + 2))
                            gather(0)
                        else:
                            pe.wait_ge(hsel_ready, it * 2 + ((NE + 2) * L + 3))
                            gather(1)
                        pe.wait_ge(hid_ready, it * 2 + (L * NE + j + 1))
                        if j == 1:
                            pe.wait_ge(pturn_ready, it * 2 + (L * NE + 1))
                        turn(pgate[1 - j], hid, t_done)
                        if j == 0:
                            pe.wait_ge(ysb_ready, it * 2 + (L * (NE + 1) + 1))
                            scatter()
                        pe.wait_ge(hturn_ready, it * 2 + (L * NE + j + 1))
                        second(j, hturn, bank(5), j, y_done)
                        x0, x1 = rounds(t, it * 2 + j)
                        with pe.If(x1 > x0):
                            with pe.Fori(x0, x1) as X:
                                pe.wait_ge(xp, X + 1)
                                for k in range(KD):
                                    for b in range(TB):
                                        ins = t.matmul(bank(4)[:, k * CAP:(k + 1) * CAP],
                                                       xs[:, b, :].rearrange("p (r k) -> p k r", k=KD)[:, k, :],
                                                       pselx[:, b, :], start=(b == 0), stop=(b == TB - 1))
                                ins.then_inc(xg, 1)
                                pe.wait_ge(xh, X + 1)
                                first(j, hselx, xH)
                                pe.wait_ge(xhid, X + 1)
                                turn(pgatex, hidx, xT)
                                pe.wait_ge(xt, X + 1)
                                second(j, tsbx[:, S:2 * S], bank(4), 0, xY)
                                pe.wait_ge(xy, X + 1)
                                for b in range(TB):
                                    for o in range(2):
                                        half = slice(64 * o, 64 * o + 64)
                                        ins = t.matmul(bank(2 * b + o), tsbx[half, b * P:(b + 1) * P], ysbx[half, :],
                                                       start=False, stop=False, skip_group_check=True)
                                ins.then_inc(xdone, 1)
                pe.wait_ge(ysb_ready, (NE + 1) * (L + 1))
                pe.wait_ge(pturn_ready, NE * (L + 1))
                scatter()
                pe.wait_ge(hsel_ready, (NE + 2) * (L + 1))
                t.matmul(bank(6)[:, 0:2], zb[:, 0:P], zb[:, 0:2], start=True, stop=True).then_inc(expert_done, 1)

            norm_T(N_MIX0)
            norm_T(N_MEM)
            mixer0()
            cross_attention(0)
            moe(0)
            norm_T(N_MIX1)
            mixer1()
            cross_attention(1)
            moe(1)


INPUTS = ["x", "mem", "final_norm_g", "even_w_in", "even_w_out", "odd_w_qkv", "odd_w_out", "xa_wq", "xa_wkv",
          "xa_wo", "moe_w1", "moe_w3", "moe_w2"]


def lay_out(inputs):
    g = {n: np.asarray(v) for n, v in inputs.items()}
    arrays = {f"in_{n}": np.ascontiguousarray(g[n]) for n in INPUTS}

    def columns(v):
        return v.reshape(-1, P).T

    def everywhere(v):
        return np.broadcast_to(v.reshape(1, -1), (P, v.size))

    consts, masks = shape_constants()
    norms = [g["norm_mix_g"][0], g["mem_norm_g"], g["norm_xattn_g"][0], g["norm_ffn_g"][0], g["norm_mix_g"][1],
             g["norm_xattn_g"][1], g["norm_ffn_g"][1]]
    router = [np.concatenate([g["moe_w_grp"][i], g["moe_w_exp"][i]], 1).reshape(P, -1) for i in range(DEPTH)]
    arrays["in_small"] = np.concatenate(
        [consts, *(n.reshape(P, KD) for n in norms),
         columns(g["conv_db"][0]), columns(g["conv_ln_g"][0]), columns(g["conv_ln_b"][0]),
         columns(g["hgrn_norm_g"][0]), columns(g["subln_g"][0]), columns(g["hgrn_lb"][0]),
         *(everywhere(np.concatenate([g["moe_b_grp"][i], g["moe_b_exp"][i]])) for i in range(DEPTH)), *router], 1)
    arrays["in_mixc"] = np.concatenate(
        [masks, g["conv_dw"][0].reshape(CONVW, HH, P).transpose(2, 1, 0).reshape(P, -1)], 1)
    early = np.zeros((P, EARLY), np.float32)
    early[:, 0:256] = everywhere(np.concatenate([g[n][0] for n in ("lam_q1", "lam_k1", "lam_q2", "lam_k2")]))
    early[0:RELS, 256:256 + DH] = g["rel_bias"]
    early[RELS, 256:256 + DH] = -BIG
    early[0:RELS + 1, 256 + DH:] = t5_onehot()
    arrays["in_early"] = early
    return arrays


def kernel(**inputs):
    import concourse.bacc as bacc
    from concourse.bass_utils import run_bass_kernel_spmd

    arrays = lay_out(inputs)
    nc = bacc.Bacc("TRN2", target_bir_lowering=False, num_devices=1)
    aps = {n[3:]: nc.dram_tensor(n, v.shape, mybir.dt.from_np(v.dtype), kind="ExternalInput").ap()
           for n, v in arrays.items()}
    y = nc.dram_tensor("out", (1, S, D), F32, kind="ExternalOutput").ap()
    build(nc, aps, y)
    r = run_bass_kernel_spmd(nc, [arrays], core_ids=[0])
    return r.results[0]["out"]
```

```python
import math
from contextlib import ExitStack

import numpy as np
import concourse.bass as bass
from concourse import mybir

F32 = mybir.dt.float32
I32 = mybir.dt.int32
R32 = mybir.dt.float32r
ALU = mybir.AluOpType
ACT = mybir.ActivationFunctionType
AX = mybir.AxisListType

P = 128
D, S, M = 1024, 256, 256
KD = D // P
TB = S // P
DEPTH = 2
EPS = 1e-6
UNIT = 4096
SLOTS = 6
PROJ = 16
PIECES = 4
NE, NG, EPG = 16, 4, 4
EU = 3
CAP = 64
EXTRA = 2
FF = 512
CONVW = 31
PAD = CONVW - 1
HH = 4
DH = 8
LAM_INIT = 0.8 - 0.6 * math.exp(-0.3)
BIG = 1e30
BW = 384
RELS = 32
LEVELS = 7
LN_SPLIT = 2.0 ** 60

N_MIX0, N_MEM, N_XA0, N_FFN0, N_MIX1, N_XA1, N_FFN1, N_FINAL = range(8)

DVE_UNITS = (10, 11, 14, 15)
R_DB, R_LNG, R_LNB, R_HG, R_SUB, R_LB = 0, 4, 8, 12, 13, 14
ROWS = 18


NR = NG + NE
O_GAINS = 5 * P + NE
O_VECS = O_GAINS + 7 * KD
O_RBIAS = O_VECS + ROWS
O_WR = O_RBIAS + DEPTH * NR
SMALL = O_WR + DEPTH * KD * NR
MIXC = (LEVELS + 1) * P + HH * CONVW
EARLY = 256 + DH + BW


def t5_onehot():
    rel = 2 * P - 1 - np.arange(BW)
    n = np.maximum(rel, 0)
    half = RELS // 2
    nf = np.maximum(n, 1).astype(np.float32)
    large = half + (np.log(nf / half) / np.float32(math.log(128 / half)) * half).astype(np.int32)
    bucket = np.where(n < half, n, np.clip(large, 0, RELS - 1))
    out = np.zeros((RELS + 1, BW), np.float32)
    ok = rel >= 0
    out[bucket[ok], np.arange(BW)[ok]] = 1.0
    out[RELS, ~ok] = 1.0
    return out


def shape_constants():
    i = np.arange(P)
    ident = np.eye(P)
    upper = (i[:, None] < i[None, :]) * 1.0
    ones = np.ones((P, P))
    places = np.tile(i % CAP + 1, (P, 1))
    s, t = i[:, None], i[None, :]
    masks = [(s == t) * 1.0]
    for lev in range(1, LEVELS + 1):
        m = 2 ** (lev - 1)
        masks.append(((s // (2 * m) == t // (2 * m)) & (s % (2 * m) < m) & (t % (2 * m) >= m)) * 1.0)
    ties = np.tile(np.arange(NE, 0, -1), (P, 1))
    return (np.concatenate([ident, upper, ones, places, ident[::-1], ties], 1).astype(np.float32),
            np.concatenate(masks, 1).astype(np.float32))


class Own:

    def __init__(self, eng):
        self.eng, self.base, self.n, self.last = eng, {}, {}, None

    def value(self, sem):
        return self.base.get(sem.name, 0) + self.n.get(sem.name, 0)

    def inc(self, ins, sem):
        self.n[sem.name] = self.n.get(sem.name, 0) + 1
        ins.then_inc(sem, 1)
        self.last = (sem, self.value(sem))

    def wait(self, back=0):
        self.eng.wait_ge(self.last[0], self.last[1] - back)

    def enter(self, i, per):
        self.outer = {s.name: self.value(s) for s in per}
        for s, k in per.items():
            self.base[s.name], self.n[s.name] = i * k + self.outer[s.name], 0

    def leave(self, times, per):
        for s, k in per.items():
            assert self.n[s.name] == k, (s.name, self.n[s.name], k)
            self.base[s.name], self.n[s.name] = self.outer[s.name] + times * k, 0


def build(nc, a, out):
    ctx = ExitStack()
    with ctx:
        offsets = {}

        def sb(name, shape, dt=F32):
            offsets[name] = (nc.sbuf_base + 31) // 32 * 32
            return ctx.enter_context(nc.sbuf_tensor(name, shape, dt))

        def in_place_of(name, at, shape):
            return nc.alloc_sbuf_tensor_at(f"{name}_{at}_r", [P, *shape], R32, offset=offsets[name] + 4 * at)

        def sem(name):
            return ctx.enter_context(nc.semaphore(name))

        ring = sb("ring", [P, SLOTS, UNIT])
        x = sb("x", [P, TB, D])
        xs = sb("xs", [P, TB, D])
        hT = sb("hT", [P, KD, S])
        memT = sb("memT", [P, KD, M])
        kmem = sb("kmem", [P, KD, M])
        vmem = sb("vmem", [P, TB, D])
        AR = 13432
        arena = sb("arena", [P, AR])
        small = sb("small", [P, SMALL])
        mixc = sb("mixc", [P, MIXC])
        st = sb("st", [P, 160])
        xtab = sb("xtab", [P, NE + 1], I32)
        ps = ctx.enter_context(nc.psum_tensor("ps", [P, 8, 512], F32))
        bias_dram = nc.dram_tensor("bias_dram", [DH, BW], F32)

        ident, upper, ones, places, anti = (small[:, i * P:(i + 1) * P] for i in range(5))
        ties = small[:, 5 * P:5 * P + NE]
        gains = small[:, O_GAINS:O_VECS].rearrange("p (n k) -> p n k", k=KD)
        vecs = small[:, O_VECS:O_RBIAS]
        rbias = [small[:, O_RBIAS + i * NR:O_RBIAS + (i + 1) * NR] for i in range(DEPTH)]
        wr = [small[:, O_WR + i * KD * NR:O_WR + (i + 1) * KD * NR].rearrange("p (k n) -> p k n", k=KD)
              for i in range(DEPTH)]
        masks = mixc[:, 0:(LEVELS + 1) * P].rearrange("p (l t) -> p l t", t=P)
        dwT = mixc[:, (LEVELS + 1) * P:].rearrange("p (c j) -> p c j", j=CONVW)

        ss, ms, rt, rs = st[:, 0:2], st[:, 2:4], st[:, 4:6], st[:, 6:8]
        lam2, lamexp, lamd, lamv = st[:, 8:10], st[:, 10:12], st[:, 12:13], st[:, 150:154]
        lbz, lbe, lbr, lbp, lb, oml = (st[:, 16 + 4 * i:20 + 4 * i] for i in range(6))
        oss, oms, ort, ors = (st[:, 40 + 16 * i:56 + 16 * i] for i in range(4))
        bn, mv, crt, crs = st[:, 104:116], st[:, 116:120], st[:, 120:122], st[:, 122:124]
        sub = st[:, 124:125]
        xmx, xsum, xrc = st[:, 126:134], st[:, 134:142], st[:, 142:150]
        xcarry = st[:, 158:159]
        dmx, dsum, drc = (st[:, 126 + 8 * i:134 + 8 * i] for i in range(3))
        cve = st[:, 138:140]
        tbl = st[:, 159:160]

        def carve(at, shape):
            n = int(np.prod(shape))
            assert at + n <= AR, (at, n)
            v = arena[:, at:at + n]
            if len(shape) == 2:
                return v.rearrange("p (a b) -> p a b", b=shape[1])
            if len(shape) == 3:
                return v.rearrange("p (a b c) -> p a b c", b=shape[1], c=shape[2])
            return v

        hThi = in_place_of("hT", 0, [KD, S])
        hTlo = [in_place_of("arena", 9336, [KD, S]), in_place_of("xs", 0, [KD, S]), in_place_of("arena", 11264, [KD, S])]
        pieces = {True: (in_place_of("kmem", 0, [PIECES, 512]), in_place_of("vmem", 0, [PIECES, 512])),
                  False: (in_place_of("arena", 1024, [PIECES, 512]), in_place_of("arena", 3072, [PIECES, 512]))}

        fgate = carve(0, [1024])
        logf = carve(1024, [1024])
        bcum = carve(2048, [1024])
        qh = carve(3072, [1024])
        kh = carve(4096, [1024])
        vh = carve(5120, [TB, 512])
        gh = carve(6144, [TB, 512])
        upad = carve(7168, [HH, PAD + S])
        cacc = carve(8312, [HH, S])
        Ebuf = [carve(1024, [1024]), carve(0, [1024])]
        Qt = [carve(9336, [1024]), carve(10360, [1024])]
        Kt = [carve(11384, [1024]), carve(12408, [1024])]
        scanmask = xs[:, 0, :]
        lntmp = xs[:, 1, :]
        scoresT = xs[:, 0, :].rearrange("p (a b) -> p a b", b=P)
        crossT = carve(0, [HH, P])
        oh = carve(9336, [TB, 512])
        ohsq = carve(11384, [TB, 512])
        cnorm = carve(10360, [TB, 512])
        csilu = carve(11384, [HH, S])
        early = carve(12408, [EARLY])
        lamrow = early[:, 0:256].rearrange("p (i n) -> p i n", i=4)
        table = early[0:RELS + 1, 256:256 + DH]
        onehot = early[0:RELS + 1, 256 + DH:]
        t5stage = carve(11384, [BW])[0:DH, :]

        qd = carve(0, [DH, S])
        kd = carve(2048, [DH, S])
        vd = carve(4096, [TB, D])
        biasd = carve(6144, [DH, 2 * P])
        biasrev = carve(4096, [DH, 2 * P])
        sD = [carve(8192, [2, 2, S]), carve(9216, [2, 2, S])]
        aTD = carve(10240, [2, TB, P])
        odsq = carve(10752, [TB, D])
        od = xs

        qx = carve(5120, [KD, S])
        px = carve(7168, [4, 2, M])
        pxT = carve(9216, [TB, 4, S])

        hsel = carve(0, [KD, P])
        psel = carve(1024, [TB, P])
        pgate = [carve(1280, [TB, P]), carve(1536, [TB, P])]
        pturn = [carve(1792, [S]), carve(2048, [S])]
        hturn = carve(2304, [S])
        sil = carve(2816, [S])
        hid = carve(3072, [S])
        ysb = [carve(3328, [512]), carve(3840, [512])]
        hselx = carve(4352, [KD, CAP])
        pselx = carve(4864, [TB, CAP])
        pgatex = carve(4992, [TB, P])
        tsbx = carve(5248, [512])
        silx = carve(5760, [S])
        hidx = carve(6016, [S])
        ysbx = carve(6272, [512])
        lg = carve(6964, [TB, NG + NE])
        r4 = [carve(7004 + 8 * i, [TB, NG]) for i in range(4)]
        r16 = [carve(7036 + 32 * i, [TB, NE]) for i in range(8)]
        r1 = [carve(7292 + 2 * i, [TB, 1]) for i in range(10)]
        gate = carve(7312, [TB, NE])
        rank = carve(7344, [TB, NE + 2])
        nx = carve(7382, [NE])
        cumx = carve(7414, [NE + 1])
        zeros = carve(7432, [512])
        fgain = carve(7944, [D])
        spare = [nc.alloc_sbuf_tensor_at("spare", [P, UNIT], F32, offset=offsets["kmem"])[:, :],
                 carve(8968, [UNIT])]

        def bank(b):
            return ps[:, b, :]

        def pair(pj):
            b = 2 * (pj % 2)
            return ps[:, b:b + 2, :]

        landed = [sem(f"landed{i}") for i in range(SLOTS)]
        spare_in = [sem(f"spare{i}_in") for i in range(2)]
        names = """x_in mem_in small_in mixc_in early_in t5_stored t5_in fgain_in out_done piece_hi piece_lo
            piece_used hi_ready lo_ready b_ready kt_zero kt_ready proj_done proj_read_act proj_read_dve
            act_step dve_step upad_zero t5_row t5_read t5_turned t5_ready lb_zero lb_exp lam_dot lam_exp sq_act
            ms_ready rt_ready rs_ready xs_act xs_dve tr_done cs_ready hT_act hT_dve x_new f_ready ln_ready
            k_ready conv_done arg_ready exp_ready lev_ready lev_done lev_read scores_ready cross_done
            cross_read o_done o_read o_sq oms_ready ort_ready on_ready ot_done ct_done cv_ready cr_ready
            cn_ready cb_done xsc_done xmax_ready xexp_ready xp_ready xpt_done xpt_read xo_done dsc_done
            dsc_read dmax_ready dexp_ready da_ready dat_done dat_read do_done do_read rl_done rexp_in
            rexp_ready member_ready rank_done table_ready psel_ready g_done hsel_used hsel_ready h_done
            sil_ready hid_ready t_done hturn_ready pturn_ready scatter_done y_done ysb_ready expert_done
            w13_free y_out more_chosen more_gathered more_tokens more_products more_silu more_hidden
            more_turned more_turns_read more_out more_out_read more_done more_step""".split()
        (x_in, mem_in, small_in, mixc_in, early_in, t5_stored, t5_in, fgain_in, out_done, piece_hi, piece_lo,
         piece_used, hi_ready, lo_ready, b_ready, kt_zero, kt_ready, proj_done, proj_read_act, proj_read_dve,
         act_step, dve_step, upad_zero, t5_row, t5_read, t5_turned, t5_ready, lb_zero, lb_exp, lam_dot, lam_exp,
         sq_act, ms_ready, rt_ready, rs_ready, xs_act, xs_dve, tr_done, cs_ready, hT_act, hT_dve, x_new,
         f_ready, ln_ready, k_ready, conv_done, arg_ready, exp_ready, lev_ready, lev_done, lev_read,
         scores_ready, cross_done, cross_read, o_done, o_read, o_sq, oms_ready, ort_ready, on_ready, ot_done,
         ct_done, cv_ready, cr_ready, cn_ready, cb_done, xsc_done, xmax_ready, xexp_ready, xp_ready, xpt_done,
         xpt_read, xo_done, dsc_done, dsc_read, dmax_ready, dexp_ready, da_ready, dat_done, dat_read, do_done,
         do_read, rl_done, rexp_in, rexp_ready, member_ready, rank_done, table_ready, psel_ready, g_done,
         hsel_used, hsel_ready, h_done, sil_ready, hid_ready, t_done, hturn_ready, pturn_ready, scatter_done,
         y_done, ysb_ready, expert_done, w13_free, y_out, more_chosen, more_gathered, more_tokens,
         more_products, more_silu, more_hidden, more_turned, more_turns_read, more_out, more_out_read,
         more_done, more_step) = (sem(n) for n in names)
        MORE_STEPS = 4

        def col_unit(w, c, by_row):
            v = w.rearrange("(p k) n -> p k n", k=KD) if by_row else w.rearrange("(k p) n -> p k n", p=P)
            return v[:, :, c * 512:(c + 1) * 512]

        def proj_source(L, u):
            if u < 6:
                if L == 0:
                    return col_unit(a["even_w_in"][0], (5, 4, 1, 0, 2, 3)[u], True)
                return col_unit(a["odd_w_qkv"][0], u, True)
            if u < 10:
                return col_unit(a["xa_wkv"][L], u - 6, True)
            if u < 12:
                return col_unit((a["even_w_out"] if L == 0 else a["odd_w_out"])[0], u - 10, False)
            if u < 14:
                return col_unit(a["xa_wq"][L], u - 12, True)
            return col_unit(a["xa_wo"][L], u - 14, False)

        LAYER_UNITS = PROJ + EU * NE
        EX_DONE = NE + 1
        assert EU * 2 == SLOTS

        def slot(L, u):
            return (L * LAYER_UNITS + u) % SLOTS

        def arrival(L, u):
            elsewhere = sum(slot(l, PROJ + EU * EXTRA + r) == slot(L, u) and (l, PROJ + EU * EXTRA) < (L, u)
                            for l in range(L + 1) for r in range(2))
            return 16 * ((L * LAYER_UNITS + u) // SLOTS + 1 - elsewhere)

        def read_count(L, u):
            mine = [v for v in range(u + 1) if (v in DVE_UNITS) == (u in DVE_UNITS)]
            per = len(DVE_UNITS) if u in DVE_UNITS else PROJ - len(DVE_UNITS)
            return (proj_read_dve if u in DVE_UNITS else proj_read_act), L * per + len(mine)

        def wait_read(eng, L, u):
            s_, v_ = read_count(L, u)
            eng.wait_ge(s_, v_)

        def wait_source(eng, n, blk):
            if n == N_MIX0:
                eng.wait_ge(x_in, 16)
            elif n == N_MEM:
                eng.wait_ge(mem_in, 16)
            elif n in (N_XA0, N_FFN0, N_XA1, N_FFN1):
                wait_read(eng, 0 if n in (N_XA0, N_FFN0) else 1, 11 if n in (N_XA0, N_XA1) else 15)
            else:
                eng.wait_ge(x_new, (2 if n == N_MIX1 else 4) - 1 + blk)

        def norm_buffers(n):
            if n == N_MEM:
                return kmem[:, :, :].rearrange("p a b -> p (a b)").rearrange("p (b d) -> p b d", b=TB), vmem, memT
            return x, xs, hT

        def rounds(e_, e):
            return (e_.value_load(xtab[0:1, bass.ds(e, 1)], min_val=0, max_val=64),
                    e_.value_load(xtab[0:1, bass.ds(e + 1, 1)], min_val=0, max_val=64))

        SPLIT = [u for u in range(PROJ) if not 6 <= u < 10]
        T_MIX, T_OUT, T_XA, T_XO = range(4)

        def split_at(L, u):
            return L * len(SPLIT) + SPLIT.index(u)

        def piece(L, u, k):
            hi, lo = pieces[u < 6 and (L, u) not in ((0, 0), (0, 1))]
            return split_at(L, u) * KD + k, hi[:, k % PIECES, :], lo[:, k % PIECES, :]

        def wait_piece_used(eng, L, u, k):
            n, k = split_at(L, u), k - PIECES
            if k < 0:
                n, k = n - 1, k + KD
            if n < 0:
                return
            if k == KD - 1:
                L_, i_ = divmod(n, len(SPLIT))
                eng.wait_ge(proj_done, L_ * PROJ + SPLIT[i_] + 1)
            else:
                eng.wait_ge(piece_used, n * (KD - 1) + k + 1)

        def turn_lo(L, t_):
            return hTlo[t_] if L == 0 and t_ in (T_MIX, T_OUT) else hTlo[2]

        def norm_turn(n):
            return {N_MIX0: (0, T_MIX), N_XA0: (0, T_XA), N_MIX1: (1, T_MIX), N_XA1: (1, T_XA)}.get(n)

        def plain_turns(n):
            return sum(norm_turn(m) is None for m in range(n + 1))

        def halves(b_, lev):
            m = 2 ** (lev - 1)
            w = b_.rearrange("p (n s m) -> p n s m", s=2, m=m)
            return w[:, :, 0, :], w[:, :, 1, :], m

        TAPS_BEFORE, TAPS_AFTER, TAPS_PER_LEVEL = 4, 13, 3

        block = ctx.enter_context(nc.Block())

        @block.sync
        def _(sp):
            sp.dma_start(x[:, :, :], a["x"][0].rearrange("(b p) d -> p b d", p=P)).then_inc(x_in, 16)
            sp.wait_ge(small_in, 16)
            for L in range(DEPTH):
                for u in range(PROJ):
                    if u >= SLOTS:
                        sp.wait_ge(proj_done, L * PROJ + u - SLOTS + 1)
                    elif L > 0:
                        e = NE - 2 + u // EU
                        if u % EU == EU - 1:
                            sp.wait_ge(expert_done, (L - 1) * EX_DONE + e + 2)
                        else:
                            sp.wait_ge(w13_free, (L - 1) * NE + e + 1)
                    s_ = slot(L, u)
                    sp.dma_start(ring[:, s_, :].rearrange("p (k n) -> p k n", k=KD),
                                 proj_source(L, u)).then_inc(landed[s_], 16)
                    if (L, u) == (0, 0):
                        sp.dma_start(norm_buffers(N_MEM)[0], a["mem"][0].rearrange("(b p) d -> p b d", p=P)
                                     ).then_inc(mem_in, 16)
                        sp.dma_start(mixc[:, :], a["mixc"]).then_inc(mixc_in, 16)

                def load_expert(e, j, r):
                    s_ = slot(L, PROJ + EU * j + r)
                    if r < 2:
                        w = a["moe_w1" if r == 0 else "moe_w3"][L]
                        dst, done = (ring[:, s_, :], landed[s_]) if type(e) is not int or e != EXTRA else (spare[r], spare_in[r])
                        sp.dma_start(dst, w[bass.ds(e, 1), :, :].rearrange("e (p k) f -> p (e k f)", k=KD)
                                     ).then_inc(done, 16)
                    else:
                        w = a["moe_w2"][L]
                        sp.dma_start(ring[:, s_, :].rearrange("p (c n) -> p c n", c=2),
                                     w[bass.ds(e, 1), :, :].rearrange("e (c r m) d -> r (e c) (m d)", c=2, m=2)
                                     ).then_inc(landed[s_], 16)

                for j in range(2):
                    for r in range(EU):
                        sp.wait_ge(proj_done, L * PROJ + PROJ - SLOTS + EU * j + r + 1)
                        load_expert(j, j, r)

                def load_w13(it, j):
                    sp.wait_ge(w13_free, it * 2 + (L * NE + j - 1))
                    load_expert(it * 2 + j, j, 0)
                    load_expert(it * 2 + j, j, 1)

                def load_w2(it, j):
                    sp.wait_ge(expert_done, it * 2 + (L * EX_DONE + j))
                    load_expert(it * 2 + j, j, 2)

                sp.wait_ge(xo_done, 4 * (L + 1))
                for r in range(2):
                    load_expert(EXTRA, 0, r)
                sp.wait_ge(w13_free, L * NE + 1)
                for r in range(2):
                    load_expert(EXTRA + 2, 0, r)
                load_w2(EXTRA // 2, 0)
                load_w13(EXTRA // 2, 1)
                load_w2(EXTRA // 2, 1)
                load_w2(EXTRA // 2 + 1, 0)
                load_w13(EXTRA // 2 + 1, 1)
                load_w2(EXTRA // 2 + 1, 1)
                with sp.Fori(EXTRA // 2 + 2, NE // 2) as it:
                    for j in range(2):
                        load_w13(it, j)
                        load_w2(it, j)
            for b in range(TB):
                sp.wait_ge(y_out, b + 1)
                sp.dma_start(out[0].rearrange("(b p) d -> p b d", p=P)[:, b, :], xs[:, b, :]).then_inc(out_done, 16)
            sp.wait_ge(out_done, 32)

        @block.gpsimd
        def _(pool):
            g_ = nc.gpsimd
            g_.memset(upad[:, :, 0:PAD], 0.0).then_inc(upad_zero, 1)

            def args(lev):
                if lev == 1:
                    pool.wait_ge(b_ready, 1)
                elif lev > 2:
                    pool.wait_ge(lev_ready, lev - 2)
                    pool.wait_ge(kt_ready, lev - 2)
                b0, b1, m = halves(bcum, lev)
                e0, e1, _ = halves(Ebuf[lev % 2], lev)
                ref = b0[:, :, m - 1:m].to_broadcast([P, 512 // m, m])
                g_.tensor_tensor(e0, ref, b0, ALU.subtract).then_inc(arg_ready, 1)
                if m < P:
                    ins = g_.tensor_tensor(e1, b1, ref, ALU.subtract)
                else:
                    ins = g_.tensor_copy(e1, b1)
                ins.then_inc(arg_ready, 1)

            def weigh_k(lev):
                pool.wait_ge(exp_ready, lev)
                if lev == 1:
                    pool.wait_ge(k_ready, 1)
                    pool.wait_ge(kt_zero, 2)
                else:
                    pool.wait_ge(lev_done, lev - 1)
                g_.tensor_tensor(halves(Kt[lev % 2], lev)[0], halves(kh, lev)[0], halves(Ebuf[lev % 2], lev)[0],
                                 ALU.mult).then_inc(kt_ready, 1)

            for L in range(DEPTH):
                for u in SPLIT:
                    for k in range(KD):
                        n, hi, lo = piece(L, u, k)
                        pool.wait_ge(piece_hi, n + 1)
                        g_.tensor_tensor(lo, ring[:, slot(L, u), k * 512:(k + 1) * 512], hi.bitcast(F32),
                                         ALU.subtract).then_inc(piece_lo, 1)
                    if (L, u) == (0, 5):
                        for lev in range(1, LEVELS + 2):
                            args(lev)
                            if lev > 1:
                                weigh_k(lev - 1)
                        weigh_k(LEVELS + 1)

        @block.scalar
        def _(act):
            s = nc.scalar
            own = Own(act)
            act.dma_start(small[:, :], a["small"]).then_inc(small_in, 16)
            act.dma_start(early, a["early"]).then_inc(early_in, 16)

            def t5_rows():
                act.wait_ge(t5_row, 1)
                own.inc(s.activation(t5stage, bank(2)[0:DH, 0:BW], ACT.Copy), t5_read)
                own.wait()
                act.dma_start(bias_dram.ap(), t5stage).then_inc(t5_stored, 16)

            def constants():
                act.wait_ge(lb_zero, 1)
                own.inc(s.activation(lbe, lbz, ACT.Exp), lb_exp)
                act.wait_ge(lam_dot, 2)
                own.inc(s.activation(lamexp, lam2, ACT.Exp), lam_exp)

            def norm(n):
                src, dst, _ = norm_buffers(n)
                if n > N_MEM:
                    own.inc(s.activation(tbl, ones[:, 0:1], ACT.Sqrt), act_step)
                wait_source(act, n, 0)
                own.inc(s.activation(dst[:, 0, :], src[:, 0, :], ACT.Square, accum_out=ss[:, 0:1]), sq_act)
                act.wait_ge(ms_ready, n + 1)
                own.inc(s.activation(rt, ms, ACT.Sqrt), rt_ready)
                if n < N_FINAL:
                    act.wait_ge(rs_ready, n + 1)
                    own.inc(s.activation(dst[:, 0, :], src[:, 0, :], ACT.Copy, scale=rs[:, 0:1]), xs_act)

            def split(L, u, half):
                for k in range(4 * half, 4 * half + 4):
                    n, hi, _ = piece(L, u, k)
                    if k == 0:
                        act.wait_ge(landed[slot(L, u)], arrival(L, u))
                    wait_piece_used(act, L, u, k)
                    own.inc(s.activation(hi, ring[:, slot(L, u), k * 512:(k + 1) * 512], ACT.Copy), piece_hi)

            def turn_hi(src, b, scale=1.0):
                own.inc(s.activation(hThi[:, 2 * b:2 * b + 2, :], src, ACT.Copy, scale=scale), hi_ready)

            def norm_T(n):
                if norm_turn(n) is not None:
                    for k in range(KD):
                        if k % 2 == 0:
                            act.wait_ge(tr_done, 4 * n + k // 2 + 1)
                        own.inc(s.activation(hThi[:, k, :], bank(4 + k // 2)[:, (k % 2) * S:(k % 2 + 1) * S],
                                             ACT.Copy, scale=gains[:, n, k:k + 1]), hi_ready if k % 2 else act_step)
                    return
                for k in range(4):
                    if k % 2 == 0:
                        act.wait_ge(tr_done, 4 * n + k // 2 + 1)
                    own.inc(s.activation(norm_buffers(n)[2][:, k, :], bank(4 + k // 2)[:, (k % 2) * S:(k % 2 + 1) * S],
                                         ACT.Copy, scale=gains[:, n, k:k + 1]), hT_act)

            def read_unit(L, u, dst, func=ACT.Copy):
                act.wait_ge(proj_done, L * PROJ + u + 1)
                own.inc(s.activation(dst, pair(L * PROJ + u), func), proj_read_act)

            def read_unit_T(L, u, dst, func=ACT.Copy):
                act.wait_ge(proj_done, L * PROJ + u + 1)
                own.inc(s.activation(dst, pair(L * PROJ + u).rearrange("p a (f t) -> p (a f) t", f=2), func),
                        proj_read_act)

            def flat(v):
                return v.rearrange("p (a b) -> p a b", a=2)

            def mixer0():
                def level_exp(lev):
                    act.wait_ge(arg_ready, 2 * lev)
                    own.inc(s.activation(Ebuf[lev % 2], Ebuf[lev % 2], ACT.Exp), exp_ready)

                split(0, 0, 1)
                split(0, 1, 0)
                read_unit(0, 0, flat(cacc[:, :, :].rearrange("p a b -> p (a b)")), ACT.Sigmoid)
                norm_T(N_MEM)
                split(0, 1, 1)
                act.wait_ge(tr_done, 4 * (N_MEM + 1))
                split(0, 2, 0)
                constants()
                read_unit_T(0, 1, upad[:, :, PAD:])
                split(0, 2, 1)
                split(0, 3, 0)
                read_unit(0, 2, flat(fgate), ACT.Sigmoid)
                split(0, 3, 1)
                act.wait_ge(f_ready, 1)
                own.inc(s.activation(lntmp, lntmp, ACT.Ln), act_step)
                own.inc(s.activation(logf, logf, ACT.Ln), ln_ready)
                split(0, 4, 0)
                read_unit(0, 3, flat(qh), ACT.Silu)
                split(0, 4, 1)
                split(0, 5, 0)
                read_unit(0, 4, vh[:, :, :])
                split(0, 5, 1)
                level_exp(1)
                level_exp(2)
                read_unit(0, 5, gh[:, :, :], ACT.Sigmoid)
                level_exp(3)
                read_unit_T(0, 6, kmem[:, 0:4, :])
                level_exp(4)
                level_exp(5)
                read_unit_T(0, 7, kmem[:, 4:8, :])
                level_exp(6)
                level_exp(7)
                read_unit(0, 8, vmem[:, :, 0:512])
                level_exp(8)
                act.wait_ge(o_done, 1)
                own.inc(s.activation(oh[:, :, :], ps[:, 6:8, :], ACT.Copy), o_read)
                own.wait()
                own.inc(s.activation(ohsq[:, :, :], oh[:, :, :], ACT.Square), o_sq)
                split(0, 10, 0)
                act.wait_ge(oms_ready, 1)
                own.inc(s.activation(ort[:, 0:8], oms[:, 0:8], ACT.Sqrt), ort_ready)
                act.wait_ge(cv_ready, 1)
                own.inc(s.activation(crt, cve, ACT.Sqrt), cr_ready)
                read_unit(0, 9, vmem[:, :, 512:1024])
                act.wait_ge(ot_done, 1)
                for b in range(2):
                    turn_hi(bank(6 + b).rearrange("p (f t) -> p f t", f=2), b, vecs[:, R_HG:R_HG + 1])
                for c in range(HH):
                    if c % 2 == 0:
                        act.wait_ge(cb_done, c // 2 + 1)
                    own.inc(s.activation(csilu[:, c, :], bank(4 + c // 2)[:, (c % 2) * S:(c % 2 + 1) * S], ACT.Silu,
                                         bias=vecs[:, R_LNB + c:R_LNB + c + 1],
                                         scale=vecs[:, R_LNG + c:R_LNG + c + 1]), cs_ready)
                for b in range(2):
                    act.wait_ge(cs_ready, 2 * b + 2)
                    turn_hi(csilu[:, 2 * b:2 * b + 2, :], 2 + b)
                out_units(0)

            def out_units(L):
                split(L, 10, 1)
                split(L, 11, 0)
                split(L, 11, 1)
                split(L, 12, 0)

            def read_memory(u):
                if u < 8:
                    read_unit_T(1, u, kmem[:, 4 * (u - 6):4 * (u - 5), :])
                else:
                    read_unit(1, u, vmem[:, :, 512 * (u - 8):512 * (u - 7)])

            def mixer1():
                act.wait_ge(t5_stored, 16)
                act.dma_start(biasrev, bass.AP(bias_dram, 0, [[1, P], [BW, DH], [1, 2 * P]])).then_inc(t5_in, 16)
                for u in range(4):
                    split(1, u, 1)
                    split(1, u + 1, 0)
                    act.wait_ge(proj_done, PROJ + u + 1)
                    dst = (qd if u < 2 else kd)[:, 4 * (u % 2):4 * (u % 2) + 4, :]
                    own.inc(s.activation(dst, pair(PROJ + u).rearrange("p a (f t) -> p (a f) t", f=2), ACT.Copy,
                                         scale=0.125 if u < 2 else 1.0), proj_read_act)
                act.wait_ge(t5_turned, 1)
                own.inc(s.activation(biasd, ps[:, 4:8, :].rearrange("p a (h k) -> p (a h) k", h=2), ACT.Copy), t5_ready)
                split(1, 4, 1)
                split(1, 5, 0)
                read_unit(1, 4, vd[:, :, 0:512])
                split(1, 5, 1)
                read_unit(1, 5, vd[:, :, 512:1024])

                def back(j):
                    hp, i = j // 2, j % 2
                    act.wait_ge(dat_done, j + 1)
                    own.inc(s.activation(aTD[:, :, 0:i + 1, :], bank(6)[:, 0:2 * P * (i + 1)].rearrange(
                        "p (h a b) -> p h a b", h=2, b=P), ACT.Copy), dat_read)
                    act.wait_ge(do_done, j + 1)
                    own.inc(s.activation(od[:, i, 2 * hp * P:2 * (hp + 1) * P], bank(7)[:, 0:2 * P], ACT.Copy), do_read)

                for j in range(DH):
                    i = j % 2
                    nk = P * (i + 1)
                    act.wait_ge(dmax_ready, j + 1)
                    for m in range(2):
                        for h in range(2):
                            c = 4 * i + 2 * m + h
                            own.inc(s.activation(sD[i][:, m, h, 0:nk], sD[i][:, m, h, 0:nk], ACT.Exp,
                                                 bias=dmx[:, c:c + 1], accum_out=dsum[:, c:c + 1]), dexp_ready)
                    if j % 2 == 0 and j >= 2:
                        read_memory(6 + j // 2 - 1)
                    if j >= 1:
                        back(j - 1)
                back(DH - 1)
                split(1, 10, 0)
                act.wait_ge(do_read, DH)
                own.inc(s.activation(odsq, od[:, :, :], ACT.Square), o_sq)
                read_memory(9)
                act.wait_ge(oms_ready, 2)
                own.inc(s.activation(ort, oms, ACT.Sqrt), ort_ready)
                for b in range(4):
                    act.wait_ge(ot_done, 2 + b)
                    turn_hi(bank(4 + b).rearrange("p (f t) -> p f t", f=2), b, sub)
                out_units(1)

            def cross_attention(L):
                split(L, 12, 1)
                split(L, 13, 0)
                read_unit_T(L, 12, qx[:, 0:4, :])
                split(L, 13, 1)
                read_unit_T(L, 13, qx[:, 4:8, :])
                for c in range(4):
                    act.wait_ge(xmax_ready, 4 * L + c + 1)
                    for j in range(2):
                        own.inc(s.activation(px[:, c, j, :], bank(4 + c)[:, j * M:(j + 1) * M], ACT.Exp,
                                             bias=xmx[:, 2 * c + j:2 * c + j + 1], scale=1.0 / 16,
                                             accum_out=xsum[:, 2 * c + j:2 * c + j + 1]), xexp_ready)
                for c in range(4):
                    i, hp = c % 2, c // 2
                    act.wait_ge(xpt_done, 4 * L + c + 1)
                    own.inc(s.activation(pxT[:, :, 2 * hp:2 * hp + 2, i * P:(i + 1) * P],
                                         bank(4 + c).rearrange("p (m h t) -> p m h t", m=2, h=2), ACT.Copy), xpt_read)
                split(L, 14, 0)
                for b in range(4):
                    act.wait_ge(xo_done, 4 * L + b + 1)
                    turn_hi(bank(4 + b).rearrange("p (f t) -> p f t", f=2), b)
                split(L, 14, 1)
                split(L, 15, 0)
                split(L, 15, 1)

            def moe(L):
                if L == DEPTH - 1:
                    act.dma_start(fgain, a["final_norm_g"].unsqueeze(0).broadcast_to([P, D])).then_inc(fgain_in, 16)
                norm_T(N_FFN0 if L == 0 else N_FFN1)
                act.wait_ge(rexp_in, 2 * L + 1)
                own.inc(s.activation(r4[1], r4[0], ACT.Exp), rexp_ready)
                act.wait_ge(rexp_in, 2 * L + 2)
                own.inc(s.activation(r1[8], r1[7], ACT.Exp), rexp_ready)
                act.wait_ge(table_ready, L + 1)
                per = {sil_ready: 2, act_step: 2, ysb_ready: 2}
                with act.Fori(0, NE // 2) as it:
                    own.enter(it, per)
                    for j in range(2):
                        act.wait_ge(h_done, it * 2 + (L * NE + j + 1))
                        own.inc(s.activation(sil, bank(4)[:, 0:S], ACT.Silu), sil_ready)
                        act.wait_ge(y_done, it * 2 + (L * NE + j + 1))
                        own.inc(s.activation(ysb[j][0:64, :], bank(5)[0:64, :], ACT.Copy), act_step)
                        own.inc(s.activation(ysb[1 - j][64:P, :], bank(5)[64:P, :], ACT.Copy), ysb_ready)
                        x0, x1 = rounds(s, it * 2 + j)
                        with act.If(x1 > x0):
                            with act.Fori(x0, x1) as X:
                                act.wait_ge(more_products, X + 1)
                                s.activation(silx, bank(4)[:, 0:S], ACT.Silu).then_inc(more_silu, 1)
                                act.wait_ge(more_out, X + 1)
                                s.activation(ysbx, bank(4), ACT.Copy).then_inc(more_out_read, 1)
                    own.leave(NE // 2, per)
                if L + 1 < DEPTH:
                    split(L + 1, 0, 0)

            norm(N_MIX0)
            norm_T(N_MIX0)
            split(0, 0, 0)
            t5_rows()
            norm(N_MEM)
            mixer0()
            norm(N_XA0)
            norm_T(N_XA0)
            cross_attention(0)
            norm(N_FFN0)
            moe(0)
            norm(N_MIX1)
            norm_T(N_MIX1)
            mixer1()
            norm(N_XA1)
            norm_T(N_XA1)
            cross_attention(1)
            norm(N_FFN1)
            moe(1)
            norm(N_FINAL)

        @block.vector
        def _(dve):
            v = nc.vector
            own = Own(dve)

            def step(ins, sem_=None):
                own.inc(ins, dve_step if sem_ is None else sem_)
                own.wait()

            def constants():
                lbv = vecs[:, R_LB:R_LB + 4]
                dve.wait_ge(small_in, 16)
                step(v.tensor_tensor(lbz, lbv, lbv, ALU.subtract), lb_zero)
                dve.wait_ge(early_in, 16)
                for i in range(2):
                    own.inc(v.tensor_tensor_reduce(lamrow[:, 2 * i, :], lamrow[:, 2 * i, :], lamrow[:, 2 * i + 1, :],
                                                   1.0, 0.0, ALU.mult, ALU.add, lam2[:, i:i + 1]), lam_dot)
                dve.wait_ge(lb_exp, 1)
                step(v.reciprocal(lbr, lbe))
                step(v.tensor_tensor(lbp, lbe, lbr, ALU.mult))
                step(v.tensor_tensor(lb, lbp, lbp, ALU.subtract))
                step(v.tensor_scalar(oml, lb, -1.0, 1.0, ALU.mult, ALU.add))
                step(v.tensor_scalar(sub, vecs[:, R_SUB:R_SUB + 1], 1.0 - LAM_INIT, None, ALU.mult))
                dve.wait_ge(lam_exp, 1)
                step(v.tensor_tensor(lamd, lamexp[:, 1:2], lamexp[:, 0:1], ALU.subtract))
                step(v.memset(lamv[:, 0:2], 1.0))
                for i in range(2):
                    step(v.tensor_scalar(lamv[:, 2 + i:3 + i], lamd, LAM_INIT, None, ALU.subtract))

            def norm(n):
                src, dst, _ = norm_buffers(n)
                wait_source(dve, n, 1)
                step(v.tensor_tensor_reduce(dst[:, 1, :], src[:, 1, :], src[:, 1, :], 1.0, 0.0, ALU.mult, ALU.add,
                                            ss[:, 1:2]))
                dve.wait_ge(sq_act, n + 1)
                own.inc(v.tensor_scalar(ms, ss, 1.0 / D, EPS, ALU.mult, ALU.add), ms_ready)
                dve.wait_ge(rt_ready, n + 1)
                step(v.reciprocal(rs, rt), rs_ready)
                if n < N_FINAL:
                    step(v.tensor_scalar(dst[:, 1, :], src[:, 1, :], rs[:, 1:2], None, ALU.mult), xs_dve)

            def turn_lo_part(L, t_, b, src, gain=None, waits=True):
                if waits:
                    dve.wait_ge(hi_ready, 4 * (4 * L + t_) + b + 1)
                for k in range(2):
                    lo, hi = turn_lo(L, t_)[:, 2 * b + k, :], hThi[:, 2 * b + k, :].bitcast(F32)
                    done = lo_ready if k else dve_step
                    if gain is None:
                        own.inc(v.tensor_tensor(lo, src[:, k * S:(k + 1) * S], hi, ALU.subtract), done)
                    else:
                        own.inc(v.scalar_tensor_tensor(out=lo, in0=src[:, k * S:(k + 1) * S], scalar=gain(k), in1=hi,
                                                       op0=ALU.mult, op1=ALU.subtract), done)

            def norm_T(n):
                if norm_turn(n) is not None:
                    for b in range(4):
                        turn_lo_part(*norm_turn(n), b, bank(4 + b), lambda k: gains[:, n, 2 * b + k:2 * b + k + 1])
                    return
                for k in range(4, 8):
                    if k % 2 == 0:
                        dve.wait_ge(tr_done, 4 * n + k // 2 + 1)
                    own.inc(v.tensor_scalar(norm_buffers(n)[2][:, k, :], bank(4 + k // 2)[:, (k % 2) * S:(k % 2 + 1) * S],
                                            gains[:, n, k:k + 1], None, ALU.mult), hT_dve)
                own.wait()

            def add_unit(L, u):
                h = (u % 2) * 512
                dve.wait_ge(proj_done, L * PROJ + u + 1)
                step(v.tensor_tensor(x[:, :, h:h + 512], x[:, :, h:h + 512], pair(L * PROJ + u), ALU.add), proj_read_dve)

            def head_norm(o, osq, nh, blocks, meanwhile=None):
                n = nh * TB
                dve.wait_ge(o_sq, blocks)
                step(v.tensor_reduce(oss[:, 0:n], osq.rearrange("p b (h c) -> p (b h) c", c=P), AX.X, ALU.add))
                own.inc(v.tensor_scalar(oms[:, 0:n], oss[:, 0:n], 1.0 / P, EPS, ALU.mult, ALU.add), oms_ready)
                if meanwhile is not None:
                    meanwhile()
                dve.wait_ge(ort_ready, blocks)
                step(v.reciprocal(ors[:, 0:n], ort[:, 0:n]))

            def forget():
                wait_read(dve, 0, 2)
                for h in range(HH):
                    own.inc(v.tensor_scalar(fgate[:, h * S:(h + 1) * S], fgate[:, h * S:(h + 1) * S],
                                            oml[:, h:h + 1], lb[:, h:h + 1], ALU.mult, ALU.add), dve_step)
                own.wait()
                step(v.tensor_scalar(lntmp, fgate, 1e-30, LN_SPLIT, ALU.max, ALU.mult))
                own.inc(v.tensor_scalar(logf, fgate, 1.0 / LN_SPLIT, None, ALU.max), dve_step)
                step(v.tensor_scalar(lntmp, lntmp, 1.0, None, ALU.min), f_ready)
                own.inc(v.tensor_scalar(kh, fgate, -1.0, 1.0, ALU.mult, ALU.add), k_ready)
                step(v.memset(scanmask, 1.0))
                step(v.memset(scanmask.rearrange("p (a b) -> p a b", b=P)[:, :, 0:1], 0.0))
                dve.wait_ge(ln_ready, 1)
                step(v.tensor_tensor(logf, logf, lntmp, ALU.add))
                step(v.tensor_tensor_scan(bcum, scanmask, logf, 0.0, ALU.mult, ALU.add), b_ready)

            def mixer0():

                def mul(lev):
                    dve.wait_ge(exp_ready, lev)
                    if lev == 1:
                        wait_read(dve, 0, 3)
                        dve.wait_ge(proj_done, 6)
                        for b_ in Qt:
                            own.inc(v.memset(b_, 0.0), dve_step)
                        own.wait()
                    step(v.tensor_tensor(halves(Qt[lev % 2], lev)[1], halves(qh, lev)[1], halves(Ebuf[lev % 2], lev)[1],
                                         ALU.mult), lev_ready)

                def take(lev):
                    b_ = 4 + 2 * (lev % 2)
                    src = ps[:, b_:b_ + 2, :].rearrange("p a (n t) -> p (a n) t", t=P)
                    mk = masks[:, lev:lev + 1, :].to_broadcast([P, 8, P])
                    dve.wait_ge(lev_done, lev + 1)
                    if lev == 0:
                        step(v.tensor_tensor(scoresT, src, mk, ALU.mult), lev_read)
                    else:
                        t_ = lntmp.rearrange("p (n t) -> p n t", t=P)
                        step(v.tensor_tensor(t_, src, mk, ALU.mult), lev_read)
                        step(v.tensor_tensor(scoresT, scoresT, t_, ALU.add), scores_ready if lev == LEVELS else None)

                taps = iter(range(CONVW))

                def tap():
                    j = next(taps, None)
                    if j is None:
                        return
                    for c in range(HH):
                        w = dwT[:, c, j:j + 1]
                        if j == 0:
                            ins = v.tensor_scalar(cacc[:, c, :], upad[:, c, 0:S], w, vecs[:, R_DB + c:R_DB + c + 1],
                                                  ALU.mult, ALU.add)
                        else:
                            ins = v.scalar_tensor_tensor(out=cacc[:, c, :], in0=upad[:, c, j:j + S], scalar=w,
                                                         in1=cacc[:, c, :], op0=ALU.mult, op1=ALU.add)
                        own.inc(ins, conv_done if j == CONVW - 1 else dve_step)
                    own.wait()

                constants()
                wait_read(dve, 0, 1)
                step(v.tensor_tensor(upad[:, :, PAD:], upad[:, :, PAD:], cacc[:, :, :], ALU.mult))
                dve.wait_ge(upad_zero, 1)
                dve.wait_ge(mixc_in, 16)
                for _ in range(TAPS_BEFORE):
                    tap()
                forget()
                dve.wait_ge(t5_stored, 16)
                for b_ in Kt:
                    own.inc(v.memset(b_, 0.0), kt_zero)
                for _ in range(TAPS_AFTER):
                    tap()
                mul(1)
                for lev in range(3, LEVELS + 2):
                    take(lev - 3)
                    mul(lev - 1)
                    for _ in range(TAPS_PER_LEVEL):
                        tap()
                take(LEVELS - 1)
                mul(LEVELS + 1)
                for _ in range(CONVW):
                    tap()
                dve.wait_ge(cross_done, 1)
                step(v.tensor_copy(crossT[:, :, :], bank(4).rearrange("p (n t) -> p n t", t=P)), cross_read)
                take(LEVELS)

                def channel_stats():
                    dve.wait_ge(ct_done, 1)
                    for b_ in range(TB):
                        own.inc(v.bn_stats(bn[:, 6 * b_:6 * b_ + 6], bank(4 + b_)), dve_step)
                    own.wait()
                    for b_ in range(TB):
                        own.inc(v.bn_aggr(mv[:, 2 * b_:2 * b_ + 2], bn[:, 6 * b_:6 * b_ + 6]), dve_step)
                    own.wait()
                    own.inc(v.tensor_scalar(cve, mv.rearrange("p (b t) -> p b t", t=2)[:, :, 1], EPS, None, ALU.add), cv_ready)

                head_norm(ohsq, ohsq, HH, 1, channel_stats)
                o_ = oh[:, :, :].rearrange("p b (h c) -> p (b h) c", c=P)
                step(v.tensor_tensor(o_, o_, ors[:, 0:8].unsqueeze(2).to_broadcast([P, 8, P]), ALU.mult))
                step(v.tensor_tensor(oh[:, :, :], oh[:, :, :], gh[:, :, :], ALU.mult), on_ready)
                dve.wait_ge(cr_ready, 1)
                step(v.reciprocal(crs, crt))
                for b_ in range(TB):
                    own.inc(v.tensor_scalar(cnorm[:, b_, :], bank(4 + b_), mv[:, 2 * b_:2 * b_ + 1], crs[:, b_:b_ + 1],
                                            ALU.subtract, ALU.mult), cn_ready)
                for b_ in range(2):
                    turn_lo_part(0, T_OUT, b_, bank(6 + b_), lambda k: vecs[:, R_HG:R_HG + 1])
                for b_ in range(2):
                    turn_lo_part(0, T_OUT, 2 + b_, csilu[:, 2 * b_:2 * b_ + 2, :].rearrange("p a b -> p (a b)"))
                add_unit(0, 10)
                add_unit(0, 11)

            def mixer1():
                def front(j):
                    hp, i = j // 2, j % 2
                    nk = P * (i + 1)
                    dve.wait_ge(dsc_done, j + 1)
                    sc = ps[:, 4:6, :].rearrange("p m (h k) -> p m h k", h=2)
                    for m in range(2):
                        step(v.tensor_tensor(sD[i][:, m, :, 0:nk], sc[:, m, :, 0:nk],
                                             biasd[:, 2 * hp:2 * hp + 2, 2 * P - nk:2 * P], ALU.add), dsc_read)
                    own.inc(v.tensor_reduce(dmx[:, 4 * i:4 * i + 4].rearrange("p (m h) -> p m h", m=2),
                                            sD[i][:, :, :, 0:nk], AX.X, ALU.max, negate=True), dmax_ready)

                def back(j):
                    i = j % 2
                    nk = P * (i + 1)
                    dve.wait_ge(dexp_ready, 4 * j + 4)
                    rc = drc[:, 4 * i:4 * i + 4]
                    step(v.reciprocal(rc, dsum[:, 4 * i:4 * i + 4]))
                    step(v.tensor_tensor(rc, rc, lamv, ALU.mult))
                    own.inc(v.tensor_tensor(sD[i][:, 1, :, 0:nk], sD[i][:, 1, :, 0:nk],
                                            rc[:, 2:4].unsqueeze(2).to_broadcast([P, 2, nk]), ALU.mult), dve_step)
                    own.wait()
                    for h in range(2):
                        own.inc(v.scalar_tensor_tensor(out=sD[i][:, 0, h, 0:nk], in0=sD[i][:, 0, h, 0:nk],
                                                       scalar=rc[:, h:h + 1], in1=sD[i][:, 1, h, 0:nk],
                                                       op0=ALU.mult, op1=ALU.add), da_ready)

                dve.wait_ge(t5_ready, 1)
                front(0)
                for j in range(DH):
                    if j + 1 < DH:
                        if j >= 1:
                            dve.wait_ge(dat_done, j)
                        front(j + 1)
                    back(j)
                own.wait()
                head_norm(od, odsq, DH, 2)
                for b_ in range(TB):
                    o_ = od[:, b_, :].rearrange("p (h c) -> p h c", c=P)
                    own.inc(v.tensor_tensor(o_, o_, ors[:, 8 * b_:8 * b_ + 8].unsqueeze(2).to_broadcast([P, 8, P]),
                                            ALU.mult), on_ready)
                for b_ in range(4):
                    turn_lo_part(1, T_OUT, b_, bank(4 + b_), lambda k: sub)
                add_unit(1, 10)
                add_unit(1, 11)

            def cross_attention(L):
                for c in range(4):
                    dve.wait_ge(xsc_done, 4 * L + c + 1)
                    step(v.tensor_reduce(xmx[:, 2 * c:2 * c + 2], bank(4 + c).rearrange("p (h m) -> p h m", h=2),
                                         AX.X, ALU.max, negate=True))
                    own.inc(v.tensor_scalar(xmx[:, 2 * c:2 * c + 2], xmx[:, 2 * c:2 * c + 2], 1.0 / 16, None, ALU.mult),
                            xmax_ready)
                for c in range(4):
                    dve.wait_ge(xexp_ready, 8 * L + 2 * c + 2)
                    step(v.reciprocal(xrc[:, 2 * c:2 * c + 2], xsum[:, 2 * c:2 * c + 2]))
                    own.inc(v.tensor_tensor(px[:, c, :, :], px[:, c, :, :],
                                            xrc[:, 2 * c:2 * c + 2].unsqueeze(2).to_broadcast([P, 2, M]), ALU.mult), xp_ready)
                for b_ in range(4):
                    turn_lo_part(L, T_XO, b_, bank(4 + b_))
                add_unit(L, 14)
                add_unit(L, 15)

            def moe(L):
                n = N_FFN0 if L == 0 else N_FFN1
                norm_T(n)
                own.inc(v.memset(zeros, 0.0), dve_step)
                for b_ in (*pturn, ysb[0]):
                    own.inc(v.memset(b_, 0.0), dve_step)
                own.inc(v.memset(ysb[1], 0.0), ysb_ready)
                own.inc(v.memset(rank[:, :, NE:], -1.0), dve_step)
                if L == 0:
                    own.inc(v.memset(xcarry, 0.0), more_step)
                def at(t, b_, e):
                    return t[:, b_, bass.ds(e, 1)]

                def build_psel(e):
                    for b_ in range(TB):
                        for j in range(2):
                            last = b_ == TB - 1 and j == 1
                            own.inc(v.tensor_scalar(psel[:, b_, j * CAP:(j + 1) * CAP], places[:, 0:CAP],
                                                    at(rank, b_, e + j), None, ALU.is_equal),
                                    psel_ready if last else dve_step)

                tie2 = ties.unsqueeze(1).to_broadcast([P, TB, NE])
                tie4 = ties[:, NE - NG:].unsqueeze(1).to_broadcast([P, TB, NG])
                g4, e16 = lg[:, :, 0:NG], lg[:, :, NG:]
                wide4 = lambda c: c.to_broadcast([P, TB, NG])
                wide = lambda c: c.to_broadcast([P, TB, NE])
                dve.wait_ge(rl_done, L + 1)
                step(v.tensor_tensor(lg, ps[:, 0:TB, 0:NG + NE],
                                     rbias[L].unsqueeze(1).to_broadcast([P, TB, NG + NE]), ALU.add))
                step(v.tensor_reduce(r1[0], g4, AX.X, ALU.max))
                step(v.tensor_tensor(r4[0], g4, wide4(r1[0]), ALU.subtract), rexp_in)
                step(v.scalar_tensor_tensor(out=r4[2], in0=r4[0], scalar=0.0, in1=tie4, op0=ALU.is_equal, op1=ALU.mult))
                step(v.tensor_reduce(r1[1], r4[2], AX.X, ALU.max))
                step(v.tensor_tensor(r4[3], r4[2], wide4(r1[1]), ALU.not_equal))
                step(v.scalar_tensor_tensor(out=r16[0].rearrange("p b (g e) -> p b g e", g=NG),
                                            in0=r4[3].unsqueeze(3).to_broadcast([P, TB, NG, EPG]), scalar=-BIG,
                                            in1=e16.rearrange("p b (g e) -> p b g e", g=NG), op0=ALU.mult, op1=ALU.add))
                step(v.tensor_reduce(r1[4], r16[0], AX.X, ALU.max))
                step(v.tensor_tensor(r16[1], r16[0], wide(r1[4]), ALU.is_equal))
                step(v.tensor_tensor(r16[2], r16[1], tie2, ALU.mult))
                step(v.tensor_reduce(r1[5], r16[2], AX.X, ALU.max))
                step(v.tensor_tensor(r16[3], r16[2], wide(r1[5]), ALU.is_equal))
                step(v.scalar_tensor_tensor(out=r16[4], in0=r16[3], scalar=-2 * BIG, in1=r16[0], op0=ALU.mult, op1=ALU.add))
                step(v.tensor_reduce(r1[6], r16[4], AX.X, ALU.max))
                step(v.tensor_tensor(r16[1], r16[4], wide(r1[6]), ALU.is_equal))
                step(v.tensor_tensor(r16[2], r16[1], tie2, ALU.mult))
                step(v.tensor_reduce(r1[5], r16[2], AX.X, ALU.max))
                step(v.tensor_tensor(r16[5], r16[2], wide(r1[5]), ALU.is_equal))
                step(v.tensor_tensor(r16[1], r16[3], r16[5], ALU.add), member_ready)
                step(v.tensor_tensor(r1[7], r1[6], r1[4], ALU.subtract), rexp_in)
                dve.wait_ge(rexp_ready, 2 * L + 2)
                step(v.tensor_reduce(r1[2], r4[1], AX.X, ALU.add))
                step(v.reciprocal(r1[3], r1[2]))
                step(v.tensor_scalar(r1[9], r1[8], 1.0, None, ALU.add))
                step(v.reciprocal(r1[5], r1[9]))
                step(v.tensor_tensor(r1[0], r1[3], r1[5], ALU.mult))
                step(v.tensor_tensor(r1[1], r1[0], r1[8], ALU.mult))
                step(v.tensor_tensor(r16[6], r16[3], wide(r1[0]), ALU.mult))
                step(v.tensor_tensor(r16[7], r16[5], wide(r1[1]), ALU.mult))
                step(v.tensor_tensor(gate, r16[6], r16[7], ALU.add))
                dve.wait_ge(rank_done, L + 1)
                rk = rank[:, :, 0:NE]
                step(v.scalar_tensor_tensor(out=rk, in0=bank(5)[:, 0:TB * NE].rearrange("p (b e) -> p b e", b=TB), scalar=1.0,
                                            in1=r16[1], op0=ALU.add, op1=ALU.mult))
                build_psel(0)
                cnt = r16[0][:, 0, :]
                step(v.tensor_copy(r16[1], bank(5)[:, 2 * NE:4 * NE].rearrange("p (b e) -> p b e", b=TB)))
                step(v.tensor_tensor(cnt, r16[1][:, 0, :], r16[1][:, 1, :], ALU.add))
                step(v.tensor_scalar(nx, cnt, float(CAP), None, ALU.is_gt))
                for i in range(2, S // CAP):
                    step(v.tensor_scalar(cumx[:, 0:NE], cnt, float(CAP * i), None, ALU.is_gt))
                    step(v.tensor_tensor(nx, nx, cumx[:, 0:NE], ALU.add))
                step(v.tensor_copy(cumx[:, 0:1], xcarry))
                step(v.tensor_tensor_scan(cumx[:, 1:NE + 1], ones[:, 0:NE], nx, xcarry, ALU.mult, ALU.add))
                step(v.tensor_copy(xcarry, cumx[:, NE:NE + 1]))
                step(v.tensor_copy(xtab[:, :], cumx), table_ready)

                def build_pgate(e, o):
                    for b_ in range(TB):
                        for j in range(2):
                            at_ = (j ^ o) * CAP
                            own.inc(v.tensor_scalar(pgate[o][:, b_, at_:at_ + CAP], places[:, 0:CAP], at(rank, b_, e + j),
                                                    at(gate, b_, e + j), ALU.is_equal, ALU.mult), dve_step)

                def take_gather(half, g, at_=6):
                    dve.wait_ge(g_done, g)
                    own.inc(v.tensor_tensor(hsel[:, 4 * half:4 * half + 4, :], bank(at_).rearrange("p (k t) -> p k t", t=P),
                                            gains[:, n, 4 * half:4 * half + 4].unsqueeze(2).to_broadcast([P, 4, P]),
                                            ALU.mult), hsel_ready)

                GB = (NE + 2) * L
                take_gather(0, GB + 1)
                take_gather(1, GB + 2, 7)
                own.wait()
                per = {dve_step: 3 + 8, psel_ready: 1, hid_ready: 2, hturn_ready: 2, pturn_ready: 2, hsel_ready: 2}
                with dve.Fori(0, NE // 2) as it:
                    own.enter(it, per)
                    for j in range(2):
                        e = it * 2
                        o = 1 - j
                        if j == 0:
                            build_pgate(e, 1)
                            build_pgate(e, 0)
                            build_psel(e + 2)
                        else:
                            dve.wait_ge(hsel_used, it + (L * (NE // 2) + 1))
                            take_gather(0, it * 2 + (GB + 3))
                        dve.wait_ge(sil_ready, it * 2 + (L * NE + j + 1))
                        own.inc(v.tensor_tensor(hid, sil, bank(4)[:, S:2 * S], ALU.mult), hid_ready)
                        dve.wait_ge(t_done, it * 2 + (L * NE + j + 1))
                        own.inc(v.tensor_copy(hturn, bank(7)[:, S:2 * S]), hturn_ready)
                        if j == 1:
                            take_gather(1, it * 2 + (GB + 4))
                        if j == 0:
                            dve.wait_ge(scatter_done, it + ((NE // 2 + 1) * L + 1))
                        own.inc(v.tensor_copy(pturn[o], bank(7)[:, 0:S]), pturn_ready)
                        further(e + j, n)
                    own.leave(NE // 2, per)
                dve.wait_ge(scatter_done, (NE // 2 + 1) * (L + 1))
                for b_ in range(TB):
                    own.inc(v.tensor_tensor(x[:, b_, :].rearrange("p (c n) -> p c n", c=2),
                                            x[:, b_, :].rearrange("p (c n) -> p c n", c=2),
                                            ps[:, 2 * b_:2 * b_ + 2, :], ALU.add), x_new)
                own.wait()

            def further(e, n):
                x0, x1 = rounds(v, e)
                with dve.If(x1 > x0):
                    with dve.Fori(x0, x1) as X:
                        own.wait()
                        dve.wait_ge(more_done, X + 1)
                        dve.wait_ge(more_step, X * MORE_STEPS + 1)
                        r_ = rank[:, :, bass.ds(e, 1)]
                        v.tensor_scalar(r_, r_, float(CAP), None, ALU.subtract).then_inc(more_step, 1)
                        dve.wait_ge(more_step, X * MORE_STEPS + 2)
                        for b_ in range(TB):
                            v.tensor_scalar(pselx[:, b_, :], places[:, 0:CAP], rank[:, b_, bass.ds(e, 1)], None,
                                            ALU.is_equal).then_inc(more_step, 1)
                        for b_ in range(TB):
                            v.tensor_scalar(pgatex[:, b_, :], places, rank[:, b_, bass.ds(e, 1)],
                                            gate[:, b_, bass.ds(e, 1)], ALU.is_equal, ALU.mult
                                            ).then_inc(more_step if b_ == 0 else more_chosen, 1)
                        dve.wait_ge(more_gathered, X + 1)
                        v.tensor_tensor(hselx, bank(4).rearrange("p (k t) -> p k t", k=KD),
                                        gains[:, n, :].unsqueeze(2).to_broadcast([P, KD, CAP]), ALU.mult).then_inc(more_tokens, 1)
                        dve.wait_ge(more_silu, X + 1)
                        v.tensor_tensor(hidx, silx, bank(4)[:, S:2 * S], ALU.mult).then_inc(more_hidden, 1)
                        dve.wait_ge(more_turned, X + 1)
                        v.tensor_copy(tsbx, bank(7)).then_inc(more_turns_read, 1)

            norm(N_MIX0)
            norm_T(N_MIX0)
            norm(N_MEM)
            norm_T(N_MEM)
            mixer0()
            norm(N_XA0)
            norm_T(N_XA0)
            cross_attention(0)
            norm(N_FFN0)
            moe(0)
            norm(N_MIX1)
            norm_T(N_MIX1)
            mixer1()
            norm(N_XA1)
            norm_T(N_XA1)
            cross_attention(1)
            norm(N_FFN1)
            moe(1)
            norm(N_FINAL)
            dve.wait_ge(fgain_in, 16)
            for b_ in range(TB):
                own.inc(v.scalar_tensor_tensor(out=xs[:, b_, :], in0=x[:, b_, :], scalar=rs[:, b_:b_ + 1], in1=fgain,
                                               op0=ALU.mult, op1=ALU.mult), y_out)

        @block.tensor
        def _(pe):
            t = nc.tensor

            pe.wait_ge(small_in, 16)
            pe.wait_ge(early_in, 16)
            t.matmul(bank(2)[0:DH, 0:BW], table, onehot, start=True, stop=True).then_inc(t5_row, 1)

            idle = small[:, 0:256].bitcast(mybir.dt.bfloat16)

            def keep_clock(n, b=4):
                for _ in range(n):
                    t.matmul(bank(b), idle[:, 0:P], idle, start=True, stop=True)

            def norm_T(n):
                dst = norm_buffers(n)[1]
                if n == N_MEM:
                    pe.wait_ge(lo_ready, 4)
                if n > N_MEM:
                    keep_clock(14)
                pe.wait_ge(xs_act, n + 1)
                pe.wait_ge(xs_dve, n + 1)
                for k in range(KD):
                    for b in range(TB):
                        at = (k % 2) * S + b * P
                        ins = t.transpose(bank(4 + k // 2)[:, at:at + P],
                                          dst[:, b, :].rearrange("p (r k) -> p k r", k=KD)[:, k, :], ident)
                    if k % 2 == 1:
                        ins.then_inc(tr_done, 1)

            def wait_hT(n):
                pe.wait_ge(hT_act, 4 * plain_turns(n))
                pe.wait_ge(hT_dve, 4 * plain_turns(n))

            def split_unit(L, u, t_, transposed, first=False):
                pj = L * PROJ + u
                if pj >= 2:
                    wait_read(pe, *divmod(pj - 2, PROJ))
                dst = pair(pj)
                h_lo = turn_lo(L, t_)
                for k in range(KD):
                    n, w_hi, w_lo = piece(L, u, k)
                    if first and k % 2 == 0:
                        pe.wait_ge(lo_ready, 4 * (4 * L + t_) + k // 2 + 1)
                    pe.wait_ge(piece_lo, n + 1)
                    for i, (w, h) in enumerate(((w_hi, hThi), (w_hi, h_lo), (w_lo, hThi))):
                        for f in range(4 if transposed else 2):
                            if transposed:
                                o_, l_, r_ = dst[:, f // 2, (f % 2) * S:(f % 2 + 1) * S], w[:, f * P:(f + 1) * P], h[:, k, :]
                            else:
                                o_, l_, r_ = dst[:, f, :], h[:, k, f * P:(f + 1) * P], w
                            ins = t.matmul(o_, l_, r_, start=(k == 0 and i == 0 and not (transposed and f % 2)),
                                           stop=(k == KD - 1 and i == 2), skip_group_check=True)
                    ins.then_inc(piece_used if k < KD - 1 else proj_done, 1)

            def unit(L, u, src, transposed, part=None):
                pj = L * PROJ + u
                if pj >= 2:
                    wait_read(pe, *divmod(pj - 2, PROJ))
                pe.wait_ge(landed[slot(L, u)], arrival(L, u))
                w = ring[:, slot(L, u), :].rearrange("p (k n) -> p k n", k=KD)
                dst = pair(pj)
                if transposed:
                    for f in range(4) if part is None else (2 * part, 2 * part + 1):
                        for k in range(KD):
                            ins = t.matmul(dst[:, f // 2, (f % 2) * S:(f % 2 + 1) * S], w[:, k, f * P:(f + 1) * P],
                                           src[:, k, :], start=(k == 0), stop=(k == KD - 1))
                else:
                    for b in range(TB) if part is None else (part,):
                        for k in range(KD):
                            ins = t.matmul(dst[:, b, :], src[:, k, b * P:(b + 1) * P], w[:, k, :],
                                           start=(k == 0), stop=(k == KD - 1))
                if part != 0:
                    ins.then_inc(proj_done, 1)

            def mixer0():
                def level(lev):
                    if lev == 0:
                        kk, qq = kh, qh
                        pe.wait_ge(k_ready, 1)
                        wait_read(pe, 0, 3)
                    else:
                        kk, qq = Kt[lev % 2], Qt[lev % 2]
                        pe.wait_ge(lev_ready, lev)
                        pe.wait_ge(kt_ready, lev)
                    if lev == LEVELS + 1:
                        pe.wait_ge(lev_read, LEVELS)
                        for h in range(HH):
                            ins = t.matmul(bank(4)[:, h * P:(h + 1) * P], kk[:, h * S:h * S + P],
                                           qq[:, h * S + P:(h + 1) * S], start=True, stop=True)
                        ins.then_inc(cross_done, 1)
                        return
                    if lev >= 2:
                        pe.wait_ge(lev_read, lev - 1)
                    for i in range(8):
                        at = i * P
                        ins = t.matmul(bank(4 + 2 * (lev % 2) + i // 4)[:, (i % 4) * P:(i % 4 + 1) * P],
                                       kk[:, at:at + P], qq[:, at:at + P], start=True, stop=True)
                    ins.then_inc(lev_done, 1)

                keep_clock(12, 0)
                split_unit(0, 0, T_MIX, True, True)
                norm_T(N_MEM)
                pe.wait_ge(t5_read, 1)
                for u in range(1, 4):
                    split_unit(0, u, T_MIX, True)
                wait_hT(N_MEM)
                split_unit(0, 4, T_MIX, False)
                level(0)
                split_unit(0, 5, T_MIX, False)
                for half in range(7):
                    unit(0, 6 + half // 2, memT, half < 4, part=half % 2)
                    if half < 6:
                        level(half + 1)
                level(LEVELS + 1)
                level(LEVELS)
                pe.wait_ge(conv_done, HH)
                pe.wait_ge(cross_read, 1)
                for b in range(TB):
                    for c in range(HH):
                        ins = t.transpose(bank(4 + b)[:, c * P:(c + 1) * P], cacc[:, c, b * P:(b + 1) * P], ident)
                ins.then_inc(ct_done, 1)
                wait_read(pe, 0, 4)
                pe.wait_ge(scores_ready, 1)
                for h in range(HH):
                    hv = slice(h * P, (h + 1) * P)
                    t.matmul(bank(6)[:, hv], scoresT[:, 2 * h, :], vh[:, 0, hv], start=True, stop=True)
                for h in range(HH):
                    hv = slice(h * P, (h + 1) * P)
                    t.matmul(bank(7)[:, hv], scoresT[:, 2 * h + 1, :], vh[:, 1, hv], start=True, stop=False)
                    ins = t.matmul(bank(7)[:, hv], crossT[:, h, :], vh[:, 0, hv], start=False, stop=True)
                ins.then_inc(o_done, 1)
                unit(0, 9, memT, False, part=1)
                pe.wait_ge(on_ready, 1)
                for h in range(HH):
                    for b in range(TB):
                        at = (h % 2) * S + b * P
                        ins = t.transpose(bank(6 + h // 2)[:, at:at + P], oh[:, b, h * P:(h + 1) * P], ident)
                ins.then_inc(ot_done, 1)
                pe.wait_ge(cn_ready, TB)
                for c in range(HH):
                    for b in range(TB):
                        at = (c % 2) * S + b * P
                        ins = t.transpose(bank(4 + c // 2)[:, at:at + P], cnorm[:, b, c * P:(c + 1) * P], ident)
                    if c % 2 == 1:
                        ins.then_inc(cb_done, 1)
                split_unit(0, 10, T_OUT, False, True)
                split_unit(0, 11, T_OUT, False)

            def mixer1():
                for u in range(4):
                    split_unit(1, u, T_MIX, True, u == 0)
                pe.wait_ge(t5_in, 16)
                for h in range(DH):
                    ins = t.matmul(bank(4 + h // 2)[:, (h % 2) * S:(h % 2 + 1) * S], anti, biasrev[:, h, :],
                                   start=True, stop=True)
                ins.then_inc(t5_turned, 1)
                split_unit(1, 4, T_MIX, False)
                split_unit(1, 5, T_MIX, False)

                def scores(j):
                    hp, i = j // 2, j % 2
                    if j >= 1:
                        pe.wait_ge(dsc_read, 2 * j)
                    for h in range(2):
                        for m in range(2):
                            mp = slice(64 * m, 64 * m + 64)
                            ins = t.matmul(bank(4 + m)[:, h * S:h * S + P * (i + 1)],
                                           qd[mp, 2 * hp + h, i * P:(i + 1) * P],
                                           kd[mp, 2 * hp + h, 0:P * (i + 1)], start=True, stop=True)
                    ins.then_inc(dsc_done, 1)

                wait_read(pe, 1, 3)
                pe.wait_ge(t5_ready, 1)
                scores(0)
                for j in range(DH):
                    hp, i = j // 2, j % 2
                    if j + 1 < DH:
                        scores(j + 1)
                        unit(1, 6 + j // 2, memT, j < 4, part=i)
                    pe.wait_ge(da_ready, 2 * j + 2)
                    if j >= 1:
                        pe.wait_ge(dat_read, j)
                    for h in range(2):
                        for c in range(i + 1):
                            at = (h * (i + 1) + c) * P
                            ins = t.transpose(bank(6)[:, at:at + P], sD[i][:, 0, h, c * P:(c + 1) * P], ident)
                    ins.then_inc(dat_done, 1)
                    pe.wait_ge(dat_read, j + 1)
                    wait_read(pe, 1, 5)
                    if j >= 1:
                        pe.wait_ge(do_read, j)
                    for h in range(2):
                        for c in range(i + 1):
                            ins = t.matmul(bank(7)[:, h * P:(h + 1) * P], aTD[:, h, c, :],
                                           vd[:, c, (2 * hp + h) * P:(2 * hp + h + 1) * P],
                                           start=(c == 0), stop=(c == i))
                    ins.then_inc(do_done, 1)
                unit(1, 9, memT, False, part=1)
                keep_clock(14)
                pe.wait_ge(do_read, DH)
                pe.wait_ge(on_ready, 1 + TB)
                for h in range(DH):
                    for b in range(TB):
                        at = (h % 2) * S + b * P
                        ins = t.transpose(bank(4 + h // 2)[:, at:at + P], od[:, b, h * P:(h + 1) * P], ident)
                    if h % 2 == 1:
                        ins.then_inc(ot_done, 1)
                split_unit(1, 10, T_OUT, False, True)
                split_unit(1, 11, T_OUT, False)

            def cross_attention(L):
                n = N_XA0 if L == 0 else N_XA1
                norm_T(n)
                split_unit(L, 12, T_XA, True, True)
                split_unit(L, 13, T_XA, True)
                wait_read(pe, L, 9)
                for c in range(4):
                    i, hp = c % 2, c // 2
                    wait_read(pe, L, 12 + hp)
                    for j in range(2):
                        for k in range(2):
                            f = 2 * (2 * hp + j) + k
                            ins = t.matmul(bank(4 + c)[:, j * M:(j + 1) * M], qx[:, f, i * P:(i + 1) * P],
                                           kmem[:, f, :], start=(k == 0), stop=(k == 1))
                    ins.then_inc(xsc_done, 1)
                for c in range(4):
                    pe.wait_ge(xp_ready, 4 * L + c + 1)
                    for m in range(2):
                        for j in range(2):
                            at = (2 * m + j) * P
                            ins = t.transpose(bank(4 + c)[:, at:at + P], px[:, c, j, m * P:(m + 1) * P], ident)
                    ins.then_inc(xpt_done, 1)
                pe.wait_ge(xpt_read, 4 * (L + 1))
                for f in range(KD):
                    for m in range(2):
                        ins = t.matmul(bank(4 + f // 2)[:, (f % 2) * S:(f % 2 + 1) * S], vmem[:, m, f * P:(f + 1) * P],
                                       pxT[:, m, f // 2, :], start=(m == 0), stop=(m == 1))
                    if f % 2 == 1:
                        ins.then_inc(xo_done, 1)
                split_unit(L, 14, T_XO, False, True)
                split_unit(L, 15, T_XO, False)

            def moe(L):
                n = N_FFN0 if L == 0 else N_FFN1
                norm_T(n)
                for k in range(KD):
                    if k < 4:
                        pe.wait_ge(hT_act, 4 * (plain_turns(n) - 1) + k + 1)
                    else:
                        pe.wait_ge(hT_dve, 4 * (plain_turns(n) - 1) + k - 3)
                    for b in range(TB):
                        ins = t.matmul(bank(b)[:, 0:NG + NE], hT[:, k, b * P:(b + 1) * P],
                                       wr[L][:, k, :], start=(k == 0), stop=(k == KD - 1))
                ins.then_inc(rl_done, 1)
                keep_clock(14)
                pe.wait_ge(member_ready, L + 1)
                mem_ = r16[1].rearrange("p b e -> p (b e)")
                t.matmul(bank(5)[:, 0:2 * NE], upper, mem_, start=True, stop=False, skip_group_check=True)
                t.matmul(bank(5)[:, NE:2 * NE], ones, mem_[:, 0:NE], start=False, stop=False, skip_group_check=True)
                t.matmul(bank(5)[:, 2 * NE:4 * NE], ones, mem_, start=False, stop=True,
                         skip_group_check=True).then_inc(rank_done, 1)

                def gather(half, ks=range(4), to=6):
                    for k in (4 * half + k_ for k_ in ks):
                        for b in range(TB):
                            ins = t.matmul(bank(to)[:, (k % 4) * P:(k % 4 + 1) * P],
                                           xs[:, b, :].rearrange("p (r k) -> p k r", k=KD)[:, k, :], psel[:, b, :],
                                           start=(b == 0), stop=(b == TB - 1))
                    if k % 4 == 3:
                        ins.then_inc(g_done, 1)

                def first(it, j, tokens, done, start_sem=None, half_used=None, half_ready=None):
                    for r in range(2):
                        if type(it) is int and it == EXTRA // 2 and j == 0:
                            pe.wait_ge(spare_in[r], 16 * (L + 1))
                            w = spare[r]
                        else:
                            pe.wait_ge(landed[slot(L, PROJ + EU * j + r)], where(it, j, r))
                            w = ring[:, slot(L, PROJ + EU * j + r), :]
                        w = w.rearrange("p (k c n) -> p k c n", k=KD, c=2)
                        for k in range(KD):
                            if r == 0 and k == KD // 2 and half_ready is not None:
                                pe.wait_ge(hsel_ready, half_ready)
                            for c in range(2):
                                ins = t.matmul(bank(4)[64 * c:64 * c + 64, r * S:(r + 1) * S], tokens[:, k, :],
                                               w[:, k, c, :], start=(k == 0), stop=(k == KD - 1))
                                if start_sem is not None:
                                    ins.then_inc(start_sem, 1)
                                    start_sem = None
                            if r == 1 and k == KD // 2 - 1 and half_used is not None:
                                ins.then_inc(half_used, 1)
                    ins.then_inc(done, 1)

                def turn(sel, hidden, done):
                    for b in range(TB):
                        t.transpose(bank(7)[:, b * P:(b + 1) * P], sel[:, b, :], ident)
                    for m in range(2):
                        ins = t.transpose(bank(7)[:, S + m * P:S + (m + 1) * P],
                                          hidden.rearrange("p (r m) -> p m r", m=2)[:, m, :], ident)
                    ins.then_inc(done, 1)

                def second(it, j, hidden, dst, swap, done):
                    pe.wait_ge(landed[slot(L, PROJ + EU * j + 2)], where(it, j, 2))
                    w = ring[:, slot(L, PROJ + EU * j + 2), :].rearrange("p (c m n) -> p c m n", c=2, m=2)
                    for c in range(2):
                        for m in range(2):
                            at = m * P + c * CAP
                            for o in range(2):
                                half = slice(64 * (o ^ swap), 64 * (o ^ swap) + 64)
                                ins = t.matmul(dst[half, :], hidden[:, at:at + CAP],
                                               w[:, c, m, o * 512:(o + 1) * 512], start=(c + m == 0), stop=(c + m == 2))
                    ins.then_inc(done, 1)

                def scatter():
                    for b in range(TB):
                        for o in range(2):
                            ins = t.matmul(bank(2 * b + o), pturn[o][:, b * P:(b + 1) * P], ysb[o],
                                           start=False, stop=False, skip_group_check=True)
                    ins.then_inc(scatter_done, 1)

                def nothing(done):
                    t.matmul(bank(0)[:, 0:2], zb[:, 0:P], zb[:, 0:2], start=False, stop=False,
                             skip_group_check=True).then_inc(done, 1)

                def where(it, j, r):
                    skipped = 16 if j == 0 and r < 2 and (type(it) is not int or it > 0) else 0
                    return it * 16 + (arrival(L, PROJ + EU * j + r) - skipped)

                wait_read(pe, L, 15)
                zb = zeros.bitcast(mybir.dt.bfloat16)
                for b in range(4):
                    ins = t.matmul(bank(b), zb[:, 0:P], zb[:, 0:512], start=True, stop=False, skip_group_check=True)
                if L == 0:
                    ins.then_inc(more_done, 1)
                pe.wait_ge(psel_ready, (NE // 2 + 1) * L + 1)
                gather(0)
                gather(1, to=7)
                def experts(it):
                    for j in range(2):
                        if j == 0:
                            pe.wait_ge(hsel_ready, it * 2 + ((NE + 2) * L + 1))
                        first(it, j, hsel[:, :, j * CAP:(j + 1) * CAP], h_done, expert_done,
                              half_used=hsel_used if j == 1 else None,
                              half_ready=it * 2 + ((NE + 2) * L + 2) if j == 0 else None)
                        pe.wait_ge(table_ready, L + 1)
                        x0, x1 = rounds(t, it * 2 + j)
                        with pe.If(x1 == x0):
                            nothing(w13_free)
                        if j == 0:
                            pe.wait_ge(psel_ready, it + ((NE // 2 + 1) * L + 2))
                            gather(0)
                        else:
                            pe.wait_ge(hsel_ready, it * 2 + ((NE + 2) * L + 3))
                            gather(1, range(2))
                        pe.wait_ge(hid_ready, it * 2 + (L * NE + j + 1))
                        if j == 1:
                            pe.wait_ge(pturn_ready, it * 2 + (L * NE + 1))
                        turn(pgate[1 - j], hid, t_done)
                        if j == 1:
                            gather(1, range(2, 4))
                        if j == 0:
                            pe.wait_ge(ysb_ready, it * 2 + (L * (NE + 1) + 1))
                            scatter()
                        pe.wait_ge(hturn_ready, it * 2 + (L * NE + j + 1))
                        second(it, j, hturn, bank(5), j, y_done)
                        with pe.If(x1 > x0):
                            with pe.Fori(x0, x1) as X:
                                pe.wait_ge(more_chosen, X + 1)
                                for k in range(KD):
                                    for b in range(TB):
                                        ins = t.matmul(bank(4)[:, k * CAP:(k + 1) * CAP],
                                                       xs[:, b, :].rearrange("p (r k) -> p k r", k=KD)[:, k, :],
                                                       pselx[:, b, :], start=(b == 0), stop=(b == TB - 1))
                                ins.then_inc(more_gathered, 1)
                                pe.wait_ge(more_tokens, X + 1)
                                first(it, j, hselx, more_products)
                                pe.wait_ge(more_hidden, X + 1)
                                turn(pgatex, hidx, more_turned)
                                pe.wait_ge(more_turns_read, X + 1)
                                second(it, j, tsbx[:, S:2 * S], bank(4), 0, more_out)
                                pe.wait_ge(more_out_read, X + 1)
                                for b in range(TB):
                                    for o in range(2):
                                        half = slice(64 * o, 64 * o + 64)
                                        ins = t.matmul(bank(2 * b + o), tsbx[half, b * P:(b + 1) * P], ysbx[half, :],
                                                       start=False, stop=False, skip_group_check=True)
                                ins.then_inc(more_done, 1)
                            nothing(w13_free)
                for pair_ in range(EXTRA // 2 + 1):
                    experts(pair_)
                with pe.Fori(EXTRA // 2 + 1, NE // 2) as it_:
                    experts(it_)
                pe.wait_ge(ysb_ready, (NE + 1) * (L + 1))
                pe.wait_ge(pturn_ready, NE * (L + 1))
                scatter()
                pe.wait_ge(hsel_ready, (NE + 2) * (L + 1))
                t.matmul(bank(6)[:, 0:2], zb[:, 0:P], zb[:, 0:2], start=True, stop=True).then_inc(expert_done, 1)

            norm_T(N_MIX0)
            mixer0()
            cross_attention(0)
            moe(0)
            norm_T(N_MIX1)
            mixer1()
            cross_attention(1)
            moe(1)


INPUTS = ["x", "mem", "final_norm_g", "even_w_in", "even_w_out", "odd_w_qkv", "odd_w_out", "xa_wq", "xa_wkv",
          "xa_wo", "moe_w1", "moe_w3", "moe_w2"]


def lay_out(inputs):
    g = {n: np.asarray(v) for n, v in inputs.items()}
    arrays = {f"in_{n}": np.ascontiguousarray(g[n]) for n in INPUTS}

    def columns(v):
        return v.reshape(-1, P).T

    def everywhere(v):
        return np.broadcast_to(v.reshape(1, -1), (P, v.size))

    consts, masks = shape_constants()
    norms = [g["norm_mix_g"][0], g["mem_norm_g"], g["norm_xattn_g"][0], g["norm_ffn_g"][0], g["norm_mix_g"][1],
             g["norm_xattn_g"][1], g["norm_ffn_g"][1]]
    router = [np.concatenate([g["moe_w_grp"][i], g["moe_w_exp"][i]], 1).reshape(P, -1) for i in range(DEPTH)]
    arrays["in_small"] = np.concatenate(
        [consts, *(n.reshape(P, KD) for n in norms),
         columns(g["conv_db"][0]), columns(g["conv_ln_g"][0]), columns(g["conv_ln_b"][0]),
         columns(g["hgrn_norm_g"][0]), columns(g["subln_g"][0]), columns(g["hgrn_lb"][0]),
         *(everywhere(np.concatenate([g["moe_b_grp"][i], g["moe_b_exp"][i]])) for i in range(DEPTH)), *router], 1)
    arrays["in_mixc"] = np.concatenate(
        [masks, g["conv_dw"][0].reshape(CONVW, HH, P).transpose(2, 1, 0).reshape(P, -1)], 1)
    early = np.zeros((P, EARLY), np.float32)
    early[:, 0:256] = everywhere(np.concatenate([g[n][0] for n in ("lam_q1", "lam_k1", "lam_q2", "lam_k2")]))
    early[0:RELS, 256:256 + DH] = g["rel_bias"]
    early[RELS, 256:256 + DH] = -BIG
    early[0:RELS + 1, 256 + DH:] = t5_onehot()
    arrays["in_early"] = early
    return arrays


def kernel(**inputs):
    import concourse.bacc as bacc
    from concourse.bass_utils import run_bass_kernel_spmd

    arrays = lay_out(inputs)
    nc = bacc.Bacc("TRN2", target_bir_lowering=False, num_devices=1)
    aps = {n[3:]: nc.dram_tensor(n, v.shape, mybir.dt.from_np(v.dtype), kind="ExternalInput").ap()
           for n, v in arrays.items()}
    y = nc.dram_tensor("out", (1, S, D), F32, kind="ExternalOutput").ap()
    build(nc, aps, y)
    r = run_bass_kernel_spmd(nc, [arrays], core_ids=[0])
    return r.results[0]["out"]
```
